# Optimizing a Trainium2 kernel written in Bass

```python
import math
import jax, jax.numpy as jnp
from jax import lax
import numpy as np

D_MODEL = 1024
BATCH = 1
SEQ = 256
DEPTH = 1
DEC_BATCH = 8
DEC_SEQ = 1
PAST_LEN = 256
PAGE_SIZE = 128

DA_HEADS = 4
DA_HD = 64
DA_WIDTH = DA_HEADS * 2 * DA_HD
SA_HEADS = 8
SA_HD = 64
SA_WIDTH = SA_HEADS * SA_HD
IDX_HEADS = 8
IDX_HD = 64
TOPK_MAX = 256
PEER_HEADS = 8
PEER_NKEYS = 128
PEER_N = PEER_NKEYS * PEER_NKEYS
PEER_QD = 256
PEER_TOPK = 16
PEER_BLOCK = 128
Q_BLOCK = 128
LN_EPS = 1e-5
RMS_EPS = 1e-5
ALPHA = (2.0 * DEPTH) ** 0.25
BETA = (8.0 * DEPTH) ** -0.25
_SPLITS = (DA_WIDTH, DA_WIDTH, DA_WIDTH, SA_WIDTH, SA_WIDTH, SA_WIDTH,
           IDX_HEADS * IDX_HD, IDX_HD, IDX_HEADS, D_MODEL, D_MODEL)
N_IN = sum(_SPLITS)

kernel_name = 'hybrid_diffattn_dsa_peer_step'

def _alibi_slopes(n):
    return jnp.asarray([2.0 ** (-8.0 * (i + 1) / n) for i in range(n)], dtype=jnp.float32)

def _layer_norm(x, g, b):
    xf = x.astype(jnp.float32)
    mu = jnp.mean(xf, -1, keepdims=True)
    var = jnp.mean(jnp.square(xf - mu), -1, keepdims=True)
    return ((xf - mu) * lax.rsqrt(var + LN_EPS) * g + b).astype(x.dtype)

def _in_proj(x, w_in):
    B, S, _ = x.shape
    z = jnp.einsum('bsd,dn->bsn', x, w_in)
    offs = np.cumsum(_SPLITS)[:-1].tolist()
    qa, ka, va, qs, ks, vs, qi, ki, wi, ga, gb = jnp.split(z, offs, axis=-1)
    return (qa.reshape(B, S, DA_HEADS, 2, DA_HD), ka.reshape(B, S, DA_HEADS, 2, DA_HD),
            va.reshape(B, S, DA_HEADS, 2 * DA_HD), qs.reshape(B, S, SA_HEADS, SA_HD),
            ks.reshape(B, S, SA_HEADS, SA_HD), vs.reshape(B, S, SA_HEADS, SA_HD),
            qi.reshape(B, S, IDX_HEADS, IDX_HD), ki, wi, ga, gb)

def _diff_lambda(lq1, lk1, lq2, lk2, lam_init):
    f = lambda a, b: jnp.exp(jnp.sum(a.astype(jnp.float32) * b.astype(jnp.float32)))
    return f(lq1, lk1) - f(lq2, lk2) + lam_init

def _diff_attend(q, k, v, q_pos, k_pos, lam, lam_init, subln_g):
    dist = (q_pos[:, None] - k_pos[None, :]).astype(jnp.float32)
    bias = jnp.where(dist >= 0, -_alibi_slopes(DA_HEADS)[:, None, None] * dist, -jnp.inf)
    s = jnp.einsum('bqhid,bkhid->bhiqk', q, k).astype(jnp.float32) * (DA_HD ** -0.5) + bias[None, :, None]
    p = jax.nn.softmax(s, axis=-1)
    attn = p[:, :, 0] - lam * p[:, :, 1]
    o = jnp.einsum('bhqk,bkhe->bqhe', attn.astype(v.dtype), v).astype(jnp.float32)
    o = o * lax.rsqrt(jnp.mean(o * o, -1, keepdims=True) + RMS_EPS) * subln_g * (1.0 - lam_init)
    return o.astype(v.dtype)

def _index_scores(qi, wi, ki):
    r = jax.nn.relu(jnp.einsum('bqhd,bld->bqhl', qi, ki).astype(jnp.float32) * (IDX_HD ** -0.5))
    return jnp.einsum('bqh,bqhl->bql', wi.astype(jnp.float32) * (IDX_HEADS ** -0.5), r)

def _select(scores, q_pos, k_pos, n_sel):
    valid = k_pos[None, :] <= q_pos[:, None]
    _, idx = lax.top_k(jnp.where(valid[None], scores, -jnp.inf), n_sel)
    return idx

def _sparse_attend(q, k_sel, v_sel, q_pos, sel_pos):
    dist = (q_pos[None, :, None] - sel_pos).astype(jnp.float32)[:, None]
    bias = jnp.where(dist >= 0, -_alibi_slopes(SA_HEADS)[None, :, None, None] * dist, -jnp.inf)
    s = jnp.einsum('bqhd,bqkhd->bhqk', q, k_sel).astype(jnp.float32) * (SA_HD ** -0.5) + bias
    p = jax.nn.softmax(s, axis=-1)
    return jnp.einsum('bhqk,bqkhd->bqhd', p.astype(v_sel.dtype), v_sel)

def _prompt_mixer(x, w_in, lam, lam_init, subln_g):
    B, S, _ = x.shape
    qa, ka, va, qs, ks, vs, qi, ki, wi, ga, gb = _in_proj(x, w_in)
    pos = jnp.arange(S)
    n_sel = min(TOPK_MAX, S // 4)
    bidx = jnp.arange(B)[:, None, None]

    def block(i):
        start = i * Q_BLOCK
        sl = lambda t: lax.dynamic_slice_in_dim(t, start, Q_BLOCK, axis=1)
        q_pos = start + jnp.arange(Q_BLOCK)
        a = _diff_attend(sl(qa), ka, va, q_pos, pos, lam, lam_init, subln_g)
        idx = _select(_index_scores(sl(qi), sl(wi), ki), q_pos, pos, n_sel)
        o = _sparse_attend(sl(qs), ks[bidx, idx], vs[bidx, idx], q_pos, idx)
        return a, o

    a, o = lax.map(block, jnp.arange(S // Q_BLOCK))
    a = jnp.moveaxis(a, 0, 1).reshape(B, S, DA_WIDTH)
    o = jnp.moveaxis(o, 0, 1).reshape(B, S, SA_WIDTH)
    return a, o, ga, gb, (ka, va, ks, vs, ki)

def _sample_mixer(x, w_in, lam, lam_init, subln_g, c_da_k, c_da_v, c_sa_k, c_sa_v, c_idx_k, page_table):
    B, S, _ = x.shape
    past = page_table.shape[1] * PAGE_SIZE
    L = past + S
    qa, ka, va, qs, ks, vs, qi, ki, wi, ga, gb = _in_proj(x, w_in)
    q_pos = past + jnp.arange(S)
    k_pos = jnp.arange(L)

    def paged(c):
        return c[page_table].reshape((B, past) + c.shape[2:])

    ka_all = jnp.concatenate([paged(c_da_k), ka], axis=1)
    va_all = jnp.concatenate([paged(c_da_v), va], axis=1)
    a = _diff_attend(qa, ka_all, va_all, q_pos, k_pos, lam, lam_init, subln_g)
    ki_all = jnp.concatenate([paged(c_idx_k), ki], axis=1)
    n_sel = min(TOPK_MAX, L // 4)
    idx = _select(_index_scores(qi, wi, ki_all), q_pos, k_pos, n_sel)
    bidx = jnp.arange(B)[:, None, None]
    in_past = (idx < past)[..., None, None]
    pidx = jnp.minimum(idx, past - 1)
    phys = page_table[bidx, pidx // PAGE_SIZE]
    row = pidx % PAGE_SIZE
    nidx = jnp.clip(idx - past, 0, S - 1)
    pick = lambda c, new: jnp.where(in_past, c[phys, row], new[bidx, nidx])
    o = _sparse_attend(qs, pick(c_sa_k, ks), pick(c_sa_v, vs), q_pos, idx)
    return a.reshape(B, S, DA_WIDTH), o.reshape(B, S, SA_WIDTH), ga, gb, (ka, va, ks, vs, ki)

def _peer(x, wq, sub_keys, u_tab, v_tab):
    shp = x.shape
    t = x.reshape(-1, D_MODEL)
    T = t.shape[0]
    q = (t @ wq).reshape(T, PEER_HEADS, 2, PEER_QD // 2)
    s = jnp.einsum('thcd,hcnd->thcn', q, sub_keys).astype(jnp.float32)
    sv, si = lax.top_k(s, PEER_TOPK)
    cand = sv[..., 0, :, None] + sv[..., 1, None, :]
    cand_id = si[..., 0, :, None] * PEER_NKEYS + si[..., 1, None, :]
    top_s, top_c = lax.top_k(cand.reshape(T, PEER_HEADS, -1), PEER_TOPK)
    experts = jnp.take_along_axis(cand_id.reshape(T, PEER_HEADS, -1), top_c, axis=-1)
    g = jax.nn.softmax(top_s, axis=-1)
    pad = (-T) % PEER_BLOCK
    nb = (T + pad) // PEER_BLOCK
    tp = jnp.pad(t, ((0, pad), (0, 0))).reshape(nb, PEER_BLOCK, D_MODEL)
    ep = jnp.pad(experts, ((0, pad), (0, 0), (0, 0))).reshape(nb, PEER_BLOCK, PEER_HEADS, PEER_TOPK)
    gp = jnp.pad(g, ((0, pad), (0, 0), (0, 0))).reshape(nb, PEER_BLOCK, PEER_HEADS, PEER_TOPK)

    def blk(args):
        xb, eb, gw = args
        pre = jnp.einsum('cd,chkd->chk', xb, u_tab[eb]).astype(jnp.float32)
        act = jax.nn.gelu(pre, approximate=False) * gw
        return jnp.einsum('chk,chkd->cd', act.astype(xb.dtype), v_tab[eb])

    out = lax.map(blk, (tp, ep, gp))
    return out.reshape(-1, D_MODEL)[:T].reshape(shp)

def _layer_tail(x, a, o, ga, gb, w_a_up, w_b_up, w_out, ln1_g, ln1_b, peer_wq, peer_sub_keys, peer_u, peer_v, ln2_g, ln2_b):
    merged = jax.nn.sigmoid(ga) * (a @ w_a_up) + jax.nn.sigmoid(gb) * (o @ w_b_up)
    h = _layer_norm(ALPHA * x + merged @ w_out, ln1_g, ln1_b)
    return _layer_norm(ALPHA * h + _peer(h, peer_wq, peer_sub_keys, peer_u, peer_v), ln2_g, ln2_b)

def setup_inputs(seed: int = 0) -> dict:
    key = jax.random.key(seed)
    ks = jax.random.split(key, 24)
    f32 = jnp.float32
    nrm = lambda k, shp, s: jax.random.normal(k, shp, f32) * s
    n_pages = PAST_LEN // PAGE_SIZE
    n_used = DEC_BATCH * n_pages
    n_pool = n_used + max(1, n_used // 4)
    page_table = jax.random.permutation(ks[7], n_pool)[:n_used].reshape(DEC_BATCH, n_pages).astype(jnp.int32)
    col_scale = [1.0, 1.0, BETA, 1.0, 1.0, BETA, 1.0, 1.0, 1.0, 1.0, 1.0]
    col_scale = jnp.concatenate([jnp.full((n,), s, f32) for n, s in zip(_SPLITS, col_scale)])
    return {
        'x_prompt': nrm(ks[0], (BATCH, SEQ, D_MODEL), 1.0),
        'x_sample': nrm(ks[1], (DEC_BATCH, DEC_SEQ, D_MODEL), 1.0),
        'cache_da_k': nrm(ks[2], (DEPTH, n_pool, PAGE_SIZE, DA_HEADS, 2, DA_HD), 1.0),
        'cache_da_v': nrm(ks[3], (DEPTH, n_pool, PAGE_SIZE, DA_HEADS, 2 * DA_HD), BETA),
        'cache_sa_k': nrm(ks[4], (DEPTH, n_pool, PAGE_SIZE, SA_HEADS, SA_HD), 1.0),
        'cache_sa_v': nrm(ks[5], (DEPTH, n_pool, PAGE_SIZE, SA_HEADS, SA_HD), BETA),
        'cache_idx_k': nrm(ks[6], (DEPTH, n_pool, PAGE_SIZE, IDX_HD), 1.0),
        'page_table': page_table,
        'w_in': nrm(ks[8], (DEPTH, D_MODEL, N_IN), D_MODEL ** -0.5) * col_scale,
        'lambda_q1': nrm(ks[9], (DEPTH, DA_HD), 0.1),
        'lambda_k1': nrm(ks[10], (DEPTH, DA_HD), 0.1),
        'lambda_q2': nrm(ks[11], (DEPTH, DA_HD), 0.1),
        'lambda_k2': nrm(ks[12], (DEPTH, DA_HD), 0.1),
        'da_subln_g': 1.0 + nrm(ks[13], (DEPTH, 2 * DA_HD), 0.02),
        'w_a_up': nrm(ks[14], (DEPTH, DA_WIDTH, D_MODEL), DA_WIDTH ** -0.5),
        'w_b_up': nrm(ks[15], (DEPTH, SA_WIDTH, D_MODEL), SA_WIDTH ** -0.5),
        'w_out': nrm(ks[16], (DEPTH, D_MODEL, D_MODEL), BETA * D_MODEL ** -0.5),
        'ln1_g': 1.0 + nrm(ks[17], (DEPTH, D_MODEL), 0.02),
        'ln1_b': nrm(ks[18], (DEPTH, D_MODEL), 0.02),
        'peer_wq': nrm(ks[19], (DEPTH, D_MODEL, PEER_HEADS * PEER_QD), D_MODEL ** -0.5),
        'peer_sub_keys': nrm(ks[20], (DEPTH, PEER_HEADS, 2, PEER_NKEYS, PEER_QD // 2), (PEER_QD // 2) ** -0.5),
        'peer_u': nrm(ks[21], (DEPTH, PEER_N, D_MODEL), D_MODEL ** -0.5),
        'peer_v': nrm(ks[22], (DEPTH, PEER_N, D_MODEL), BETA),
        'ln2_g': 1.0 + nrm(ks[23], (DEPTH, D_MODEL), 0.02),
        'ln2_b': nrm(jax.random.fold_in(ks[23], 1), (DEPTH, D_MODEL), 0.02),
    }

def reference(x_prompt, x_sample, cache_da_k, cache_da_v, cache_sa_k, cache_sa_v, cache_idx_k, page_table,
              w_in, lambda_q1, lambda_k1, lambda_q2, lambda_k2, da_subln_g, w_a_up, w_b_up, w_out,
              ln1_g, ln1_b, peer_wq, peer_sub_keys, peer_u, peer_v, ln2_g, ln2_b):
    y_p, y_s = x_prompt, x_sample
    p_new, s_new = [], []
    for l in range(DEPTH):
        lam_init = 0.8 - 0.6 * math.exp(-0.3 * l)
        lam = _diff_lambda(lambda_q1[l], lambda_k1[l], lambda_q2[l], lambda_k2[l], lam_init)
        tail = (w_a_up[l], w_b_up[l], w_out[l], ln1_g[l], ln1_b[l], peer_wq[l], peer_sub_keys[l],
                peer_u[l], peer_v[l], ln2_g[l], ln2_b[l])
        a, o, ga, gb, st = _prompt_mixer(y_p, w_in[l], lam, lam_init, da_subln_g[l])
        y_p = _layer_tail(y_p, a, o, ga, gb, *tail)
        p_new.append(st)
        a, o, ga, gb, st = _sample_mixer(y_s, w_in[l], lam, lam_init, da_subln_g[l], cache_da_k[l], cache_da_v[l],
                                         cache_sa_k[l], cache_sa_v[l], cache_idx_k[l], page_table)
        y_s = _layer_tail(y_s, a, o, ga, gb, *tail)
        s_new.append(st)
    stk = lambda lst, j: jnp.stack([e[j] for e in lst])
    return (y_p, y_s,
            stk(p_new, 0), stk(p_new, 1), stk(p_new, 2), stk(p_new, 3), stk(p_new, 4),
            stk(s_new, 0), stk(s_new, 1), stk(s_new, 2), stk(s_new, 3), stk(s_new, 4))


_drawn_inputs = setup_inputs


def setup_inputs(seed=0):
    import zlib

    import numpy as np

    out = dict(_drawn_inputs(seed))
    spreads = {}
    factors = {'lambda_q1': 3.225,
     'lambda_k1': 6.378,
     'ln2_g': 8.463,
     'ln2_b': 8.061,
     'da_subln_g': 2.914}
    for name, (base, spread) in spreads.items():
        noise = np.random.default_rng([zlib.crc32(name.encode()), seed]).standard_normal(out[name].shape)
        drawn = base * np.exp(spread * noise) if base else spread * noise
        out[name] = __import__('jax').numpy.asarray(drawn.astype(out[name].dtype))
    for name, factor in factors.items():
        out[name] = (out[name] * factor).astype(out[name].dtype)
    return out
```

```python
import math
from contextlib import ExitStack

import numpy as np

import concourse.bass as bass
import concourse.mybir as mybir

F32 = mybir.dt.float32
U32 = mybir.dt.uint32
I32 = mybir.dt.int32
ALU = mybir.AluOpType
ACT = mybir.ActivationFunctionType
AX = mybir.AxisListType

P = 128
D = 1024
DC = D // P
TP, TS = 256, 8
T = TP + TS
PAST = 256
PAGE = 128
PAGES = PAST // PAGE
KEYS = PAST + 1
HD = 64
SUBHEADS = 8
NSEL = 64
SCALE = HD ** -0.5
ALPHA = 2.0 ** 0.25
LAM_INIT = 0.8 - 0.6 * math.exp(0.0)
EPS = 1e-5
NEG = -1e30
TAKEN = -3e38
HC = 16
NK = 128
TOP = 16
TOKEN_TILES = [(0, P), (P, P), (TP, TS)]

QA, QS, QI, KA, KS, VA, VS, KI, WI, GA, GB = 0, 4, 8, 12, 16, 20, 24, 28, 29, 30, 38
Z_TILES, GATE_TILES = 30, 16
UP_AT = Z_TILES + GATE_TILES
OUT_AT = UP_AT + DC
WQ_AT = OUT_AT + DC
TILES = WQ_AT + HC
RING = 4
KV_TILES = KI + 1 - KA

C_IDENT, C_ONES, C_IOTA, C_IOTA16 = 0, P, 2 * P, 3 * P
C_EXPAND = C_IOTA16 + TOP
C_HEADROW = C_EXPAND + 64
C_DIAG = C_HEADROW + 64
CONSTS = C_DIAG + TS
B_SPARSE, B_CAUSAL = 4, 12
BIASES = 13
SMALL = 1736
SB_FIRST, SB_SECOND, SBIAS = 2 * KEYS, 2 * KEYS + 1, 2 * KEYS + 2
P_LN1G, P_LN1B, P_LN2G, P_LN2B, P_SUBLN, P_LAM, PARAMS = 0, 8, 16, 24, 32, 33, 37

SCORE_UNITS = [(0, 0, 0, 4), (0, 1, 0, 4), (1, 0, 0, 2), (1, 0, 2, 2), (1, 1, 0, 2), (1, 1, 2, 2)]
PT_TILES = [(0, 0), (1, 0), (1, 1)]

UNIT_ORDER = (["wi"] + [f"idx{u}" for u in range(6)] + ["v_diff0", "v_diff1", "v_sparse0", "v_sparse1"]
              + [f"diff{u}" for u in range(6)] + ["isum"] + [f"sparse{u}" for u in range(6)]
              + [f"diffT{u}" for u in range(3)] + ["diff_o0", "diff_o1"]
              + [f"sparseT{u}" for u in range(6)] + ["sparse_o0", "sparse_o1"]
              + ["sampT", "samp_o"] + [f"rms{u}" for u in range(3)])
UNIT = {name: n for n, name in enumerate(UNIT_ORDER)}
ROT, ROT_AT = 3, 5


def build_program(nc, x_t, weights, experts_u, experts_v, k_diff, k_sparse, k_idx, v_diff, v_sparse,
                  page_table, sub_keys, params, consts, alibi, sample_bias, kv_out, y_out):
    with ExitStack() as ctx:
        def region(name, words, dt=F32, parts=P):
            return ctx.enter_context(nc.sbuf_tensor(name, [parts, words], dt))

        names = """x_loaded consts_loaded params_loaded alibi_loaded table_loaded subkeys_loaded
            tiles_done z_even_free z_odd_free kv_stored y_stored
            unit_filled qpad_zero qpad_ready wi_ready lam_products lam_ready pool_chain dve_chain act_chain
            relu_done idx_sum relu_sample isum_weight isum_copied sel_prompt sel_sample sample_mask_used
            bias_masked k_ready k_used v_ready v_used sample_scored gates_done
            diff_max diff_exp diff_attn sparse_max sparse_exp sparse_attn
            samp_max samp_exp samp_attn samp_att_ready out_sample_ready
            rms_square rms_recip rms_root up_free merged out_free
            ln_stat ln_centred ln_square ln_recip ln_root ln_done
            q_evac score_filled score_free u_done gelu_done route_ready route_exp gates_normed
            route_filled route_copied p2_ready g_filled g_free
            v_filled acc_added acc_ready""".split()
        S = {n: ctx.enter_context(nc.semaphore(n)) for n in names}
        w_loaded = [ctx.enter_context(nc.semaphore(f"w_loaded{s}")) for s in range(RING)]
        v_loaded = [ctx.enter_context(nc.semaphore(f"v_loaded{s}")) for s in range(2)]
        k_loaded = [ctx.enter_context(nc.semaphore(f"k_loaded{s}")) for s in range(2)]
        vc_loaded = [ctx.enter_context(nc.semaphore(f"vc_loaded{s}")) for s in range(2)]
        drained = [ctx.enter_context(nc.semaphore(f"drained{s}")) for s in range(ROT)]

        ring = region("ring", RING * D)
        xt = region("xt", DC * T)
        ht = region("ht", DC * T)
        cst = region("cst", CONSTS)
        par = region("par", PARAMS)
        table = region("table", PAGES * TS, I32, 1)
        sbias = region("sbias", SBIAS)
        arena = region("arena", P * T)
        work = region("work", 8192)
        small = region("small", SMALL)

        class Carve:
            def __init__(self, of):
                self.of, self.at = of, 0

            def __call__(self, words):
                self.at += words
                return self.of[:, self.at - words:self.at]

        a = Carve(arena)
        z = a(Z_TILES * T).rearrange("p (n t) -> p n t", t=T)
        gate = a(GATE_TILES * T).rearrange("p (n t) -> p n t", t=T)
        qpad_flat = a(2 * 2048 + 512)
        qpad = {"diff": qpad_flat[:, 0:2048].rearrange("p (j b n) -> p j b n", j=4, b=TS),
                "sparse": qpad_flat[:, 2048:4096].rearrange("p (j b n) -> p j b n", j=4, b=TS),
                "idx": qpad_flat[:, 4096:4608].rearrange("p (b n) -> p b n", b=TS)}
        kbuf = [{"diff": a(4 * KEYS).rearrange("p (j k) -> p j k", j=4),
                 "sparse": a(4 * KEYS).rearrange("p (j k) -> p j k", j=4),
                 "idx": a(KEYS)} for _ in range(2)]
        vbuf = [{"diff": a(PAGES * 512).rearrange("p (g e) -> p g e", g=PAGES),
                 "sparse": a(PAGES * 512).rearrange("p (g e) -> p g e", g=PAGES)} for _ in range(2)]
        bias = a(BIASES * 256).rearrange("p (n k) -> p n k", n=BIASES)
        s_diff = a(8 * 384)
        gelu_all = arena[:, :].rearrange("p (b t) -> p b t", t=T)
        o_diff, o_sparse = z[:, QI:QI + 4, :], z[:, QA:QA + 4, :]
        merged = z[:, KA:KA + DC, :]

        w = Carve(work)
        s_sparse = w(8 * 384)
        pt = w(8 * 3 * P).rearrange("p (n q) -> p n q", q=P)
        v_tok = {k: w(2 * 512).rearrange("p (g e) -> p g e", g=2) for k in ("diff", "sparse")}
        pre = work[:, 0:DC * T].rearrange("p (c t) -> p c t", c=DC)
        squares = work[:, 8 * 384:8 * 384 + DC * T]
        subk = work[:, 6144:8192].rearrange("p (n k) -> p n k", n=HC)
        route_val = work[:, 0:768].rearrange("p (g n k) -> p g n k", g=3, n=HC)
        route_idx = work[:, 768:1536].bitcast(U32).rearrange("p (g n k) -> p g n k", g=3, n=HC)
        route_idxf = work[:, 1536:2304].rearrange("p (g n k) -> p g n k", g=3, n=HC)
        cand = work[:, 3072:5120]
        onehot = work[:, 5120:7168]
        rest = [work[:, 7168 + 256 * n:7424 + 256 * n] for n in range(2)]
        p1 = work[:, 0:1024].rearrange("p (s k) -> p s k", s=8)
        p2 = work[:, 1024:2048].rearrange("p (s k) -> p s k", s=8)
        vring = [ring[:, :].rearrange("p (s n) -> p s n", s=4),
                 work[:, 3072:7168].rearrange("p (s n) -> p s n", s=4)]

        c = Carve(small)
        mx = c(32)
        sums = c(32)
        recip = c(32)
        lam = c(4)
        neglam = c(1)
        head_w = c(2 * 8 + 8)
        wsel = c(8)
        samp_small = c(8)
        top8 = c(3 * 8)
        phase = c.at
        iscore = [c(P), c(256), c(KEYS)]
        s_samp = {"diff": c(KEYS), "sparse": c(KEYS)}
        relu_samp = s_samp["diff"]
        new_diag = [iscore[1][:, 0:64], iscore[1][:, 64:128]]
        att = c(288)
        new_part = c(64)
        assert c.at <= SMALL, c.at
        c.at = phase
        ln_mean, ln_root = c(T), c(T)
        c.at = phase
        up_tmp = [c(T), c(T)]
        c.at = phase
        q_sb = [c(T), c(T)]
        rest128 = [c(P) for _ in range(3)]
        c.at = phase
        top_val = c(3 * P).rearrange("p (g n) -> p g n", g=3)
        top_pos = c(P).bitcast(U32)
        pos_part = c(P).bitcast(U32)
        pos_f = c(P)
        first_id = c(3 * P).rearrange("p (g n) -> p g n", g=3)
        second_id = c(3 * P).rearrange("p (g n) -> p g n", g=3)
        denom = c(24).rearrange("p (g n) -> p g n", g=3)
        assert c.at <= SMALL, c.at
        slot_first, slot_second, slot_gate = (work[:, 2048:2048 + T], work[:, 2048 + T:2048 + 2 * T],
                                              work[:, 2048 + 2 * T:2048 + 3 * T])

        ident = cst[:, C_IDENT:C_IDENT + P]
        ones = cst[:, C_ONES:C_ONES + P]
        iota = cst[:, C_IOTA:C_IOTA + P]
        iota16 = cst[:, C_IOTA16:C_IOTA16 + TOP]

        psum = ctx.enter_context(nc.psum_tensor("psum", [P, 8, 512], F32))

        def bank(name):
            return psum[:, ROT_AT + UNIT[name] % ROT, :]

        def s_view(buf, qt):
            return (buf[:, 0:1024] if qt == 0 else buf[:, 1024:3072]).rearrange("p (m k) -> p m k", m=8)

        def of_unit(heads, unit):
            _, i, j0, n = unit
            return heads.rearrange("p (j i) k -> p i j k", i=2)[:, i, j0:j0 + n, :]

        def await_unit(eng, name):
            eng.wait_ge(S["unit_filled"], UNIT[name] + 1)

        def drain_unit(ins, name):
            ins.then_inc(drained[UNIT[name] % ROT], 1)

        def await_drained(eng, name):
            eng.wait_ge(drained[UNIT[name] % ROT], UNIT[name] // ROT + 1)

        class Chain:
            def __init__(self, eng, sem):
                self.eng, self.sem, self.n = eng, sem, 0

            def put(self, ins):
                self.n += 1
                ins.then_inc(self.sem, 1)

            def settle(self):
                self.eng.wait_ge(self.sem, self.n)

            def __call__(self, ins):
                self.put(ins)
                self.settle()

        uses = [len(range(s, TILES, RING)) for s in range(RING)]
        U_SLOT = TILES % RING

        block = ctx.enter_context(nc.Block())

        @block.sync
        def _(sp):
            sp.dma_start(xt[:, :], x_t).then_inc(S["x_loaded"], 16)
            for t in range(RING):
                sp.dma_start(ring[:, t * D:(t + 1) * D], weights[t]).then_inc(w_loaded[t], 16)

            def load_tile(i, s, t):
                sp.wait_ge(S["tiles_done"], t - RING + 1)
                sp.dma_start(ring[:, s * D:(s + 1) * D], weights[t]).then_inc(w_loaded[s], 16)

            with sp.Fori(1, TILES // RING) as i:
                for s in range(RING):
                    load_tile(i, s, i * RING + s)
            for t in range(TILES // RING * RING, TILES):
                load_tile(0, t % RING, t)

            for b in range(RING):
                s = (U_SLOT + b) % RING
                sp.wait_ge(S["tiles_done"], TILES - RING + b + 1)
                sp.dma_start(ring[:, s * D:(s + 1) * D], experts_u[b]).then_inc(w_loaded[s], 16)
            with sp.Fori(1, NK // RING) as i:
                for k in range(RING):
                    s = (U_SLOT + k) % RING
                    sp.wait_ge(S["u_done"], i * RING + k - RING + 1)
                    sp.dma_start(ring[:, s * D:(s + 1) * D], experts_u[i * RING + k]).then_inc(w_loaded[s], 16)

            sp.wait_ge(S["u_done"], NK)
            sp.dma_start(vring[0], experts_v[0:4].rearrange("b p n -> p b n")).then_inc(v_loaded[0], 16)
            sp.wait_ge(S["gates_normed"], 1)
            sp.dma_start(vring[1], experts_v[4:8].rearrange("b p n -> p b n")).then_inc(v_loaded[1], 16)
            with sp.Fori(1, NK // 8) as i:
                for q in range(2):
                    sp.wait_ge(S["v_filled"], (i * 2 + q - 1) * DC)
                    sp.dma_start(vring[q], experts_v[bass.ds(i * 8 + q * 4, 4)].rearrange("b p n -> p b n"))\
                        .then_inc(v_loaded[q], 16)
            sp.wait_ge(S["ln_done"], 2 * DC)
            sp.dma_start(y_out, pre).then_inc(S["y_stored"], 16)
            sp.wait_ge(S["y_stored"], 16)
            sp.wait_ge(S["kv_stored"], 16)

        @block.gpsimd
        def _(pool):
            chain = Chain(pool, S["pool_chain"])
            pool.dma_start(table[:, :], page_table).then_inc(S["table_loaded"], 16)
            pool.memset(qpad_flat, 0.0).then_inc(S["qpad_zero"], 1)
            pool.wait_ge(S["table_loaded"], 16)

            def page_of(b, g):
                return pool.value_load(table[0:1, b * PAGES + g:b * PAGES + g + 1], min_val=0,
                                       max_val=k_idx.shape[0] - 1)

            def load_keys(b):
                buf, sem = kbuf[b % 2], k_loaded[b % 2]
                for g in range(PAGES):
                    page = page_of(b, g)
                    cols = slice(g * PAGE, (g + 1) * PAGE)
                    pool.dma_start(buf["diff"][:, :, cols], k_diff[bass.ds(page, 1)].rearrange("o p j k -> p (o j) k"))\
                        .then_inc(sem, 16)
                    pool.dma_start(buf["sparse"][:, :, cols], k_sparse[bass.ds(page, 1)].rearrange("o p j k -> p (o j) k"))\
                        .then_inc(sem, 16)
                    pool.dma_start(buf["idx"][:, cols], k_idx[bass.ds(page, 1)].rearrange("o p k -> p (o k)"))\
                        .then_inc(sem, 16)

            def load_values(b):
                for g in range(PAGES):
                    page = page_of(b, g)
                    for kind, cache in (("diff", v_diff), ("sparse", v_sparse)):
                        pool.dma_start(vbuf[b % 2][kind][:, g, :], cache[bass.ds(page, 1)].rearrange("o p e -> p (o e)"))\
                            .then_inc(vc_loaded[b % 2], 16)

            load_keys(0)
            load_keys(1)
            load_values(0)
            load_values(1)
            pool.wait_ge(S["z_even_free"], 1 + Z_TILES // 2)
            pool.wait_ge(S["z_odd_free"], 1 + Z_TILES // 2)
            pool.dma_start(kv_out, z[:, KA:KI + 1, :]).then_inc(S["kv_stored"], 16)
            for b in range(TS):
                buf = kbuf[b % 2]
                pool.wait_ge(k_loaded[b % 2], 96 * (b // 2 + 1))
                chain.put(pool.tensor_copy(buf["diff"][:, :, PAST], z[:, KA:KA + 4, TP + b]))
                chain.put(pool.tensor_copy(buf["sparse"][:, :, PAST], z[:, KS:KS + 4, TP + b]))
                pool.tensor_copy(buf["idx"][:, PAST:KEYS], z[:, KI, TP + b:TP + b + 1]).then_inc(S["k_ready"], 1)
                if b + 2 < TS:
                    pool.wait_ge(S["k_used"], b + 1)
                    load_keys(b + 2)
            for qt in range(2):
                pool.wait_ge(S["sel_prompt"], qt + 1)
                keys = P if qt == 0 else 2 * P
                table_cols = bias[:, B_SPARSE:B_SPARSE + 8, 256 - keys:256]
                pool.tensor_tensor(s_view(s_sparse, qt), table_cols,
                                   iscore[qt].unsqueeze(1).to_broadcast([P, 8, keys]), ALU.add)\
                    .then_inc(S["bias_masked"], 1)
            for b in range(2, TS):
                pool.wait_ge(S["v_used"], b - 1)
                load_values(b)
            await_unit(pool, "sparse_o1")
            pool.dma_start(subk, sub_keys).then_inc(S["subkeys_loaded"], 16)
            pool.sem_inc(S["merged"], 2)
            with pool.Fori(0, 2) as i:
                for k in range(4):
                    n = i * 4 + k
                    pool.wait_ge(S["up_free"], 2 + n + 1)
                    pool.wait_ge(S["table_loaded"], 16)
                    m = merged[:, bass.ds(n, 1), :].rearrange("p o t -> p (o t)")
                    pool.tensor_tensor(m, m, up_tmp[k % 2], ALU.add).then_inc(S["merged"], 1)

        @block.scalar
        def _(act):
            act.dma_start(cst[:, :], consts).then_inc(S["consts_loaded"], 16)
            act.dma_start(par[:, :], params).then_inc(S["params_loaded"], 16)
            act.dma_start(bias, alibi).then_inc(S["alibi_loaded"], 16)
            act.dma_start(sbias[0:64, :], sample_bias).then_inc(S["alibi_loaded"], 16)
            act.sem_inc(S["z_even_free"], 1)
            act.wait_ge(S["consts_loaded"], 16)

            def evac_z(n, tile):
                act.wait_ge(S["tiles_done"], tile + 1)
                act.wait_ge(S["consts_loaded"], 16)
                act.activation(z[:, bass.ds(tile, 1), :].rearrange("p o t -> p (o t)"), psum[:, 0, 0:T], ACT.Copy)\
                    .then_inc(S["z_even_free"], 1)

            with act.Fori(0, Z_TILES // 2) as i:
                evac_z(i, i * 2)
            await_unit(act, "wi")
            act.activation(lam[:, 2:4], bank("wi")[:, 128:130], ACT.Exp).then_inc(S["lam_ready"], 1)
            for u, unit in enumerate(SCORE_UNITS):
                await_unit(act, f"idx{u}")
                qt, keys = unit[0], P * (unit[0] + 1)
                drain_unit(act.activation(of_unit(s_view(s_sparse, qt), unit),
                                          bank(f"idx{u}").rearrange("p (m k) -> p m k", k=keys),
                                          ACT.Relu, scale=SCALE), f"idx{u}")
            for kind in ("diff", "sparse"):
                for kt in range(2):
                    await_unit(act, f"v_{kind}{kt}")
                    drain_unit(act.activation(v_tok[kind][:, kt, :], bank(f"v_{kind}{kt}"), ACT.Copy), f"v_{kind}{kt}")
            act.wait_ge(S["sample_scored"], 1)
            act.activation(relu_samp[0:64, :], psum[0:64, 4, 0:KEYS], ACT.Relu, scale=SCALE)\
                .then_inc(S["relu_sample"], 1)

            def evac_gate(i, k):
                n = i * 4 + k
                act.wait_ge(S["tiles_done"], Z_TILES + n + 1)
                act.wait_ge(S["consts_loaded"], 16)
                act.activation(gate[:, bass.ds(n, 1), :].rearrange("p o t -> p (o t)"), psum[:, k % 2, 0:T],
                               ACT.Sigmoid).then_inc(S[("z_even_free", "z_odd_free")[k % 2]], 1)

            with act.Fori(0, GATE_TILES // 4) as i:
                for k in range(4):
                    evac_gate(i, k)

            def prompt_exp(kind, buf, col):
                for u, (qt, i, j0, n) in enumerate(SCORE_UNITS):
                    act.wait_ge(S[f"{kind}_max"], u + 1)
                    for m in range(2 * j0 + i, 2 * (j0 + n) + i, 2):
                        at = col + qt * 8 + m
                        row = s_view(buf, qt)[:, m, :]
                        act.activation(row, row, ACT.Exp, bias=mx[:, at:at + 1], accum_out=sums[:, at:at + 1])\
                            .then_inc(S[f"{kind}_exp"], 1)

            def sample_exp(n, kind):
                act.wait_ge(S["samp_max"], n + 1)
                act.activation(s_samp[kind][0:64, :], s_samp[kind][0:64, :], ACT.Exp,
                               bias=samp_small[0:64, n:n + 1], accum_out=samp_small[0:64, 2 + n:3 + n])\
                    .then_inc(S["samp_exp"], 1)

            prompt_exp("diff", s_diff, 0)
            prompt_exp("sparse", s_sparse, 16)
            sample_exp(0, "diff")
            sample_exp(1, "sparse")

            def evac_pt(kind, u):
                name = f"{kind}T{u}"
                await_unit(act, name)
                drain_unit(act.activation(pt[:, 4 * u:4 * u + 4, :].rearrange("p n q -> p (n q)"), bank(name), ACT.Copy), name)

            def evac_o(kind, u, dst):
                name = f"{kind}_o{u}"
                await_unit(act, name)
                drain_unit(act.activation(dst[:, 2 * u:2 * u + 2, 0:TP], bank(name).rearrange("p (j q) -> p j q", j=2),
                                          ACT.Copy), name)

            for u in range(3):
                evac_pt("diff", u)
            for u in range(2):
                evac_o("diff", u, o_diff)
            for u in range(6):
                evac_pt("sparse", u)
            for u in range(2):
                evac_o("sparse", u, o_sparse)
            act.wait_ge(S["out_sample_ready"], 1)
            await_drained(act, "sparse_o1")
            act.activation(s_diff[:, 0:4 * T], o_diff.rearrange("p j t -> p (j t)"), ACT.Square)\
                .then_inc(S["rms_square"], 1)
            act.wait_ge(S["rms_recip"], 1)
            act.activation(s_diff[:, 4 * T:8 * T], s_diff[:, 4 * T:8 * T], ACT.Sqrt).then_inc(S["rms_root"], 1)

            def norm(n):
                act.wait_ge(S["ln_centred"], n + 1)
                act.activation(squares, pre.rearrange("p c t -> p (c t)"), ACT.Square).then_inc(S["ln_square"], 1)
                act.wait_ge(S["ln_recip"], n + 1)
                act.activation(ln_root, ln_root, ACT.Sqrt).then_inc(S["ln_root"], 1)

            norm(0)
            act.sem_inc(S["q_evac"], 2)
            with act.Fori(0, HC // 4) as i:
                for k in range(4):
                    act.wait_ge(S["score_filled"], i * 4 + k + 1)
                    act.wait_ge(S["tiles_done"], WQ_AT + i * 4 + k + 1)
                    act.activation(q_sb[k % 2], psum[:, k % 2, 0:T], ACT.Copy).then_inc(S["q_evac"], 1)
            act.sem_inc(S["gelu_done"], 4)
            with act.Fori(0, NK // RING) as i:
                for k in range(RING):
                    act.wait_ge(S["u_done"], i * RING + k + 1)
                    act.wait_ge(S["consts_loaded"], 16)
                    act.activation(gelu_all[:, bass.ds(i * RING + k, 1), :].rearrange("p o t -> p (o t)"),
                                   psum[:, 4 + k, 0:T], ACT.Gelu).then_inc(S["gelu_done"], 1)
            act.wait_ge(S["route_ready"], 1)
            for n, (_, rows) in enumerate(TOKEN_TILES):
                act.activation(top_val[0:rows, n, :], top_val[0:rows, n, :], ACT.Exp).then_inc(S["route_exp"], 1)
            norm(1)

        @block.vector
        def _(dve):
            chain = Chain(dve, S["dve_chain"])
            dve.sem_inc(S["z_odd_free"], 1)
            dve.wait_ge(S["params_loaded"], 16)
            dve.tensor_tensor(lam[0:64, 0:2], par[0:64, P_LAM:P_LAM + 2], par[0:64, P_LAM + 2:P_LAM + 4], ALU.mult)\
                .then_inc(S["lam_products"], 1)
            with dve.Fori(0, Z_TILES // 2) as i:
                dve.wait_ge(S["tiles_done"], i * 2 + 2)
                dve.wait_ge(S["params_loaded"], 16)
                dve.tensor_copy(z[:, bass.ds(i * 2 + 1, 1), :].rearrange("p o t -> p (o t)"), psum[:, 1, 0:T])\
                    .then_inc(S["z_odd_free"], 1)

            dve.wait_ge(S["qpad_zero"], 1)
            dve.wait_ge(S["z_even_free"], 1 + Z_TILES // 2)
            dve.wait_ge(S["z_odd_free"], 1 + Z_TILES // 2)
            for kind, at, tile, steps in (("diff", 0, QA, (514, 72)), ("sparse", 2048, QS, (514, 72)),
                                          ("idx", 4096, QI, (2, 72))):
                for i in range(2):
                    half = slice(i * HD, (i + 1) * HD)
                    spread = qpad_flat[half, at + i:at + i + 1]
                    dst = bass.AP(spread.tensor, spread.offset,
                                  [list(spread.ap[0]), [steps[0], 4], [steps[1], TS]])
                    dve.tensor_copy(dst, z[half, tile:tile + 4, TP:T]).then_inc(S["qpad_ready"], 1)

            await_unit(dve, "wi")
            dve.wait_ge(S["lam_ready"], 1)
            chain.put(dve.tensor_scalar(head_w[:, 0:16], bank("wi")[:, 0:16], SUBHEADS ** -0.5, None, ALU.mult))
            chain(dve.tensor_scalar(head_w[0:64, 16:24], bank("wi")[0:64, 16:24], SUBHEADS ** -0.5, None, ALU.mult))
            drain_unit(dve.tensor_tensor(wsel[0:64, :], head_w[0:64, 16:24], cst[0:64, C_DIAG:C_DIAG + TS],
                                         ALU.mult), "wi")
            chain(dve.tensor_tensor(neglam, lam[:, 3:4], lam[:, 2:3], ALU.subtract))
            chain(dve.tensor_scalar(neglam, neglam, -LAM_INIT, None, ALU.add))

            dve.wait_ge(S["alibi_loaded"], 32)
            for qt in range(2):
                keys = P * (qt + 1)
                for m in range(SUBHEADS):
                    u = next(u for u, (g, i, j0, n) in enumerate(SCORE_UNITS)
                             if g == qt and i == m % 2 and j0 <= m // 2 < j0 + n)
                    await_drained(dve, f"idx{u}")
                    r = s_view(s_sparse, qt)[:, m, :]
                    weight = head_w[:, qt * 8 + m:qt * 8 + m + 1]
                    if m == 0:
                        chain(dve.tensor_scalar(iscore[qt], r, weight, None, ALU.mult))
                    else:
                        chain(dve.scalar_tensor_tensor(iscore[qt], r, weight, iscore[qt], ALU.mult, ALU.add))
                chain(dve.tensor_tensor(iscore[qt], iscore[qt], bias[:, B_CAUSAL, 256 - keys:256], ALU.add))

            def score(kind, buf, col, u):
                qt, i, j0, n = unit = SCORE_UNITS[u]
                keys = P * (qt + 1)
                name = f"{kind}{u}"
                await_unit(dve, name)
                src = bank(name).rearrange("p (m k) -> p m k", k=keys)
                dst = of_unit(s_view(buf, qt), unit)
                if kind == "diff":
                    added = bias[:, j0:j0 + n, 256 - keys:256]
                else:
                    dve.wait_ge(S["bias_masked"], qt + 1)
                    added = dst
                drain_unit(dve.scalar_tensor_tensor(dst, src, SCALE, added, ALU.mult, ALU.add), name)
                await_drained(dve, name)
                rows_max = mx[:, col + qt * 8:col + qt * 8 + 8].rearrange("p (j i) -> p i j", i=2)[:, i, j0:j0 + n]
                dve.tensor_reduce(rows_max, dst, AX.X, ALU.max, negate=True)\
                    .then_inc(S[f"{kind}_max"], 1)

            for u in range(6):
                score("diff", s_diff, 0, u)

            await_unit(dve, "isum")
            drain_unit(dve.tensor_copy(iscore[2][0:TS, :], bank("isum")[0:TS, 0:KEYS]), "isum")
            await_drained(dve, "isum")
            rows = [P, P, TS]
            for r in range(NSEL // 8):
                for n in range(3):
                    chain.put(dve.max(top8[0:rows[n], 8 * n:8 * n + 8], iscore[n][0:rows[n], :]))
                chain.settle()
                for n in range(3):
                    chain.put(dve.match_replace(iscore[n][0:rows[n], :], top8[0:rows[n], 8 * n:8 * n + 8],
                                                iscore[n][0:rows[n], :], TAKEN))
                chain.settle()
            for n in (0, 1, 2):
                dve.tensor_scalar(iscore[n][0:rows[n], :], iscore[n][0:rows[n], :], TAKEN * 0.97, NEG,
                                  ALU.is_gt, ALU.mult).then_inc(S["sel_prompt" if n < 2 else "sel_sample"], 1)

            def reciprocals(kind, col):
                dve.wait_ge(S[f"{kind}_exp"], 16)
                chain(dve.reciprocal(recip[:, col:col + 16], sums[:, col:col + 16]))

            reciprocals("diff", 0)
            odd = recip[:, 0:16].rearrange("p (m i) -> p m i", i=2)[:, :, 1]
            chain(dve.tensor_scalar(odd, odd, neglam, None, ALU.mult))
            for qt in range(2):
                s = s_view(s_diff, qt)
                keys = P * (qt + 1)
                chain(dve.tensor_tensor(s, s, recip[:, qt * 8:qt * 8 + 8].unsqueeze(2).to_broadcast([P, 8, keys]), ALU.mult))
                pairs = s.rearrange("p (j i) k -> p j i k", i=2)
                dve.tensor_tensor(pairs[:, :, 0, :], pairs[:, :, 0, :], pairs[:, :, 1, :], ALU.add)\
                    .then_inc(S["diff_attn"], 1)
            for u in range(6):
                score("sparse", s_sparse, 16, u)
            for n, kind in enumerate(("diff", "sparse")):
                dve.wait_ge(S["sample_scored"], 1 + n)
                chain(dve.scalar_tensor_tensor(s_samp[kind][0:64, :], psum[0:64, 2 + n, 0:KEYS], SCALE,
                                               sbias[0:64, n * KEYS:(n + 1) * KEYS], ALU.mult, ALU.add))
                dve.tensor_reduce(samp_small[0:64, n:n + 1], s_samp[kind][0:64, :], AX.X, ALU.max, negate=True)\
                    .then_inc(S["samp_max"], 1)
            reciprocals("sparse", 16)
            for qt in range(2):
                s = s_view(s_sparse, qt)
                dve.tensor_tensor(s, s, recip[:, 16 + qt * 8:24 + qt * 8].unsqueeze(2)
                                  .to_broadcast([P, 8, P * (qt + 1)]), ALU.mult).then_inc(S["sparse_attn"], 1)
            dve.wait_ge(S["samp_exp"], 2)
            chain(dve.reciprocal(samp_small[0:64, 4:6], samp_small[0:64, 2:4]))
            chain(dve.scalar_tensor_tensor(samp_small[0:64, 6:7], sbias[0:64, SB_SECOND:SB_SECOND + 1], neglam[0:64, :],
                                           sbias[0:64, SB_FIRST:SB_FIRST + 1], ALU.mult, ALU.add))
            chain(dve.tensor_tensor(samp_small[0:64, 4:5], samp_small[0:64, 4:5], samp_small[0:64, 6:7], ALU.mult))
            for n, kind in enumerate(("diff", "sparse")):
                chain(dve.tensor_scalar(s_samp[kind][0:64, :], s_samp[kind][0:64, :], samp_small[0:64, 4 + n:5 + n],
                                        None, ALU.mult))
                dve.tensor_scalar(new_diag[n][0:64, :], ident[0:64, 0:64], s_samp[kind][0:64, PAST:KEYS], None, ALU.mult)\
                    .then_inc(S["samp_attn"], 1)
            await_unit(dve, "sampT")
            chain.put(dve.tensor_reduce(att[:, 0:96], bank("sampT")[:, 0:192].rearrange("p (n i) -> p n i", i=2),
                                        AX.X, ALU.add))
            chain.settle()
            drain_unit(dve.tensor_copy(att[:, 96:288], bank("sampT")[:, 192:384]), "sampT")
            await_drained(dve, "sampT")
            new_d = att[:, 64:96].rearrange("p (b j) -> p j b", j=4)
            new_s = att[:, 224:288].rearrange("p (b j i) -> p j b i", j=4, i=2)
            part_d = new_part[:, 0:32].rearrange("p (j b) -> p j b", j=4)
            part_s = new_part[:, 32:64].rearrange("p (j b) -> p j b", j=4)
            chain.put(dve.tensor_tensor(part_d, new_d, z[:, VA:VA + 4, TP:T], ALU.mult))
            for i in range(2):
                half = slice(i * HD, (i + 1) * HD)
                chain.put(dve.tensor_tensor(part_s[half], new_s[half, :, :, i], z[half, VS:VS + 4, TP:T], ALU.mult))
            chain.settle()
            await_unit(dve, "samp_o")
            o_d = bank("samp_o")[:, 0:32].rearrange("p (j b) -> p j b", j=4)
            o_s = bank("samp_o")[:, 32:96].rearrange("p (j b i) -> p j b i", j=4, i=2)
            for i in range(2):
                half = slice(i * HD, (i + 1) * HD)
                chain.put(dve.tensor_tensor(o_sparse[half, :, TP:T], o_s[half, :, :, i], part_s[half], ALU.add))
            drain_unit(dve.tensor_tensor(o_diff[:, :, TP:T], o_d, part_d, ALU.add), "samp_o")
            await_drained(dve, "samp_o")
            await_drained(dve, "diff_o1")
            dve.sem_inc(S["out_sample_ready"], 1)
            for u in range(3):
                await_unit(dve, f"rms{u}")
                drain_unit(dve.tensor_scalar(s_diff[:, 4 * T + 352 * u:4 * T + 352 * (u + 1)], bank(f"rms{u}")[:, 0:352],
                                             1.0 / P, EPS, ALU.mult, ALU.add), f"rms{u}")
                await_drained(dve, f"rms{u}")
            dve.reciprocal(s_diff[:, 4 * T:8 * T], s_diff[:, 4 * T:8 * T]).then_inc(S["rms_recip"], 1)
            dve.wait_ge(S["rms_root"], 1)
            o_flat = o_diff.rearrange("p j t -> p (j t)")
            chain(dve.tensor_tensor(o_flat, o_flat, s_diff[:, 4 * T:8 * T], ALU.mult))
            chain(dve.tensor_scalar(o_flat, o_flat, par[:, P_SUBLN:P_SUBLN + 1], 1.0 - LAM_INIT, ALU.mult, ALU.mult))
            dve.sem_inc(S["out_sample_ready"], 1)

            dve.sem_inc(S["up_free"], 2)
            with dve.Fori(0, 2) as i:
                for k in range(4):
                    n = i * 4 + k

                    def row(of, at=n):
                        return of[:, bass.ds(at, 1), :].rearrange("p o t -> p (o t)")

                    dve.wait_ge(S["tiles_done"], UP_AT + n + 1)
                    dve.tensor_tensor(row(merged), psum[:, 2 * (k % 2), 0:T], row(gate), ALU.mult)
                    dve.wait_ge(S["merged"], n + 1)
                    dve.tensor_tensor(up_tmp[k % 2], psum[:, 2 * (k % 2) + 1, 0:T], row(gate, n + DC), ALU.mult)\
                        .then_inc(S["up_free"], 1)
            dve.sem_inc(S["out_free"], 4)
            with dve.Fori(0, 2) as i:
                for k in range(4):
                    n = i * 4 + k
                    dve.wait_ge(S["tiles_done"], OUT_AT + n + 1)
                    dve.scalar_tensor_tensor(pre[:, bass.ds(n, 1), :].rearrange("p o t -> p (o t)"),
                                             xt[:, bass.ds(n * T, T)], ALPHA, psum[:, 4 + k, 0:T], ALU.mult, ALU.add)\
                        .then_inc(S["out_free"], 1)

            def norm(n, dst, g, b):
                dve.wait_ge(S["ln_stat"], 2 * n + 1)
                chain(dve.tensor_scalar(ln_mean, psum[:, 0, 0:T], 1.0 / D, None, ALU.mult))
                dve.tensor_tensor(pre, pre, ln_mean.unsqueeze(1).to_broadcast([P, DC, T]), ALU.subtract)\
                    .then_inc(S["ln_centred"], 1)
                dve.wait_ge(S["ln_stat"], 2 * n + 2)
                chain(dve.tensor_scalar(ln_root, psum[:, 1, 0:T], 1.0 / D, EPS, ALU.mult, ALU.add))
                dve.reciprocal(ln_root, ln_root).then_inc(S["ln_recip"], 1)
                dve.wait_ge(S["ln_root"], n + 1)
                chain(dve.tensor_tensor(pre, pre, ln_root.unsqueeze(1).to_broadcast([P, DC, T]), ALU.mult))
                for k in range(DC):
                    dve.tensor_scalar(dst[:, k, :], pre[:, k, :], par[:, g + k:g + k + 1], par[:, b + k:b + k + 1],
                                      ALU.mult, ALU.add).then_inc(S["ln_done"], 1)

            h = ht[:, :].rearrange("p (c t) -> p c t", c=DC)
            norm(0, h, P_LN1G, P_LN1B)

            dve.sem_inc(S["score_free"], 2)
            for hc in range(HC):
                dve.wait_ge(S["score_filled"], 2 + hc + 1)
                scores = [psum[0:r, 2 + hc % 2, n * P:(n + 1) * P] for n, (_, r) in enumerate(TOKEN_TILES)]
                val = [route_val[0:r, n, hc, :] for n, (_, r) in enumerate(TOKEN_TILES)]
                idx = [route_idx[0:r, n, hc, :] for n, (_, r) in enumerate(TOKEN_TILES)]
                left = [rest128[n][0:r, :] for n, (_, r) in enumerate(TOKEN_TILES)]
                for n in range(3):
                    chain.put(dve.max(val[n][:, 0:8], scores[n]))
                chain.settle()
                for n in range(3):
                    chain.put(dve.match_replace(left[n], val[n][:, 0:8], scores[n], TAKEN))
                for n in range(3):
                    last = dve.max_index(idx[n][:, 0:8], val[n][:, 0:8], scores[n])
                    if n == 2:
                        last.then_inc(S["score_free"], 1)
                chain.settle()
                for n in range(3):
                    chain.put(dve.max(val[n][:, 8:16], left[n]))
                chain.settle()
                for n in range(3):
                    chain.put(dve.max_index(idx[n][:, 8:16], val[n][:, 8:16], left[n]))
            chain.settle()

            dve.tensor_scalar(xt[:, :], ht[:, :], ALPHA, None, ALU.mult).then_inc(S["acc_ready"], 1)
            for n, (_, r) in enumerate(TOKEN_TILES):
                chain(dve.tensor_copy(route_idxf[0:r, n], route_idx[0:r, n]))
                halves = route_val[0:r, n].rearrange("p (h c) k -> p h c k", c=2)
                first = halves[:, :, 0, :].unsqueeze(3).to_broadcast([r, 8, TOP, TOP])
                second = halves[:, :, 1, :].unsqueeze(2).to_broadcast([r, 8, TOP, TOP])
                sums4 = cand[0:r, :].rearrange("p (h i j) -> p h i j", h=8, i=TOP)
                chain(dve.tensor_tensor(sums4, first, second, ALU.add))
                best = top_val[0:r, n, :].rearrange("p (h k) -> p h k", h=8)
                pos = top_pos[0:r, :].rearrange("p (h k) -> p h k", h=8)
                for hp in range(0, 8, 2):
                    pair = [(cand[0:r, (hp + q) * 256:(hp + q + 1) * 256], rest[q][0:r, :], hp + q) for q in range(2)]
                    for rows_c, _, hh in pair:
                        chain.put(dve.max(best[:, hh, 0:8], rows_c))
                    chain.settle()
                    for rows_c, left, hh in pair:
                        chain.put(dve.match_replace(left, best[:, hh, 0:8], rows_c, TAKEN))
                    for rows_c, left, hh in pair:
                        chain.put(dve.max_index(pos[:, hh, 0:8], best[:, hh, 0:8], rows_c))
                    chain.settle()
                    for rows_c, left, hh in pair:
                        chain.put(dve.max(best[:, hh, 8:16], left))
                    chain.settle()
                    for rows_c, left, hh in pair:
                        chain.put(dve.max_index(pos[:, hh, 8:16], best[:, hh, 8:16], left))
                    chain.settle()
                for op, arg, c2, dst in ((ALU.logical_shift_right, 4, 0, first_id), (ALU.bitwise_and, 15, 1, second_id)):
                    chain(dve.tensor_single_scalar(pos_part[0:r, :], top_pos[0:r, :], arg, op))
                    chain(dve.tensor_copy(pos_f[0:r, :], pos_part[0:r, :]))
                    oh = onehot[0:r, :].rearrange("p (n i) -> p n i", i=TOP)
                    chain(dve.tensor_tensor(oh, pos_f[0:r, :].unsqueeze(2).to_broadcast([r, P, TOP]),
                                            iota16[0:r, :].unsqueeze(1).to_broadcast([r, P, TOP]), ALU.is_equal))
                    oh4 = onehot[0:r, :].rearrange("p (h k i) -> p h k i", h=8, k=TOP)
                    ids = route_idxf[0:r, n].rearrange("p (h c) k -> p h c k", c=2)[:, :, c2, :]
                    chain(dve.tensor_tensor(oh4, oh4, ids.unsqueeze(2).to_broadcast([r, 8, TOP, TOP]), ALU.mult))
                    chain(dve.tensor_reduce(dst[0:r, n, :], oh, AX.X, ALU.add))
                chain(dve.tensor_copy(denom[0:r, n, :], best[:, :, 0]))
                chain(dve.tensor_tensor(best, best, denom[0:r, n, :].unsqueeze(2).to_broadcast([r, 8, TOP]), ALU.subtract))
            dve.sem_inc(S["route_ready"], 1)
            for n, (_, r) in enumerate(TOKEN_TILES):
                best = top_val[0:r, n, :].rearrange("p (h k) -> p h k", h=8)
                dve.wait_ge(S["route_exp"], n + 1)
                chain(dve.tensor_reduce(denom[0:r, n, :], best, AX.X, ALU.add))
                chain(dve.reciprocal(denom[0:r, n, :], denom[0:r, n, :]))
                chain(dve.tensor_tensor(best, best, denom[0:r, n, :].unsqueeze(2).to_broadcast([r, 8, TOP]), ALU.mult))
            dve.sem_inc(S["gates_normed"], 1)
            for n, dst in enumerate((slot_first, slot_second, slot_gate)):
                dve.wait_ge(S["route_filled"], n + 1)
                dve.tensor_copy(dst, psum[:, 1 + n, 0:T]).then_inc(S["route_copied"], 1)

            dve.sem_inc(S["g_free"], 2)
            dve.wait_ge(S["route_copied"], 3)
            dve.wait_ge(S["gelu_done"], 4 + NK)
            with dve.Fori(0, T // 8) as i:
                for q in range(2):
                    dve.wait_ge(S["g_filled"], i * 2 + q + 1)
                    for k in range(4):
                        t = i * 8 + q * 4 + k
                        dve.tensor_scalar(p1[:, 4 * q + k, :], iota, slot_first[:, bass.ds(t, 1)], None, ALU.is_equal)
                        last = dve.tensor_scalar(p2[:, 4 * q + k, :], iota, slot_second[:, bass.ds(t, 1)],
                                                 slot_gate[:, bass.ds(t, 1)], ALU.is_equal, ALU.mult)
                    last.then_inc(S["p2_ready"], 1)
                for q in range(2):
                    dve.wait_ge(S["g_filled"], 2 + i * 2 + q + 1)
                    cells = gelu_all[:, :, bass.ds(i * 8 + q * 4, 4)].rearrange("p b t -> p t b")
                    dve.tensor_tensor(cells, psum[:, 4 + q, :].rearrange("p (t b) -> p t b", t=4), cells, ALU.mult)\
                        .then_inc(S["g_free"], 1)

            acc = xt[:, :].rearrange("p (c t) -> p c t", c=DC)
            dve.wait_ge(S["acc_ready"], 1)
            dve.sem_inc(S["acc_added"], DC)
            with dve.Fori(0, NK // 4) as g:
                for k in range(DC):
                    dve.wait_ge(S["acc_added"], g * DC + k + 1)
                    dve.wait_ge(S["v_filled"], g * DC + k + 1)
                    dve.tensor_tensor(acc[:, k, :], psum[:, k, 0:T], acc[:, k, :], ALU.add).then_inc(S["acc_added"], 1)
            dve.wait_ge(S["acc_added"], DC + NK // 4 * DC)
            dve.tensor_copy(pre, acc).then_inc(S["acc_ready"], 1)
            dve.wait_ge(S["acc_ready"], 2)
            norm(1, pre, P_LN2G, P_LN2B)

        @block.tensor
        def _(pe):
            def fill(name):
                n = UNIT[name]
                if n >= ROT:
                    pe.wait_ge(drained[n % ROT], n // ROT)

            def project(slot, loaded, out, moving, chunks=DC, first=0):
                if loaded is not None:
                    pe.wait_ge(w_loaded[slot], loaded)
                for k in range(chunks):
                    at = slot * D + (first + k) * P
                    last = pe.matmul(out, ring[:, at:at + P], moving(k), start=(k == 0), stop=(k == chunks - 1))
                return last

            x = xt[:, :].rearrange("p (c t) -> p c t", c=DC)
            pe.wait_ge(S["x_loaded"], 16)
            banks_free = (S["z_even_free"], S["z_odd_free"])
            with pe.Fori(0, Z_TILES // RING) as i:
                for s in range(RING):
                    pe.wait_ge(banks_free[s % 2], i * 2 + s // 2 + 1)
                    project(s, 16 * i + 16, psum[:, s % 2, 0:T], lambda k: x[:, k, :]).then_inc(S["tiles_done"], 1)
            for t in range(Z_TILES // RING * RING, Z_TILES):
                pe.wait_ge(banks_free[t % 2], t // 2 + 1)
                project(t % RING, 16 * (t // RING) + 16, psum[:, t % 2, 0:T], lambda k: x[:, k, :])\
                    .then_inc(S["tiles_done"], 1)

            pe.wait_ge(S["consts_loaded"], 16)
            pe.wait_ge(S["z_even_free"], 1 + Z_TILES // 2)
            pe.wait_ge(S["z_odd_free"], 1 + Z_TILES // 2)
            pe.wait_ge(S["lam_products"], 1)
            fill("wi")
            b = bank("wi")
            for qt in range(2):
                pe.matmul(b[:, 8 * qt:8 * qt + 8], z[0:8, WI, qt * P:(qt + 1) * P], ident[0:8, 0:8], start=True, stop=True)
            pe.matmul(b[0:64, 16:24], cst[0:8, C_HEADROW:C_HEADROW + 64], z[0:8, WI, TP:T], start=True, stop=True)
            pe.matmul(b[:, 128:130], ones[0:64, :], lam[0:64, 0:2], start=True, stop=True)\
                .then_inc(S["unit_filled"], 1)

            def scores(kind, u, q_tile, keys_of):
                qt, i, j0, n = SCORE_UNITS[u]
                fill(f"{kind}{u}")
                b, keys = bank(f"{kind}{u}"), P * (qt + 1)
                half = slice(i * HD, (i + 1) * HD)
                for j in range(n):
                    m = 2 * (j0 + j) + i
                    last = pe.matmul(b[:, j * keys:(j + 1) * keys],
                                     z[half, q_tile + m // 2, qt * P:(qt + 1) * P],
                                     z[half, keys_of(m), 0:keys], start=True, stop=True)
                last.then_inc(S["unit_filled"], 1)

            for u in range(6):
                scores("idx", u, QI, lambda m: KI)
            for kind, tile in (("diff", VA), ("sparse", VS)):
                for kt in range(2):
                    fill(f"v_{kind}{kt}")
                    for j in range(4):
                        last = pe.transpose(bank(f"v_{kind}{kt}")[:, j * P:(j + 1) * P],
                                            z[:, tile + j, kt * P:(kt + 1) * P], ident)
                    last.then_inc(S["unit_filled"], 1)
            for u in range(6):
                scores("diff", u, QA, lambda m: KA + m // 2)

            pe.wait_ge(S["qpad_ready"], 6)
            for b in range(TS):
                pe.wait_ge(S["k_ready"], b + 1)
                buf = kbuf[b % 2]
                for n, kind in enumerate(("diff", "sparse")):
                    for j in range(4):
                        last = pe.matmul(psum[0:64, 2 + n, 0:KEYS], qpad[kind][:, j, b, :], buf[kind][:, j, :],
                                         start=(b == 0 and j == 0), stop=(b == TS - 1 and j == 3 and n == 0))
                last = pe.matmul(psum[0:64, 4, 0:KEYS], qpad["idx"][:, b, :], buf["idx"],
                                 start=(b == 0), stop=(b == TS - 1))
                last.then_inc(S["k_used"] if b < TS - 1 else S["sample_scored"], 1)
            pe.wait_ge(S["relu_sample"], 1)
            await_drained(pe, "wi")
            fill("isum")
            pe.matmul(bank("isum")[0:TS, 0:KEYS], wsel[0:64, :], relu_samp[0:64, :], start=True, stop=True)\
                .then_inc(S["unit_filled"], 1)

            def ring_use(t):
                return 16 * (t // RING + 1)

            with pe.Fori(0, GATE_TILES // 4) as i:
                for k in range(4):
                    t = Z_TILES + k
                    pe.wait_ge(banks_free[k % 2], Z_TILES // 2 + i * 2 + k // 2 + 1)
                    project(t % RING, i * 16 + ring_use(t), psum[:, k % 2, 0:T], lambda k: x[:, k, :])\
                        .then_inc(S["tiles_done"], 1)

            pe.wait_ge(S["sel_sample"], 1)
            pe.matmul(psum[0:64, 3, 0:KEYS], cst[0:TS, C_EXPAND:C_EXPAND + 64], iscore[2][0:TS, :],
                      start=False, stop=True).then_inc(S["sample_scored"], 1)
            for u in range(6):
                scores("sparse", u, QS, lambda m: KS + m // 2)

            def transposes(kind, buf, heads, head_of):
                for u in range(heads * 3 // 4):
                    fill(f"{kind}T{u}")
                    for q in range(4):
                        h, (qt, kt) = (4 * u + q) // 3, PT_TILES[(4 * u + q) % 3]
                        last = pe.transpose(bank(f"{kind}T{u}")[:, q * P:(q + 1) * P],
                                            s_view(buf, qt)[:, head_of(h), kt * P:(kt + 1) * P], ident)
                    last.then_inc(S["unit_filled"], 1)

            def outputs(kind, heads, width):
                for u in range(2):
                    fill(f"{kind}_o{u}")
                    n = heads // 2
                    for h in range(u * n, (u + 1) * n):
                        row = (h * width) % P
                        col = ((h * width) // P % 2) * TP
                        out = bank(f"{kind}_o{u}")[row:row + width, :]
                        v = v_tok[kind][:, :, h * width:(h + 1) * width]
                        pe.matmul(out[:, col:col + TP], v[:, 0, :],
                                  pt[:, 3 * h:3 * h + 2, :].rearrange("p n q -> p (n q)"), start=True, stop=False)
                        last = pe.matmul(out[:, col + P:col + TP], v[:, 1, :], pt[:, 3 * h + 2, :],
                                         start=False, stop=True)
                    last.then_inc(S["unit_filled"], 1)

            pe.wait_ge(S["diff_attn"], 2)
            transposes("diff", s_diff, 4, lambda h: 2 * h)
            await_drained(pe, "diffT2")
            outputs("diff", 4, P)
            pe.wait_ge(S["sparse_attn"], 2)
            transposes("sparse", s_sparse, 8, lambda h: h)
            await_drained(pe, "sparseT5")
            outputs("sparse", 8, HD)

            pe.wait_ge(S["samp_attn"], 2)
            fill("sampT")
            b = bank("sampT")
            for n, kind in enumerate(("diff", "sparse")):
                for g in range(PAGES):
                    pe.transpose(b[:, 192 * n + 64 * g:192 * n + 64 * (g + 1)],
                                 s_samp[kind][0:64, g * PAGE:(g + 1) * PAGE], ident[0:64, 0:64])
                last = pe.matmul(b[:, 192 * n + 128:192 * n + 192], ones[0:64, :], new_diag[n][0:64, :],
                                 start=True, stop=True)
            last.then_inc(S["unit_filled"], 1)
            await_drained(pe, "sampT")
            fill("samp_o")
            o = bank("samp_o")
            for b in range(TS):
                pe.wait_ge(vc_loaded[b % 2], 64 * (b // 2 + 1))
                buf = vbuf[b % 2]
                for j in range(4):
                    for g in range(PAGES):
                        pe.matmul(o[:, j * 8 + b:j * 8 + b + 1], buf["diff"][:, g, j * P:(j + 1) * P],
                                  att[:, g * 32 + b * 4 + j:g * 32 + b * 4 + j + 1], start=(g == 0), stop=(g == 1))
                    for g in range(PAGES):
                        at = 96 + g * 64 + b * 8 + 2 * j
                        last = pe.matmul(o[:, 32 + j * 16 + b * 2:34 + j * 16 + b * 2], buf["sparse"][:, g, j * P:(j + 1) * P],
                                         att[:, at:at + 2], start=(g == 0), stop=(g == 1))
                last.then_inc(S["v_used"] if b < TS - 1 else S["unit_filled"], 1)

            pe.wait_ge(S["rms_square"], 1)
            for u in range(3):
                fill(f"rms{u}")
                pe.matmul(bank(f"rms{u}")[:, 0:352], ones, s_diff[:, 352 * u:352 * (u + 1)], start=True, stop=True)\
                    .then_inc(S["unit_filled"], 1)

            pe.wait_ge(S["out_sample_ready"], 2)
            with pe.Fori(0, DC // 4) as i:
                for k in range(4):
                    t = UP_AT + k
                    pe.wait_ge(S["up_free"], i * 4 + k + 1)
                    project(t % RING, i * 16 + ring_use(t), psum[:, 2 * (k % 2), 0:T], lambda c: o_diff[:, c, :], chunks=4)
                    project(t % RING, None, psum[:, 2 * (k % 2) + 1, 0:T], lambda c: o_sparse[:, c, :], chunks=4, first=4)\
                        .then_inc(S["tiles_done"], 1)
            pe.wait_ge(S["merged"], 2 + DC)
            with pe.Fori(0, DC // 4) as i:
                for k in range(4):
                    t = OUT_AT + k
                    pe.wait_ge(S["out_free"], i * 4 + k + 1)
                    project(t % RING, i * 16 + ring_use(t), psum[:, 4 + k, 0:T], lambda c: merged[:, c, :])\
                        .then_inc(S["tiles_done"], 1)

            def norm(n):
                for k in range(DC):
                    last = pe.matmul(psum[:, 0, 0:T], ones, pre[:, k, :], start=(k == 0), stop=(k == DC - 1))
                last.then_inc(S["ln_stat"], 1)
                pe.wait_ge(S["ln_square"], n + 1)
                for k in range(DC):
                    last = pe.matmul(psum[:, 1, 0:T], ones, squares[:, k * T:(k + 1) * T], start=(k == 0), stop=(k == DC - 1))
                last.then_inc(S["ln_stat"], 1)

            pe.wait_ge(S["out_free"], 4 + DC)
            norm(0)

            h = ht[:, :].rearrange("p (c t) -> p c t", c=DC)
            pe.wait_ge(S["ln_done"], DC)
            pe.wait_ge(S["subkeys_loaded"], 16)
            pe.sem_inc(S["score_filled"], 2)
            with pe.Fori(0, HC // 4) as i:
                def sub_scores(k):
                    pe.wait_ge(S["q_evac"], 2 + i * 4 + k + 1)
                    pe.wait_ge(S["score_free"], i * 4 + k + 1)
                    for n, (t0, r) in enumerate(TOKEN_TILES):
                        last = pe.matmul(psum[0:r, 2 + k % 2, n * P:(n + 1) * P], q_sb[k % 2][:, t0:t0 + r],
                                         subk[:, bass.ds(i * 4 + k, 1), :].rearrange("p o n -> p (o n)"),
                                         start=True, stop=True)
                    last.then_inc(S["score_filled"], 1)

                for k in range(4):
                    t = WQ_AT + k
                    pe.wait_ge(S["q_evac"], i * 4 + k + 1)
                    project(t % RING, i * 16 + ring_use(t), psum[:, k % 2, 0:T], lambda c: h[:, c, :])\
                        .then_inc(S["tiles_done"], 1)
                    if k:
                        sub_scores(k - 1)
                sub_scores(3)

            with pe.Fori(0, NK // RING) as i:
                for k in range(RING):
                    s = (U_SLOT + k) % RING
                    pe.wait_ge(S["gelu_done"], i * RING + k + 1)
                    project(s, i * 16 + 16 * uses[s] + 16, psum[:, 4 + k, 0:T], lambda c: h[:, c, :])\
                        .then_inc(S["u_done"], 1)

            for n, src in enumerate((first_id, second_id, top_val)):
                pe.wait_ge(S["route_ready"], 1)
                if n == 2:
                    pe.wait_ge(S["gates_normed"], 1)
                for g, (t0, r) in enumerate(TOKEN_TILES):
                    last = pe.transpose(psum[:, 1 + n, t0:t0 + r], src[0:r, g, :], ident[0:r, 0:r])
                last.then_inc(S["route_filled"], 1)
            pe.wait_ge(S["gelu_done"], 4 + NK)
            pe.sem_inc(S["g_filled"], 2)
            with pe.Fori(0, T // 8) as i:
                for q in range(2):
                    pe.wait_ge(S["p2_ready"], i * 2 + q + 1)
                    pe.wait_ge(S["g_free"], i * 2 + q + 1)
                    for k in range(4):
                        last = pe.matmul(psum[:, 4 + q, k * P:(k + 1) * P], p1[:, 4 * q + k, :], p2[:, 4 * q + k, :],
                                         start=True, stop=True)
                    last.then_inc(S["g_filled"], 1)
            pe.wait_ge(S["g_free"], 2 + T // 4)
            with pe.Fori(0, NK // 8) as i:
                for q in range(2):
                    for k in range(DC):
                        if k == 0:
                            pe.wait_ge(v_loaded[q], i * 16 + 16)
                        pe.wait_ge(S["acc_added"], i * 16 + q * 8 + k + 1)
                        for e in range(4):
                            last = pe.matmul(psum[:, k, 0:T], vring[q][:, e, k * P:(k + 1) * P],
                                             gelu_all[:, bass.ds(i * 8 + q * 4 + e, 1), :].rearrange("p o t -> p (o t)"),
                                             start=(e == 0), stop=(e == 3))
                        last.then_inc(S["v_filled"], 1)
            pe.wait_ge(S["acc_ready"], 2)
            norm(1)


def shape_constants():
    f = np.float32
    consts = np.zeros((P, CONSTS), f)
    consts[:, C_IDENT:C_IDENT + P] = np.eye(P, dtype=f)
    consts[:, C_ONES:C_ONES + P] = 1
    consts[:, C_IOTA:C_IOTA + P] = np.arange(P, dtype=f)
    consts[:, C_IOTA16:C_IOTA16 + TOP] = np.arange(TOP, dtype=f)
    for b in range(TS):
        for m in range(8):
            consts[b, C_EXPAND + b * 8 + m] = 1
            consts[m, C_HEADROW + b * 8 + m] = 1
            consts[b * 8 + m, C_DIAG + b] = 1
    slopes = lambda n: [2.0 ** (-8.0 * (i + 1) / n) for i in range(n)]
    dist = (128 + np.arange(P)[:, None] - np.arange(256)[None, :]).astype(f)
    alibi = np.zeros((P, BIASES, 256), f)
    for n, s in enumerate(slopes(4) + slopes(8) + [0.0]):
        alibi[:, n] = np.where(dist >= 0, -f(s) * dist, f(NEG))
    gap = (PAST - np.arange(KEYS)).astype(f)
    sample = np.zeros((64, SBIAS), f)
    for row in range(64):
        m = row % 8
        sample[row, 0:KEYS] = -f(slopes(4)[m // 2]) * gap
        sample[row, KEYS:2 * KEYS] = -f(slopes(8)[m]) * gap
        sample[row, SB_FIRST + m % 2] = 1
    return consts, alibi.reshape(P, -1), sample


def kernel(x_prompt, x_sample, cache_da_k, cache_da_v, cache_sa_k, cache_sa_v, cache_idx_k, page_table,
           w_in, lambda_q1, lambda_k1, lambda_q2, lambda_k2, da_subln_g, w_a_up, w_b_up, w_out,
           ln1_g, ln1_b, peer_wq, peer_sub_keys, peer_u, peer_v, ln2_g, ln2_b):
    import concourse.bacc as bacc
    from concourse.bass_utils import run_bass_kernel_spmd

    arr = lambda v: np.asarray(v)
    x = np.concatenate([arr(x_prompt).reshape(TP, D), arr(x_sample).reshape(TS, D)])
    x_t = x.T.reshape(DC, P, T).transpose(1, 0, 2)

    wi = arr(w_in)[0]
    at = np.cumsum([0, 512, 512, 512, 512, 512, 512, 512, 64, 8, 1024, 1024]).tolist()
    qa, ka, va, qs, ks, vs, qi, ki, wx, ga, gb = [wi[:, at[n]:at[n + 1]] for n in range(11)]
    pad = np.zeros((D, P - 8), wi.dtype)
    cols = np.concatenate([qa, qs, qi, ka, ks, va, vs, ki, ki, wx, pad, ga, gb], axis=1)
    tiled = lambda m: m.reshape(DC, P, -1, P).transpose(2, 1, 0, 3).reshape(-1, P, D)
    up = np.concatenate([arr(w_a_up)[0], arr(w_b_up)[0]], axis=0)
    weights = np.concatenate([tiled(cols), tiled(up), tiled(arr(w_out)[0]), tiled(arr(peer_wq)[0])])

    keys = lambda c: arr(c)[0].reshape(-1, PAGE, 4, P).transpose(0, 3, 2, 1)
    idx_t = arr(cache_idx_k)[0].transpose(0, 2, 1)
    rows = lambda c: arr(c)[0].reshape(-1, PAGE, 512)
    vec = lambda v: arr(v)[0].reshape(DC, P).T
    lam = np.zeros((P, 4), wi.dtype)
    for n, v in enumerate((lambda_q1, lambda_q2, lambda_k1, lambda_k2)):
        lam[0:HD, n] = arr(v)[0]
    params = np.concatenate([vec(ln1_g), vec(ln1_b), vec(ln2_g), vec(ln2_b), arr(da_subln_g)[0][:, None], lam], axis=1)
    consts, alibi, sample = shape_constants()
    ins = {
        "x_t": x_t, "weights": weights,
        "experts_u": arr(peer_u)[0].reshape(P, P, DC, P).transpose(1, 3, 2, 0).reshape(P, P, D),
        "experts_v": arr(peer_v)[0].reshape(P, P, D).transpose(1, 0, 2),
        "k_diff": keys(cache_da_k), "k_sparse": keys(cache_sa_k),
        "k_idx": np.concatenate([idx_t, idx_t], axis=1),
        "v_diff": rows(cache_da_v), "v_sparse": rows(cache_sa_v),
        "page_table": arr(page_table).astype(np.int32).reshape(1, -1),
        "sub_keys": arr(peer_sub_keys)[0].reshape(HC, NK, P).transpose(2, 0, 1),
        "params": params, "consts": consts, "alibi": alibi, "sample_bias": sample,
    }
    outs = {"kv_out": (P, KV_TILES, T), "y_out": (P, DC, T)}
    nc = bacc.Bacc("TRN2", target_bir_lowering=False, num_devices=1)
    arrays, args = {}, {}
    for name, v in ins.items():
        v = np.ascontiguousarray(v)
        arrays[f"{name}_dram"] = v
        args[name] = nc.dram_tensor(f"{name}_dram", v.shape, mybir.dt.from_np(v.dtype), kind="ExternalInput").ap()
    for name, shape in outs.items():
        args[name] = nc.dram_tensor(f"{name}_dram", shape, F32, kind="ExternalOutput").ap()
    build_program(nc, **args)
    r = run_bass_kernel_spmd(nc, [arrays], core_ids=[0]).results[0]
    kv, y = np.asarray(r["kv_out_dram"]), np.asarray(r["y_out_dram"])
    y = y.transpose(2, 1, 0).reshape(T, D)
    kv = kv.transpose(2, 1, 0)
    out = [y[:TP].reshape(1, TP, D), y[TP:].reshape(TS, 1, D)]
    for lo, hi, (bb, ss) in ((0, TP, (1, TP)), (TP, T, (TS, 1))):
        part = lambda t0, width: kv[lo:hi, t0 - KA:t0 - KA + 4].reshape(hi - lo, -1)[:, :width]
        out += [part(KA, 512).reshape(1, bb, ss, 4, 2, 64), part(VA, 512).reshape(1, bb, ss, 4, 128),
                part(KS, 512).reshape(1, bb, ss, 8, 64), part(VS, 512).reshape(1, bb, ss, 8, 64),
                kv[lo:hi, KI - KA, 0:HD].reshape(1, bb, ss, HD)]
    return tuple(np.ascontiguousarray(o) for o in out)
```

```python
import math
from contextlib import ExitStack

import numpy as np

import concourse.bass as bass
import concourse.mybir as mybir

F32 = mybir.dt.float32
F32R = mybir.dt.float32r
U32 = mybir.dt.uint32
I32 = mybir.dt.int32
ALU = mybir.AluOpType
ACT = mybir.ActivationFunctionType
AX = mybir.AxisListType

P = 128
D = 1024
DC = D // P
TP, TS = 256, 8
T = TP + TS
PAST = 256
PAGE = 128
PAGES = PAST // PAGE
KEYS = PAST + 1
HD = 64
SUBHEADS = 8
NSEL = 64
SCALE = HD ** -0.5
ALPHA = 2.0 ** 0.25
LAM_INIT = 0.8 - 0.6 * math.exp(0.0)
EPS = 1e-5
NEG = -1e30
TAKEN = -3e38
HC = 16
NK = 128
TOP = 16
TOKEN_TILES = [(0, P), (P, P), (TP, TS)]

QA, QS, QI, KA, KS, VA, VS, KI, WI, GA, GB = 0, 4, 8, 12, 16, 20, 24, 28, 29, 30, 38
Z_TILES, GATE_TILES = 30, 16
EARLY_GATES = 12
UP_AT = Z_TILES + GATE_TILES
OUT_AT = UP_AT + DC
WQ_AT = OUT_AT + DC
TILES = WQ_AT + HC
RING = 4
KV_TILES = KI + 1 - KA

C_IDENT, C_ONES, C_IOTA, C_IOTA16 = 0, P, 2 * P, 3 * P
C_EXPAND = C_IOTA16 + TOP
C_HEADROW = C_EXPAND + 64
C_DIAG = C_HEADROW + 64
C_PAIR = C_DIAG + TS
C_HEAD = C_PAIR + 4
CONSTS = C_HEAD + 8
B_SPARSE, B_CAUSAL = 4, 12
BIASES = 13
ARENA_FREE = P * T - 4 * D
ROUTED = 96
SMALL = 1736
SB_FIRST, SB_SECOND, SBIAS = 2 * KEYS, 2 * KEYS + 1, 2 * KEYS + 2
P_LN1G, P_LN1B, P_LN2G, P_LN2B, P_SUBLN, P_LAM, PARAMS = 0, 8, 16, 24, 32, 33, 37

SCORE_UNITS = [(0, 0, 0, 4), (0, 1, 0, 4), (1, 0, 0, 2), (1, 0, 2, 2), (1, 1, 0, 2), (1, 1, 2, 2)]
PT_TILES = [(0, 0), (1, 0), (1, 1)]

UNIT_ORDER = (["wi"] + [f"idx{u}" for u in range(6)] + ["v_diff0", "v_diff1", "v_sparse0", "v_sparse1"]
              + [f"diff{u}" for u in range(6)] + ["isum"] + [f"sparse{u}" for u in range(6)]
              + [f"diffT{u}" for u in range(3)] + ["diff_o0", "diff_o1"]
              + [f"sparseT{u}" for u in range(6)] + ["sparse_o0", "sparse_o1"]
              + ["sampT", "rms0", "rms1", "samp_diff", "samp_sparse", "samp_o", "rms2"])
UNIT = {name: n for n, name in enumerate(UNIT_ORDER)}
ROT, ROT_AT = 3, 5
RMS = 4 * T


def build_program(nc, x_t, weights, experts_u, experts_v, k_diff, k_sparse, k_idx, v_diff, v_sparse,
                  page_table, sub_keys, params, consts, alibi, sample_bias, kv_out, y_out):
    with ExitStack() as ctx:
        map_at = {"next": 0}
        base = -(-nc.sbuf_base // 32) * 32

        def region(name, words, dt=F32, parts=P):
            map_at[name] = map_at["next"]
            map_at["next"] += -(-words // 8) * 8
            return nc.alloc_sbuf_tensor_at(name, [parts, words], dt, offset=base + 4 * map_at[name])

        def rounded(name, over, at, words):
            return nc.alloc_sbuf_tensor_at(name, [P, words], F32R, offset=base + 4 * (map_at[over] + at))

        names = """consts_loaded params_loaded alibi_loaded table_loaded subkeys_loaded
            x_hi_made x_lo_made z_hi_made z_lo_made tiles_done z_even_free z_odd_free kv_stored y_stored
            unit_filled qpad_zero qpad_ready wi_ready lam_products lam_ready pool_chain dve_chain act_chain
            relu_done idx_sum relu_sample isum_weight isum_copied sel_prompt sel_sample sample_mask_used
            bias_masked k_ready k_used sample_scored gates_done
            diff_max diff_exp diff_attn sparse_max sparse_exp sparse_attn
            samp_max samp_exp samp_attn pad_zero pad_filled out_sample_ready
            rms_square rms_recip rms_root up_b_filled up_b_free up_a_free merged out_free
            ln_stat ln_centred ln_square ln_recip ln_root ln_scaled ln_even ln_odd
            q_evac score_filled score_free wq_hi_made wq_lo_made h_hi_made h_lo_made
            u_hi_made u_hi_used u_lo_made u_done gelu_done route_ready route_exp gates_normed
            route_filled route_copied tok_ready rows_bare rows_ready rows_weighted g_filled g_free g_applied h_restored
            v_hi_made v_hi_used v_lo_made cells_hi_made cells_split v_done v_filled acc_ready""".split()
        S = {n: ctx.enter_context(nc.semaphore(n)) for n in names}
        x_loaded = [ctx.enter_context(nc.semaphore(f"x_loaded{n}")) for n in range(2)]
        w_loaded = [ctx.enter_context(nc.semaphore(f"w_loaded{s}")) for s in range(RING)]
        k_loaded = [ctx.enter_context(nc.semaphore(f"k_loaded{s}")) for s in range(2)]
        vc_loaded = [ctx.enter_context(nc.semaphore(f"vc_loaded{s}")) for s in range(TS)]
        drained = [ctx.enter_context(nc.semaphore(f"drained{s}")) for s in range(ROT)]

        ring = region("ring", RING * D)
        xt = region("xt", DC * T)
        ht = region("ht", DC * T)
        cst = region("cst", CONSTS)
        par = region("par", PARAMS)
        table = region("table", PAGES * TS, I32, 1)
        sbias = region("sbias", SBIAS)
        arena = region("arena", P * T)
        work = region("work", 8192)
        small = region("small", SMALL)

        x_hi = rounded("x_hi", "ht", 0, DC * T)
        x_lo = rounded("x_lo", "work", 0, DC * T)
        z_hi = rounded("z_hi", "work", 2112, 2 * D)
        z_lo = rounded("z_lo", "work", 4160, 2 * D)
        wq_hi = rounded("wq_hi", "arena", ARENA_FREE, 2 * D)
        wq_lo = rounded("wq_lo", "arena", ARENA_FREE + 2 * D, 2 * D)
        h_hi = rounded("h_hi", "ht", 0, DC * T)
        h_lo = rounded("h_lo", "work", 0, DC * T)
        w_hi = rounded("w_hi", "xt", 0, 2 * D)
        w_lo = rounded("w_lo", "work", 3648, 2 * D)
        cells_hi = rounded("cells_hi", "work", 6144, 2 * T)
        cells_lo = rounded("cells_lo", "work", 6144 + 2 * T, 2 * T)

        class Carve:
            def __init__(self, of):
                self.of, self.at = of, 0

            def __call__(self, words):
                self.at += words
                return self.of[:, self.at - words:self.at]

        a = Carve(arena)
        z = a(Z_TILES * T).rearrange("p (n t) -> p n t", t=T)
        gate = a(GATE_TILES * T).rearrange("p (n t) -> p n t", t=T)
        qpad_flat = a(2 * 2048 + 512)
        qpad = {"diff": qpad_flat[:, 0:2048].rearrange("p (j b n) -> p j b n", j=4, b=TS),
                "sparse": qpad_flat[:, 2048:4096].rearrange("p (j b n) -> p j b n", j=4, b=TS),
                "idx": qpad_flat[:, 4096:4608].rearrange("p (b n) -> p b n", b=TS)}
        kspace_at = a.at
        kbuf = [{"diff": a(4 * KEYS).rearrange("p (j k) -> p j k", j=4),
                 "sparse": a(4 * KEYS).rearrange("p (j k) -> p j k", j=4),
                 "idx": a(KEYS)} for _ in range(2)]
        vspace = [a(2 * PAGES * 512) for _ in range(2)]
        bias = a(BIASES * 256).rearrange("p (n k) -> p n k", n=BIASES)
        s_diff = a(8 * 384)
        kspace = arena[:, kspace_at:kspace_at + 2 * (8 * KEYS + KEYS)]
        bias_words = bias.rearrange("p n k -> p (n k)")
        qs_words = z[:, QS:QS + 4, :].rearrange("p n t -> p (n t)")
        halves = [(v[:, 0:1024], v[:, 1024:2048]) for v in
                  vspace + [qpad_flat[:, 0:2048], qpad_flat[:, 2048:4096], kspace[:, 0:2048], kspace[:, 2048:4096],
                            bias_words[:, 0:2048]]] + [(qs_words[:, 0:1024], bias_words[:, 2048:3072])]
        vbuf = [{"diff": d.rearrange("p (g e) -> p g e", g=PAGES), "sparse": e.rearrange("p (g e) -> p g e", g=PAGES)}
                for d, e in halves]
        gelu_all = arena[:, :].rearrange("p (b t) -> p b t", t=T)
        o_diff, o_sparse = z[:, QI:QI + 4, :], z[:, QA:QA + 4, :]
        merged = z[:, KA:KA + DC, :]

        w = Carve(work)
        s_sparse = w(8 * 384)
        pt = w(8 * 3 * P).rearrange("p (n q) -> p n q", q=P)
        samp_pad = s_sparse[:, 0:2048].rearrange("p (n g c) -> p n g c", n=2, g=PAGES)
        samp_rows = s_sparse[:, 2048:3072].rearrange("p (n e) -> p n e", n=2)
        v_tok = {k: w(2 * 512).rearrange("p (g e) -> p g e", g=2) for k in ("diff", "sparse")}
        pre = work[:, 0:DC * T].rearrange("p (c t) -> p c t", c=DC)
        squares = work[:, 8 * 384:8 * 384 + DC * T].rearrange("p (c t) -> p c t", c=DC)
        y_t = pre
        subk = work[:, 6144:8192].rearrange("p (n k) -> p n k", n=HC)
        route_val = work[:, 2112:2880].rearrange("p (g n k) -> p g n k", g=3, n=HC)
        route_idx = work[:, 2880:3648].bitcast(U32).rearrange("p (g n k) -> p g n k", g=3, n=HC)
        route_idxf = work[:, 2880:3648].rearrange("p (g n k) -> p g n k", g=3, n=HC)
        cand = onehot = work[:, 6144:8192]
        rest = [sbias[:, 256 * n:256 * (n + 1)] for n in range(2)]
        p1 = work[:, 6144:7168].rearrange("p (s k) -> p s k", s=8)
        p2 = work[:, 7168:8192].rearrange("p (s k) -> p s k", s=8)

        c = Carve(small)
        mx = c(32)
        sums = c(32)
        recip = c(32)
        lam = c(4)
        neglam = c(1)
        head_w = c(2 * 8 + 8)
        wsel = c(8)
        samp_small = c(8)
        top8 = c(3 * 8)
        phase = c.at
        iscore = [c(P), c(256), c(KEYS)]
        s_samp = {"diff": c(KEYS), "sparse": c(KEYS)}
        relu_samp = s_samp["diff"]
        new_diag = [iscore[1][:, 0:64], iscore[1][:, 64:128]]
        att = c(96)
        new_part = c(64)
        assert c.at <= SMALL, c.at
        c.at = phase
        ln_mean, ln_root = c(T), c(T)
        c.at = phase
        up_tmp = [c(T), c(T)]
        c.at = phase
        q_sb = [c(T), c(T)]
        rest128 = [c(P) for _ in range(3)]
        c.at = phase
        gtmp = c(8 * P).rearrange("p (q n) -> p q n", q=2)
        c.at = phase
        top_val = c(3 * P).rearrange("p (g n) -> p g n", g=3)
        top_pos = c(P).bitcast(U32)
        pos_part = c(P).bitcast(U32)
        pos_f = c(P)
        first_id = c(3 * P).rearrange("p (g n) -> p g n", g=3)
        second_id = c(3 * P).rearrange("p (g n) -> p g n", g=3)
        denom = c(24).rearrange("p (g n) -> p g n", g=3)
        assert c.at <= SMALL, c.at
        slots = work[:, 2112:2112 + 3 * T].rearrange("p (n t) -> p n t", n=3)
        tok = work[:, 2112 + 3 * T:2112 + 3 * T + 48].rearrange("p (h n t) -> p h n t", h=2, n=3)

        h = xt[:, :].rearrange("p (c t) -> p c t", c=DC)
        acc = ring[:, 0:DC * T].rearrange("p (c t) -> p c t", c=DC)
        ident = cst[:, C_IDENT:C_IDENT + P]
        ones = cst[:, C_ONES:C_ONES + P]
        iota = cst[:, C_IOTA:C_IOTA + P]
        iota16 = cst[:, C_IOTA16:C_IOTA16 + TOP]

        psum = ctx.enter_context(nc.psum_tensor("psum", [P, 8, 512], F32))

        def bank(name):
            return psum[:, ROT_AT + UNIT[name] % ROT, :]

        def s_view(buf, qt):
            return (buf[:, 0:1024] if qt == 0 else buf[:, 1024:3072]).rearrange("p (m k) -> p m k", m=8)

        def of_unit(heads, unit):
            _, i, j0, n = unit
            return heads.rearrange("p (j i) k -> p i j k", i=2)[:, i, j0:j0 + n, :]

        def await_unit(eng, name):
            eng.wait_ge(S["unit_filled"], UNIT[name] + 1)

        def drain_unit(ins, name):
            ins.then_inc(drained[UNIT[name] % ROT], 1)

        def await_drained(eng, name):
            eng.wait_ge(drained[UNIT[name] % ROT], UNIT[name] // ROT + 1)

        class Chain:
            def __init__(self, eng, sem):
                self.eng, self.sem, self.n = eng, sem, 0

            def put(self, ins):
                self.n += 1
                ins.then_inc(self.sem, 1)

            def settle(self):
                self.eng.wait_ge(self.sem, self.n)

            def __call__(self, ins):
                self.put(ins)
                self.settle()

        uses = [len(range(s, TILES, RING)) for s in range(RING)]
        U_SLOT = TILES % RING

        def expert_tile(i, k):
            s = (U_SLOT + k) % RING
            return ring[:, s * D:(s + 1) * D], w_loaded[s], 16 * (uses[s] + k // RING) + 16 + i * 16

        def halves_of(buf, k, n):
            return buf[:, (k % 2) * n:(k % 2 + 1) * n]

        def part(buf, k, n):
            return buf[:, k * n:(k + 1) * n]

        def ring_tile(t):
            return part(ring, t % RING, D), w_loaded[t % RING], 16 * (t // RING + 1)

        block = ctx.enter_context(nc.Block())

        @block.sync
        def _(sp):
            sp.dma_start(ring[:, 0:D], weights[0]).then_inc(w_loaded[0], 16)
            for n in range(2):
                sp.dma_start(xt[:, n * 4 * T:(n + 1) * 4 * T], x_t[:, n * 4:(n + 1) * 4, :]).then_inc(x_loaded[n], 16)
            for t in range(1, RING):
                sp.dma_start(ring[:, t * D:(t + 1) * D], weights[t]).then_inc(w_loaded[t], 16)

            def load_tile(i, s, t):
                sp.wait_ge(S["tiles_done"], t - RING + 1)
                sp.dma_start(ring[:, s * D:(s + 1) * D], weights[t]).then_inc(w_loaded[s], 16)

            with sp.Fori(1, TILES // RING) as i:
                for s in range(RING):
                    load_tile(i, s, i * RING + s)
            for t in range(TILES // RING * RING, TILES):
                load_tile(0, t % RING, t)

            for b in range(RING):
                s = (U_SLOT + b) % RING
                sp.wait_ge(S["tiles_done"], TILES - RING + b + 1)
                sp.dma_start(ring[:, s * D:(s + 1) * D], experts_u[b]).then_inc(w_loaded[s], 16)
            with sp.Fori(1, NK // RING) as i:
                for k in range(RING):
                    s = (U_SLOT + k) % RING
                    sp.wait_ge(S["u_lo_made"], 2 + i * RING + k - RING + 1)
                    sp.dma_start(ring[:, s * D:(s + 1) * D], experts_u[i * RING + k]).then_inc(w_loaded[s], 16)
            for b in range(RING):
                s = (U_SLOT + b) % RING
                sp.wait_ge(S["u_lo_made"], 2 + NK - RING + b + 1)
                sp.dma_start(ring[:, s * D:(s + 1) * D], experts_v[b]).then_inc(w_loaded[s], 16)
            with sp.Fori(1, NK // RING) as i:
                for k in range(RING):
                    s = (U_SLOT + k) % RING
                    sp.wait_ge(S["v_lo_made"], 2 + i * RING + k - RING + 1)
                    sp.dma_start(ring[:, s * D:(s + 1) * D], experts_v[i * RING + k]).then_inc(w_loaded[s], 16)
            for k in range(0, DC, 2):
                sp.wait_ge(S["ln_even"], DC // 2 + k // 2 + 1)
                sp.wait_ge(S["ln_odd"], DC // 2 + k // 2 + 1)
                sp.dma_start(y_out[:, k:k + 2, :], y_t[:, k:k + 2, :]).then_inc(S["y_stored"], 16)
            sp.wait_ge(S["y_stored"], 16 * DC // 2)
            sp.wait_ge(S["kv_stored"], 16)

        @block.gpsimd
        def _(pool):
            chain = Chain(pool, S["pool_chain"])
            pool.dma_start(table[:, :], page_table).then_inc(S["table_loaded"], 16)
            pool.memset(qpad_flat, 0.0).then_inc(S["qpad_zero"], 1)
            pool.wait_ge(S["table_loaded"], 16)

            def page_of(b, g):
                return pool.value_load(table[0:1, b * PAGES + g:b * PAGES + g + 1], min_val=0,
                                       max_val=k_idx.shape[0] - 1)

            def load_keys(b):
                buf, sem = kbuf[b % 2], k_loaded[b % 2]
                for g in range(PAGES):
                    page = page_of(b, g)
                    cols = slice(g * PAGE, (g + 1) * PAGE)
                    pool.dma_start(buf["diff"][:, :, cols], k_diff[bass.ds(page, 1)].rearrange("o p j k -> p (o j) k"))\
                        .then_inc(sem, 16)
                    pool.dma_start(buf["sparse"][:, :, cols], k_sparse[bass.ds(page, 1)].rearrange("o p j k -> p (o j) k"))\
                        .then_inc(sem, 16)
                    pool.dma_start(buf["idx"][:, cols], k_idx[bass.ds(page, 1)].rearrange("o p k -> p (o k)"))\
                        .then_inc(sem, 16)

            def load_values(b):
                for g in range(PAGES):
                    page = page_of(b, g)
                    for kind, cache in (("diff", v_diff), ("sparse", v_sparse)):
                        pool.dma_start(vbuf[b][kind][:, g, :], cache[bass.ds(page, 1)].rearrange("o p e -> p (o e)"))\
                            .then_inc(vc_loaded[b], 16)

            load_keys(0)
            load_keys(1)
            load_values(0)
            load_values(1)
            pool.wait_ge(S["z_even_free"], 1 + Z_TILES // 2)
            pool.wait_ge(S["z_odd_free"], 1 + Z_TILES // 2)
            pool.dma_start(kv_out, z[:, KA:KI + 1, :]).then_inc(S["kv_stored"], 16)
            for b in range(TS):
                buf = kbuf[b % 2]
                pool.wait_ge(k_loaded[b % 2], 96 * (b // 2 + 1))
                chain.put(pool.tensor_copy(buf["diff"][:, :, PAST], z[:, KA:KA + 4, TP + b]))
                chain.put(pool.tensor_copy(buf["sparse"][:, :, PAST], z[:, KS:KS + 4, TP + b]))
                pool.tensor_copy(buf["idx"][:, PAST:KEYS], z[:, KI, TP + b:TP + b + 1]).then_inc(S["k_ready"], 1)
                if b + 2 < TS:
                    pool.wait_ge(S["k_used"], b + 1)
                    load_keys(b + 2)
                else:
                    qt = b + 2 - TS
                    pool.wait_ge(S["sel_prompt"], qt + 1)
                    keys = P if qt == 0 else 2 * P
                    pool.tensor_tensor(s_view(s_sparse, qt), bias[:, B_SPARSE:B_SPARSE + 8, 256 - keys:256],
                                       iscore[qt].unsqueeze(1).to_broadcast([P, 8, keys]), ALU.add)\
                        .then_inc(S["bias_masked"], 1)
            pool.wait_ge(S["sample_scored"], 1)
            for b in range(2, 6):
                load_values(b)
            pool.wait_ge(S["bias_masked"], 2)
            pool.wait_ge(S["diff_max"], 6)
            load_values(6)
            await_unit(pool, "sparse5")
            load_values(7)
            await_unit(pool, "sparseT5")
            pool.memset(s_sparse[:, 0:2048], 0.0).then_inc(S["pad_zero"], 1)
            await_unit(pool, "sparse_o1")
            pool.dma_start(subk, sub_keys).then_inc(S["subkeys_loaded"], 16)
            pool.sem_inc(S["merged"], 2)
            with pool.Fori(0, 2) as i:
                for k in range(4):
                    n = i * 4 + k
                    pool.wait_ge(S["up_a_free"], 4 + n + 1)
                    pool.wait_ge(S["table_loaded"], 16)
                    m = merged[:, bass.ds(n, 1), :].rearrange("p o t -> p (o t)")
                    pool.tensor_tensor(m, m, up_tmp[k % 2], ALU.add).then_inc(S["merged"], 1)
            def wq_low(i, k):
                raw, _, _ = ring_tile(WQ_AT + k)
                pool.wait_ge(S["wq_hi_made"], i * RING + k + 1)
                pool.tensor_tensor(halves_of(wq_lo, k, D), raw, halves_of(wq_hi, k, D), ALU.subtract)\
                    .then_inc(S["wq_lo_made"], 1)

            wq_low(0, 0)
            wq_low(0, 1)
            with pool.Fori(0, HC // 4 - 1) as i:
                for k in range(4):
                    pool.wait_ge(S["tiles_done"], WQ_AT + i * 4 + k + 1)
                    wq_low(i, k + 2)
            for k in range(2):
                pool.wait_ge(S["tiles_done"], WQ_AT + HC - 4 + k + 1)
                wq_low(HC // 4 - 1, k + 2)
            pool.sem_inc(S["u_lo_made"], 2)
            with pool.Fori(0, NK // RING) as i:
                for k in range(RING):
                    raw, _, _ = expert_tile(i, k)
                    pool.wait_ge(S["u_hi_made"], i * RING + k + 1)
                    pool.wait_ge(S["u_done"], i * RING + k + 1)
                    pool.tensor_tensor(halves_of(w_lo, k, D), raw, halves_of(w_hi, k, D), ALU.subtract)\
                        .then_inc(S["u_lo_made"], 1)
            pool.wait_ge(S["u_done"], 2 + NK)
            pool.tensor_tensor(pre.rearrange("p c t -> p (c t)"), h_hi[:, :], h_lo[:, :], ALU.add)\
                .then_inc(S["h_restored"], 1)
            pool.wait_ge(S["gelu_done"], 4 + NK)
            pool.sem_inc(S["g_applied"], 2)
            with pool.Fori(0, T // 8) as i:
                for q in range(2):
                    pool.wait_ge(S["g_free"], 2 + i * 2 + q + 1)
                    pool.wait_ge(S["table_loaded"], 16)
                    cells = gelu_all[:, :, bass.ds(i * 8 + q * 4, 4)].rearrange("p b t -> p t b")
                    pool.tensor_tensor(cells, gtmp[:, q, :].rearrange("p (t b) -> p t b", t=4), cells, ALU.mult)\
                        .then_inc(S["g_applied"], 1)

        @block.scalar
        def _(act):
            act.dma_start(cst[:, :], consts).then_inc(S["consts_loaded"], 16)
            act.dma_start(par[:, :], params).then_inc(S["params_loaded"], 16)
            act.dma_start(bias, alibi).then_inc(S["alibi_loaded"], 16)
            act.dma_start(sbias[0:64, :], sample_bias).then_inc(S["alibi_loaded"], 16)
            act.sem_inc(S["z_even_free"], 1)
            act.wait_ge(S["consts_loaded"], 16)

            def evac_z(i, tile):
                act.wait_ge(S["tiles_done"], tile + 1)
                act.wait_ge(S["consts_loaded"], 16)
                act.activation(z[:, bass.ds(tile, 1), :].rearrange("p o t -> p (o t)"), psum[:, 0, 0:T], ACT.Copy)\
                    .then_inc(S["z_even_free"], 1)


            def z_high(i, k):
                raw, sem, count = ring_tile(k)
                act.wait_ge(sem, count + i * 16)
                act.activation(halves_of(z_hi, k, D), raw, ACT.Copy).then_inc(S["z_hi_made"], 1)

            z_high(0, 0)
            for k in range(DC):
                act.wait_ge(x_loaded[k // 4], 16)
                act.activation(part(x_hi, k, T), part(xt, k, T), ACT.Copy).then_inc(S["x_hi_made"], 1)
            z_high(0, 1)
            with act.Fori(0, Z_TILES // RING) as i:
                for k in range(RING):
                    act.wait_ge(S["tiles_done"], i * RING + k + 1)
                    z_high(i, k + 2)
                    if k % 2 == 0:
                        evac_z(i, i * RING + k)
            evac_z(0, Z_TILES - 2)
            await_unit(act, "wi")
            act.activation(lam[:, 2:4], bank("wi")[:, 128:130], ACT.Exp).then_inc(S["lam_ready"], 1)
            for u, unit in enumerate(SCORE_UNITS):
                await_unit(act, f"idx{u}")
                qt, keys = unit[0], P * (unit[0] + 1)
                drain_unit(act.activation(of_unit(s_view(s_sparse, qt), unit),
                                          bank(f"idx{u}").rearrange("p (m k) -> p m k", k=keys),
                                          ACT.Relu, scale=SCALE), f"idx{u}")
            for kind in ("diff", "sparse"):
                for kt in range(2):
                    await_unit(act, f"v_{kind}{kt}")
                    drain_unit(act.activation(v_tok[kind][:, kt, :], bank(f"v_{kind}{kt}"), ACT.Copy), f"v_{kind}{kt}")
            def prompt_exp(kind, buf, col):
                for u, (qt, i, j0, n) in enumerate(SCORE_UNITS):
                    act.wait_ge(S[f"{kind}_max"], u + 1)
                    for m in range(2 * j0 + i, 2 * (j0 + n) + i, 2):
                        at = col + qt * 8 + m
                        row = s_view(buf, qt)[:, m, :]
                        act.activation(row, row, ACT.Exp, bias=mx[:, at:at + 1], accum_out=sums[:, at:at + 1])\
                            .then_inc(S[f"{kind}_exp"], 1)

            def sample_exp(n, kind):
                act.wait_ge(S["samp_max"], n + 1)
                act.activation(s_samp[kind][0:64, :], s_samp[kind][0:64, :], ACT.Exp,
                               bias=samp_small[0:64, n:n + 1], accum_out=samp_small[0:64, 2 + n:3 + n])\
                    .then_inc(S["samp_exp"], 1)

            def evac_gate(n):
                act.wait_ge(S["tiles_done"], Z_TILES + n + 1)
                act.activation(gate[:, n, :], psum[:, n % 2, 0:T], ACT.Sigmoid)\
                    .then_inc(S[("z_even_free", "z_odd_free")[n % 2]], 1)

            def evac_pt(kind, u):
                name = f"{kind}T{u}"
                await_unit(act, name)
                drain_unit(act.activation(pt[:, 4 * u:4 * u + 4, :].rearrange("p n q -> p (n q)"), bank(name), ACT.Copy), name)

            def evac_o(kind, u, dst):
                name = f"{kind}_o{u}"
                await_unit(act, name)
                drain_unit(act.activation(dst[:, 2 * u:2 * u + 2, 0:TP], bank(name).rearrange("p (j q) -> p j q", j=2),
                                          ACT.Copy), name)

            prompt_exp("diff", s_diff, 0)
            for n in range(EARLY_GATES):
                evac_gate(n)
            act.wait_ge(S["sample_scored"], 1)
            act.activation(relu_samp[0:64, :], psum[0:64, 4, 0:KEYS], ACT.Relu, scale=SCALE)\
                .then_inc(S["relu_sample"], 1)
            prompt_exp("sparse", s_sparse, 16)
            evac_gate(EARLY_GATES)
            evac_gate(EARLY_GATES + 1)
            for u in range(3):
                evac_pt("diff", u)
            for u in range(2):
                evac_o("diff", u, o_diff)
            await_drained(act, "diff_o1")
            act.activation(s_diff[:, 0:4 * TP].rearrange("p (j t) -> p j t", j=4), o_diff[:, :, 0:TP], ACT.Square)\
                .then_inc(S["rms_square"], 1)
            evac_gate(EARLY_GATES + 2)
            evac_gate(EARLY_GATES + 3)
            for u in range(6):
                evac_pt("sparse", u)
            sample_exp(0, "diff")
            sample_exp(1, "sparse")
            for u in range(2):
                evac_o("sparse", u, o_sparse)
            act.wait_ge(S["rms_recip"], 1)
            act.activation(s_diff[:, RMS:RMS + 4 * TP], s_diff[:, RMS:RMS + 4 * TP], ACT.Sqrt).then_inc(S["rms_root"], 1)
            act.wait_ge(S["out_sample_ready"], 1)
            act.activation(s_diff[:, 4 * TP:4 * T].rearrange("p (j t) -> p j t", j=4), o_diff[:, :, TP:T], ACT.Square)\
                .then_inc(S["rms_square"], 1)
            act.wait_ge(S["rms_recip"], 2)
            act.activation(s_diff[:, RMS + 4 * TP:RMS + 4 * T], s_diff[:, RMS + 4 * TP:RMS + 4 * T], ACT.Sqrt)\
                .then_inc(S["rms_root"], 1)

            def norm(n, src, dst, g, b):
                for k in range(DC):
                    act.wait_ge(S["ln_centred"], n * DC + k + 1)
                    act.activation(squares[:, k, :], src[:, k, :], ACT.Square).then_inc(S["ln_square"], 1)
                act.wait_ge(S["ln_recip"], n + 1)
                act.activation(ln_root, ln_root, ACT.Sqrt).then_inc(S["ln_root"], 1)
                for k in range(0, DC, 2):
                    act.wait_ge(S["ln_scaled"], n * DC + k + 1)
                    act.activation(dst[:, k, :], src[:, k, :], ACT.Identity, bias=par[:, b + k:b + k + 1],
                                   scale=par[:, g + k:g + k + 1]).then_inc(S["ln_even"], 1)

            def wq_high(i, k):
                raw, sem, count = ring_tile(WQ_AT + k)
                act.wait_ge(sem, count + i * 16)
                act.activation(halves_of(wq_hi, k, D), raw, ACT.Copy).then_inc(S["wq_hi_made"], 1)

            act.wait_ge(S["out_sample_ready"], 2)
            act.wait_ge(S["merged"], 2 + DC)
            wq_high(0, 0)
            wq_high(0, 1)
            act.wait_ge(S["params_loaded"], 16)
            norm(0, pre, h, P_LN1G, P_LN1B)
            for k in range(0, DC, 2):
                act.wait_ge(S["ln_even"], k // 2 + 1)
                act.wait_ge(S["ln_odd"], k // 2 + 1)
                act.activation(h_hi[:, k * T:(k + 2) * T], xt[:, k * T:(k + 2) * T], ACT.Copy).then_inc(S["h_hi_made"], 1)
            act.sem_inc(S["q_evac"], 2)

            def evac_q(i, k):
                act.wait_ge(S["score_filled"], i * 4 + k + 1)
                act.wait_ge(S["tiles_done"], WQ_AT + i * 4 + k + 1)
                act.activation(q_sb[k % 2], psum[:, k % 2, 0:T], ACT.Copy).then_inc(S["q_evac"], 1)

            with act.Fori(0, HC // 4 - 1) as i:
                for k in range(4):
                    evac_q(i, k)
                    wq_high(i, k + 2)
            for k in range(4):
                evac_q(HC // 4 - 1, k)
                if k < 2:
                    wq_high(HC // 4 - 1, k + 2)

            def high_part(i, k):
                raw, sem, count = expert_tile(i, k)
                act.wait_ge(sem, count)
                act.wait_ge(S["u_hi_used"], i * RING + k + 1)
                act.wait_ge(S["u_lo_made"], i * RING + k + 1)
                act.activation(halves_of(w_hi, k, D), raw, ACT.Copy).then_inc(S["u_hi_made"], 1)

            def gelu(i, k):
                act.wait_ge(S["u_done"], 2 + i * RING + k + 1)
                act.wait_ge(S["consts_loaded"], 16)
                act.activation(gelu_all[:, bass.ds(i * RING + k, 1), :].rearrange("p o t -> p (o t)"),
                               psum[:, 4 + k, 0:T], ACT.Gelu).then_inc(S["gelu_done"], 1)

            act.wait_ge(S["h_lo_made"], DC // 2)
            high_part(0, 0)
            high_part(0, 1)
            act.sem_inc(S["gelu_done"], 4)
            with act.Fori(0, ROUTED // RING) as i:
                for k in range(RING):
                    high_part(i, k + 2)
                    gelu(i, k)
            act.wait_ge(S["route_ready"], 1)
            for n, (_, rows) in enumerate(TOKEN_TILES):
                act.activation(top_val[0:rows, n, :], top_val[0:rows, n, :], ACT.Exp).then_inc(S["route_exp"], 1)
            with act.Fori(ROUTED // RING, NK // RING - 1) as i:
                for k in range(RING):
                    high_part(i, k + 2)
                    gelu(i, k)
            for k in range(RING):
                if k < RING - 2:
                    high_part(NK // RING - 1, k + 2)
                gelu(NK // RING - 1, k)
            act.sem_inc(S["g_free"], 2)

            def weigh(n, q, side):
                act.wait_ge(S["rows_bare"], n * 2 + q + 1)
                for k in range(4 * q, 4 * q + 2):
                    act.activation(p2[:, k, :], p2[:, k, :], ACT.Copy, scale=tok[:, side, 2, k:k + 1])\
                        .then_inc(S["rows_weighted"], 1)

            def evac_g(n, q):
                act.wait_ge(S["g_applied"], n * 2 + q + 1)
                act.wait_ge(S["g_filled"], 2 + n * 2 + q + 1)
                act.activation(gtmp[:, q, :], psum[:, 4 + q, :], ACT.Copy).then_inc(S["g_free"], 1)

            weigh(0, 0, 0)
            with act.Fori(0, T // 16) as i:
                for side in range(2):
                    n = i * 2 + side
                    weigh(n, 1, side)
                    evac_g(n, 0)
                    weigh(n + 1, 0, 1 - side)
                    evac_g(n, 1)
            weigh(T // 8 - 1, 1, 0)
            for q in range(2):
                evac_g(T // 8 - 1, q)
            with act.Fori(0, NK // RING) as i:
                for k in range(RING):
                    raw, sem, count = expert_tile(i, k)
                    act.wait_ge(sem, count + 16 * NK // RING)
                    act.wait_ge(S["v_hi_used"], i * RING + k + 1)
                    act.wait_ge(S["v_lo_made"], i * RING + k + 1)
                    act.activation(halves_of(w_hi, k, D), raw, ACT.Copy).then_inc(S["v_hi_made"], 1)
            norm(1, acc, y_t, P_LN2G, P_LN2B)

        @block.vector
        def _(dve):
            chain = Chain(dve, S["dve_chain"])
            dve.sem_inc(S["z_odd_free"], 1)
            dve.wait_ge(S["params_loaded"], 16)
            dve.tensor_tensor(lam[0:64, 0:2], par[0:64, P_LAM:P_LAM + 2], par[0:64, P_LAM + 2:P_LAM + 4], ALU.mult)\
                .then_inc(S["lam_products"], 1)
            for k in range(DC):
                dve.wait_ge(x_loaded[k // 4], 16)
                dve.wait_ge(S["x_hi_made"], k + 1)
                dve.tensor_tensor(part(x_lo, k, T), part(xt, k, T), part(x_hi, k, T), ALU.subtract)\
                    .then_inc(S["x_lo_made"], 1)

            def z_low(i, k):
                raw, _, _ = ring_tile(k)
                dve.wait_ge(S["z_hi_made"], i * RING + k + 1)
                dve.tensor_tensor(halves_of(z_lo, k, D), raw, halves_of(z_hi, k, D), ALU.subtract)\
                    .then_inc(S["z_lo_made"], 1)

            def evac_z(tile):
                dve.wait_ge(S["tiles_done"], tile + 1)
                dve.wait_ge(S["params_loaded"], 16)
                dve.tensor_copy(z[:, bass.ds(tile, 1), :].rearrange("p o t -> p (o t)"), psum[:, 1, 0:T])\
                    .then_inc(S["z_odd_free"], 1)

            z_low(0, 0)
            z_low(0, 1)
            with dve.Fori(0, Z_TILES // RING) as i:
                for k in range(RING):
                    dve.wait_ge(S["tiles_done"], i * RING + k + 1)
                    z_low(i, k + 2)
                    if k % 2:
                        evac_z(i * RING + k)
            evac_z(Z_TILES - 1)

            dve.wait_ge(S["qpad_zero"], 1)
            dve.wait_ge(S["z_even_free"], 1 + Z_TILES // 2)
            dve.wait_ge(S["z_odd_free"], 1 + Z_TILES // 2)
            for kind, at, tile, steps in (("diff", 0, QA, (514, 72)), ("sparse", 2048, QS, (514, 72)),
                                          ("idx", 4096, QI, (2, 72))):
                for i in range(2):
                    half = slice(i * HD, (i + 1) * HD)
                    spread = qpad_flat[half, at + i:at + i + 1]
                    dst = bass.AP(spread.tensor, spread.offset,
                                  [list(spread.ap[0]), [steps[0], 4], [steps[1], TS]])
                    dve.tensor_copy(dst, z[half, tile:tile + 4, TP:T]).then_inc(S["qpad_ready"], 1)

            await_unit(dve, "wi")
            dve.wait_ge(S["lam_ready"], 1)
            chain.put(dve.tensor_scalar(head_w[:, 0:16], bank("wi")[:, 0:16], SUBHEADS ** -0.5, None, ALU.mult))
            chain(dve.tensor_scalar(head_w[0:64, 16:24], bank("wi")[0:64, 16:24], SUBHEADS ** -0.5, None, ALU.mult))
            drain_unit(dve.tensor_tensor(wsel[0:64, :], head_w[0:64, 16:24], cst[0:64, C_DIAG:C_DIAG + TS],
                                         ALU.mult), "wi")
            chain(dve.tensor_tensor(neglam, lam[:, 3:4], lam[:, 2:3], ALU.subtract))
            chain(dve.tensor_scalar(neglam, neglam, -LAM_INIT, None, ALU.add))

            dve.wait_ge(S["alibi_loaded"], 32)
            for qt in range(2):
                keys = P * (qt + 1)
                for m in range(SUBHEADS):
                    u = next(u for u, (g, i, j0, n) in enumerate(SCORE_UNITS)
                             if g == qt and i == m % 2 and j0 <= m // 2 < j0 + n)
                    await_drained(dve, f"idx{u}")
                    r = s_view(s_sparse, qt)[:, m, :]
                    weight = head_w[:, qt * 8 + m:qt * 8 + m + 1]
                    if m == 0:
                        chain(dve.tensor_scalar(iscore[qt], r, weight, None, ALU.mult))
                    else:
                        chain(dve.scalar_tensor_tensor(iscore[qt], r, weight, iscore[qt], ALU.mult, ALU.add))
                chain(dve.tensor_tensor(iscore[qt], iscore[qt], bias[:, B_CAUSAL, 256 - keys:256], ALU.add))

            def score(kind, buf, col, u):
                qt, i, j0, n = unit = SCORE_UNITS[u]
                keys = P * (qt + 1)
                name = f"{kind}{u}"
                await_unit(dve, name)
                src = bank(name).rearrange("p (m k) -> p m k", k=keys)
                dst = of_unit(s_view(buf, qt), unit)
                if kind == "diff":
                    added = bias[:, j0:j0 + n, 256 - keys:256]
                else:
                    dve.wait_ge(S["bias_masked"], qt + 1)
                    added = dst
                drain_unit(dve.scalar_tensor_tensor(dst, src, SCALE, added, ALU.mult, ALU.add), name)
                await_drained(dve, name)
                rows_max = mx[:, col + qt * 8:col + qt * 8 + 8].rearrange("p (j i) -> p i j", i=2)[:, i, j0:j0 + n]
                dve.tensor_reduce(rows_max, dst, AX.X, ALU.max, negate=True)\
                    .then_inc(S[f"{kind}_max"], 1)

            for u in range(6):
                score("diff", s_diff, 0, u)

            def select(which, sem):
                for _ in range(NSEL // 8):
                    for n, r in which:
                        chain.put(dve.max(top8[0:r, 8 * n:8 * n + 8], iscore[n][0:r, :]))
                    chain.settle()
                    for n, r in which:
                        chain.put(dve.match_replace(iscore[n][0:r, :], top8[0:r, 8 * n:8 * n + 8],
                                                    iscore[n][0:r, :], TAKEN))
                    chain.settle()
                for n, r in which:
                    dve.tensor_scalar(iscore[n][0:r, :], iscore[n][0:r, :], TAKEN * 0.97, NEG,
                                      ALU.is_gt, ALU.mult).then_inc(sem, 1)

            select([(0, P), (1, P)], S["sel_prompt"])

            def reciprocals(kind, col):
                dve.wait_ge(S[f"{kind}_exp"], 16)
                chain(dve.reciprocal(recip[:, col:col + 16], sums[:, col:col + 16]))

            reciprocals("diff", 0)
            odd = recip[:, 0:16].rearrange("p (m i) -> p m i", i=2)[:, :, 1]
            chain(dve.tensor_scalar(odd, odd, neglam, None, ALU.mult))
            for qt in range(2):
                s = s_view(s_diff, qt)
                keys = P * (qt + 1)
                chain(dve.tensor_tensor(s, s, recip[:, qt * 8:qt * 8 + 8].unsqueeze(2).to_broadcast([P, 8, keys]), ALU.mult))
                pairs = s.rearrange("p (j i) k -> p j i k", i=2)
                dve.tensor_tensor(pairs[:, :, 0, :], pairs[:, :, 0, :], pairs[:, :, 1, :], ALU.add)\
                    .then_inc(S["diff_attn"], 1)
            await_unit(dve, "isum")
            drain_unit(dve.tensor_copy(iscore[2][0:TS, :], bank("isum")[0:TS, 0:KEYS]), "isum")
            for u in range(6):
                score("sparse", s_sparse, 16, u)
            await_drained(dve, "isum")
            select([(2, TS)], S["sel_sample"])
            reciprocals("sparse", 16)
            for qt in range(2):
                s = s_view(s_sparse, qt)
                dve.tensor_tensor(s, s, recip[:, 16 + qt * 8:24 + qt * 8].unsqueeze(2)
                                  .to_broadcast([P, 8, P * (qt + 1)]), ALU.mult).then_inc(S["sparse_attn"], 1)
            for n, kind in enumerate(("diff", "sparse")):
                dve.wait_ge(S["sample_scored"], 1 + n)
                chain(dve.scalar_tensor_tensor(s_samp[kind][0:64, :], psum[0:64, 2 + n, 0:KEYS], SCALE,
                                               sbias[0:64, n * KEYS:(n + 1) * KEYS], ALU.mult, ALU.add))
                dve.tensor_reduce(samp_small[0:64, n:n + 1], s_samp[kind][0:64, :], AX.X, ALU.max, negate=True)\
                    .then_inc(S["samp_max"], 1)
            dve.wait_ge(S["samp_exp"], 2)
            chain(dve.reciprocal(samp_small[0:64, 4:6], samp_small[0:64, 2:4]))
            chain(dve.scalar_tensor_tensor(samp_small[0:64, 6:7], sbias[0:64, SB_SECOND:SB_SECOND + 1], neglam[0:64, :],
                                           sbias[0:64, SB_FIRST:SB_FIRST + 1], ALU.mult, ALU.add))
            chain(dve.tensor_tensor(samp_small[0:64, 4:5], samp_small[0:64, 4:5], samp_small[0:64, 6:7], ALU.mult))
            for n, kind in enumerate(("diff", "sparse")):
                chain(dve.tensor_scalar(s_samp[kind][0:64, :], s_samp[kind][0:64, :], samp_small[0:64, 4 + n:5 + n],
                                        None, ALU.mult))
                dve.tensor_scalar(new_diag[n][0:64, :], ident[0:64, 0:64], s_samp[kind][0:64, PAST:KEYS], None, ALU.mult)\
                    .then_inc(S["samp_attn"], 1)
            await_unit(dve, "sampT")
            dve.wait_ge(S["pad_zero"], 1)
            for n in range(2):
                base = samp_pad[:, n, 0, 0:1]
                dst = bass.AP(base.tensor, base.offset, [list(base.ap[0]), [512, PAGES], [72, TS], [1, 8]])
                dve.tensor_copy(dst, bank("sampT")[:, 192 * n:192 * n + 128].rearrange("p (g b m) -> p g b m", g=PAGES, b=TS))\
                    .then_inc(S["pad_filled"], 1)
            chain.put(dve.tensor_reduce(att[:, 0:32], bank("sampT")[:, 128:192].rearrange("p (n i) -> p n i", i=2),
                                        AX.X, ALU.add))
            chain.settle()
            drain_unit(dve.tensor_copy(att[:, 32:96], bank("sampT")[:, 320:384]), "sampT")
            await_drained(dve, "sampT")
            new_d = att[:, 0:32].rearrange("p (b j) -> p j b", j=4)
            new_s = att[:, 32:96].rearrange("p (b j i) -> p j b i", j=4, i=2)
            part_d = new_part[:, 0:32].rearrange("p (j b) -> p j b", j=4)
            part_s = new_part[:, 32:64].rearrange("p (j b) -> p j b", j=4)
            chain.put(dve.tensor_tensor(part_d, new_d, z[:, VA:VA + 4, TP:T], ALU.mult))
            for i in range(2):
                half = slice(i * HD, (i + 1) * HD)
                chain.put(dve.tensor_tensor(part_s[half], new_s[half, :, :, i], z[half, VS:VS + 4, TP:T], ALU.mult))
            chain.settle()

            def mean_squares(u, at, n):
                await_unit(dve, f"rms{u}")
                drain_unit(dve.tensor_scalar(s_diff[:, RMS + at:RMS + at + n], bank(f"rms{u}")[:, 0:n], 1.0 / P, EPS,
                                             ALU.mult, ALU.add), f"rms{u}")
                await_drained(dve, f"rms{u}")

            def rms_apply(t0, t1):
                o = o_diff[:, :, t0:t1]
                roots = s_diff[:, RMS + 4 * t0:RMS + 4 * t1].rearrange("p (j t) -> p j t", j=4)
                chain(dve.tensor_tensor(o, o, roots, ALU.mult))
                chain(dve.tensor_scalar(o, o, par[:, P_SUBLN:P_SUBLN + 1], 1.0 - LAM_INIT, ALU.mult, ALU.mult))

            def pick(n, name, mask, heads):
                await_unit(dve, name)
                drain_unit(dve.tensor_tensor(samp_rows[0:64, n, :].rearrange("p (h e) -> p h e", h=heads),
                                             bank(name)[0:64, :].rearrange("p (h e) -> p h e", h=heads),
                                             cst[0:64, mask:mask + heads].unsqueeze(2).to_broadcast([64, heads, 512 // heads]),
                                             ALU.mult), name)

            for u in range(2):
                mean_squares(u, 512 * u, 512)
            dve.reciprocal(s_diff[:, RMS:RMS + 4 * TP], s_diff[:, RMS:RMS + 4 * TP]).then_inc(S["rms_recip"], 1)
            pick(0, "samp_diff", C_PAIR, 4)
            dve.wait_ge(S["rms_root"], 1)
            rms_apply(0, TP)
            pick(1, "samp_sparse", C_HEAD, 8)
            await_unit(dve, "samp_o")
            o_d = bank("samp_o")[:, 0:32].rearrange("p (j b) -> p j b", j=4)
            o_s = bank("samp_o")[:, 32:64].rearrange("p (j b) -> p j b", j=4)
            await_drained(dve, "sparse_o1")
            await_drained(dve, "diff_o1")
            chain(dve.tensor_tensor(o_sparse[:, :, TP:T], o_s, part_s, ALU.add))
            drain_unit(dve.tensor_tensor(o_diff[:, :, TP:T], o_d, part_d, ALU.add), "samp_o")
            await_drained(dve, "samp_o")
            dve.sem_inc(S["out_sample_ready"], 1)
            mean_squares(2, 4 * TP, 4 * TS)
            dve.reciprocal(s_diff[:, RMS + 4 * TP:RMS + 4 * T], s_diff[:, RMS + 4 * TP:RMS + 4 * T])\
                .then_inc(S["rms_recip"], 1)
            dve.wait_ge(S["rms_root"], 2)
            rms_apply(TP, T)
            dve.sem_inc(S["out_sample_ready"], 1)

            dve.wait_ge(S["kv_stored"], 16)
            dve.sem_inc(S["up_b_free"], 4)
            dve.sem_inc(S["up_a_free"], 4)
            with dve.Fori(0, 2) as i:
                def row(of, at):
                    return of[:, bass.ds(at, 1), :].rearrange("p o t -> p (o t)")

                for k in range(4):
                    n = i * 4 + k
                    dve.wait_ge(S["up_b_filled"], n + 1)
                    dve.tensor_tensor(row(merged, n), psum[:, k, 0:T], row(gate, n + DC), ALU.mult)\
                        .then_inc(S["up_b_free"], 1)
                for k in range(4):
                    n = i * 4 + k
                    dve.wait_ge(S["tiles_done"], UP_AT + n + 1)
                    dve.wait_ge(S["merged"], n + 1)
                    dve.tensor_tensor(up_tmp[k % 2], psum[:, 4 + k, 0:T], row(gate, n), ALU.mult)\
                        .then_inc(S["up_a_free"], 1)
            dve.sem_inc(S["out_free"], 4)
            with dve.Fori(0, 2) as i:
                for k in range(4):
                    n = i * 4 + k
                    dve.wait_ge(S["tiles_done"], OUT_AT + n + 1)
                    dve.scalar_tensor_tensor(pre[:, bass.ds(n, 1), :].rearrange("p o t -> p (o t)"),
                                             xt[:, bass.ds(n * T, T)], ALPHA, psum[:, k, 0:T], ALU.mult, ALU.add)\
                        .then_inc(S["out_free"], 1)

            def norm(n, src, dst, g, b):
                dve.wait_ge(S["ln_stat"], 2 * n + 1)
                chain(dve.tensor_scalar(ln_mean, psum[:, 6, 0:T], 1.0 / D, None, ALU.mult))
                for k in range(DC):
                    dve.tensor_tensor(src[:, k, :], src[:, k, :], ln_mean, ALU.subtract).then_inc(S["ln_centred"], 1)
                dve.wait_ge(S["ln_stat"], 2 * n + 2)
                chain(dve.tensor_scalar(ln_root, psum[:, 7, 0:T], 1.0 / D, EPS, ALU.mult, ALU.add))
                dve.reciprocal(ln_root, ln_root).then_inc(S["ln_recip"], 1)
                dve.wait_ge(S["ln_root"], n + 1)
                for k in range(DC):
                    dve.tensor_tensor(src[:, k, :], src[:, k, :], ln_root, ALU.mult).then_inc(S["ln_scaled"], 1)
                    if k % 2:
                        dve.wait_ge(S["ln_scaled"], n * DC + k + 1)
                        dve.tensor_scalar(dst[:, k, :], src[:, k, :], par[:, g + k:g + k + 1], par[:, b + k:b + k + 1],
                                          ALU.mult, ALU.add).then_inc(S["ln_odd"], 1)

            norm(0, pre, h, P_LN1G, P_LN1B)
            for k in range(0, DC, 2):
                dve.wait_ge(S["h_hi_made"], k // 2 + 1)
                dve.tensor_tensor(h_lo[:, k * T:(k + 2) * T], xt[:, k * T:(k + 2) * T], h_hi[:, k * T:(k + 2) * T],
                                  ALU.subtract).then_inc(S["h_lo_made"], 1)

            dve.sem_inc(S["score_free"], 2)
            for hc in range(HC):
                dve.wait_ge(S["score_filled"], 2 + hc + 1)
                scores = [psum[0:r, 2 + hc % 2, n * P:(n + 1) * P] for n, (_, r) in enumerate(TOKEN_TILES)]
                val = [route_val[0:r, n, hc, :] for n, (_, r) in enumerate(TOKEN_TILES)]
                idx = [route_idx[0:r, n, hc, :] for n, (_, r) in enumerate(TOKEN_TILES)]
                left = [rest128[n][0:r, :] for n, (_, r) in enumerate(TOKEN_TILES)]
                for n in range(3):
                    chain.put(dve.max(val[n][:, 0:8], scores[n]))
                chain.settle()
                for n in range(3):
                    chain.put(dve.match_replace(left[n], val[n][:, 0:8], scores[n], TAKEN))
                for n in range(3):
                    last = dve.max_index(idx[n][:, 0:8], val[n][:, 0:8], scores[n])
                    if n == 2:
                        last.then_inc(S["score_free"], 1)
                chain.settle()
                for n in range(3):
                    chain.put(dve.max(val[n][:, 8:16], left[n]))
                chain.settle()
                for n in range(3):
                    chain.put(dve.max_index(idx[n][:, 8:16], val[n][:, 8:16], left[n]))
            chain.settle()

            for n, (_, r) in enumerate(TOKEN_TILES):
                chain(dve.tensor_copy(route_idxf[0:r, n], route_idx[0:r, n]))
                halves = route_val[0:r, n].rearrange("p (h c) k -> p h c k", c=2)
                first = halves[:, :, 0, :].unsqueeze(3).to_broadcast([r, 8, TOP, TOP])
                second = halves[:, :, 1, :].unsqueeze(2).to_broadcast([r, 8, TOP, TOP])
                sums4 = cand[0:r, :].rearrange("p (h i j) -> p h i j", h=8, i=TOP)
                chain(dve.tensor_tensor(sums4, first, second, ALU.add))
                best = top_val[0:r, n, :].rearrange("p (h k) -> p h k", h=8)
                pos = top_pos[0:r, :].rearrange("p (h k) -> p h k", h=8)
                for hp in range(0, 8, 2):
                    pair = [(cand[0:r, (hp + q) * 256:(hp + q + 1) * 256], rest[q][0:r, :], hp + q) for q in range(2)]
                    for rows_c, _, hh in pair:
                        chain.put(dve.max(best[:, hh, 0:8], rows_c))
                    chain.settle()
                    for rows_c, left, hh in pair:
                        chain.put(dve.match_replace(left, best[:, hh, 0:8], rows_c, TAKEN))
                    for rows_c, left, hh in pair:
                        chain.put(dve.max_index(pos[:, hh, 0:8], best[:, hh, 0:8], rows_c))
                    chain.settle()
                    for rows_c, left, hh in pair:
                        chain.put(dve.max(best[:, hh, 8:16], left))
                    chain.settle()
                    for rows_c, left, hh in pair:
                        chain.put(dve.max_index(pos[:, hh, 8:16], best[:, hh, 8:16], left))
                    chain.settle()
                for op, arg, c2, dst in ((ALU.logical_shift_right, 4, 0, first_id), (ALU.bitwise_and, 15, 1, second_id)):
                    chain(dve.tensor_single_scalar(pos_part[0:r, :], top_pos[0:r, :], arg, op))
                    chain(dve.tensor_copy(pos_f[0:r, :], pos_part[0:r, :]))
                    oh = onehot[0:r, :].rearrange("p (n i) -> p n i", i=TOP)
                    chain(dve.tensor_tensor(oh, pos_f[0:r, :].unsqueeze(2).to_broadcast([r, P, TOP]),
                                            iota16[0:r, :].unsqueeze(1).to_broadcast([r, P, TOP]), ALU.is_equal))
                    oh4 = onehot[0:r, :].rearrange("p (h k i) -> p h k i", h=8, k=TOP)
                    ids = route_idxf[0:r, n].rearrange("p (h c) k -> p h c k", c=2)[:, :, c2, :]
                    chain(dve.tensor_tensor(oh4, oh4, ids.unsqueeze(2).to_broadcast([r, 8, TOP, TOP]), ALU.mult))
                    chain(dve.tensor_reduce(dst[0:r, n, :], oh, AX.X, ALU.add))
                chain(dve.tensor_copy(denom[0:r, n, :], best[:, :, 0]))
                chain(dve.tensor_tensor(best, best, denom[0:r, n, :].unsqueeze(2).to_broadcast([r, 8, TOP]), ALU.subtract))
            dve.sem_inc(S["route_ready"], 1)
            for n, (_, r) in enumerate(TOKEN_TILES):
                best = top_val[0:r, n, :].rearrange("p (h k) -> p h k", h=8)
                dve.wait_ge(S["route_exp"], n + 1)
                chain(dve.tensor_reduce(denom[0:r, n, :], best, AX.X, ALU.add))
                chain(dve.reciprocal(denom[0:r, n, :], denom[0:r, n, :]))
                chain(dve.tensor_tensor(best, best, denom[0:r, n, :].unsqueeze(2).to_broadcast([r, 8, TOP]), ALU.mult))
            dve.sem_inc(S["gates_normed"], 1)
            for n in range(3):
                dve.wait_ge(S["route_filled"], n + 1)
                dve.tensor_copy(slots[:, n, :], psum[:, 1 + n, 0:T]).then_inc(S["route_copied"], 1)

            dve.wait_ge(S["route_copied"], 3)

            def rows_of(n, side, last_turn=False):
                dve.wait_ge(S["tok_ready"], n + 1)
                for q in range(2):
                    dve.wait_ge(S["g_filled"], n * 2 + q + 1)
                    if q and not last_turn:
                        dve.tensor_copy(tok[:, 1 - side], slots[:, :, bass.ds(n * 8 + 8, 8)])\
                            .then_inc(S["tok_ready"], 1)
                    four = slice(4 * q, 4 * q + 4)
                    two = slice(4 * q, 4 * q + 2)
                    dve.tensor_tensor(p2[:, two, :], iota.unsqueeze(1).to_broadcast([P, 2, P]),
                                      tok[:, side, 1, two].unsqueeze(2).to_broadcast([P, 2, P]), ALU.is_equal)\
                        .then_inc(S["rows_bare"], 1)
                    dve.tensor_tensor(p1[:, four, :], iota.unsqueeze(1).to_broadcast([P, 4, P]),
                                      tok[:, side, 0, four].unsqueeze(2).to_broadcast([P, 4, P]), ALU.is_equal)
                    for k in range(4 * q + 2, 4 * q + 4):
                        last = dve.tensor_scalar(p2[:, k, :], iota, tok[:, side, 1, k:k + 1], tok[:, side, 2, k:k + 1],
                                                 ALU.is_equal, ALU.mult)
                    last.then_inc(S["rows_ready"], 1)

            dve.tensor_copy(tok[:, 0], slots[:, :, 0:8]).then_inc(S["tok_ready"], 1)
            with dve.Fori(0, T // 16) as i:
                for side in range(2):
                    rows_of(i * 2 + side, side)
            rows_of(T // 8 - 1, 0, last_turn=True)

            dve.wait_ge(S["g_applied"], 2 + T // 4)
            dve.sem_inc(S["v_lo_made"], 2)
            with dve.Fori(0, NK // RING) as i:
                for k in range(RING):
                    raw, _, _ = expert_tile(i, k)
                    cells = gelu_all[:, bass.ds(i * RING + k, 1), :].rearrange("p o t -> p (o t)")
                    dve.wait_ge(S["v_done"], i * RING + k + 1)
                    dve.wait_ge(S["params_loaded"], 16)
                    dve.tensor_copy(halves_of(cells_hi, k, T), cells).then_inc(S["cells_hi_made"], 1)
                    dve.wait_ge(S["cells_hi_made"], i * RING + k + 1)
                    dve.wait_ge(S["params_loaded"], 16)
                    dve.tensor_tensor(halves_of(cells_lo, k, T), cells, halves_of(cells_hi, k, T), ALU.subtract)\
                        .then_inc(S["cells_split"], 1)
                    dve.wait_ge(S["v_hi_made"], i * RING + k + 1)
                    dve.tensor_tensor(halves_of(w_lo, k, D), raw, halves_of(w_hi, k, D), ALU.subtract)\
                        .then_inc(S["v_lo_made"], 1)
            dve.wait_ge(S["h_restored"], 1)
            dve.wait_ge(S["v_lo_made"], 2 + NK)
            for k in range(DC):
                dve.wait_ge(S["v_filled"], k + 1)
                dve.scalar_tensor_tensor(acc[:, k, :], pre[:, k, :], ALPHA, psum[:, k, 0:T], ALU.mult, ALU.add)\
                    .then_inc(S["acc_ready"], 1)
            dve.wait_ge(S["acc_ready"], DC)
            norm(1, acc, y_t, P_LN2G, P_LN2B)

        @block.tensor
        def _(pe):
            def fill(name):
                n = UNIT[name]
                if n >= ROT:
                    pe.wait_ge(drained[n % ROT], n // ROT)

            def project(slot, loaded, out, moving, chunks=DC, first=0):
                if loaded is not None:
                    pe.wait_ge(w_loaded[slot], loaded)
                for k in range(chunks):
                    at = slot * D + (first + k) * P
                    last = pe.matmul(out, ring[:, at:at + P], moving(k), start=(k == 0), stop=(k == chunks - 1))
                return last

            x = xt[:, :].rearrange("p (c t) -> p c t", c=DC)
            for n in range(2):
                pe.wait_ge(x_loaded[n], 16)
            banks_free = (S["z_even_free"], S["z_odd_free"])

            def project_parts(out, hi, lo, x_parts, hi_sem, lo_sem, count, x_sem=None, x_step=1):
                pe.wait_ge(hi_sem, count)
                for c in range(DC):
                    if x_sem is not None and c % x_step == 0:
                        pe.wait_ge(x_sem, c // x_step + 1)
                    pe.matmul(out, part(hi, c, P), part(x_parts[0], c, T), start=(c == 0), stop=False)
                    pe.matmul(out, part(hi, c, P), part(x_parts[1], c, T), start=False, stop=False)
                pe.wait_ge(lo_sem, count)
                for c in range(DC):
                    last = pe.matmul(out, part(lo, c, P), part(x_parts[0], c, T), start=False, stop=(c == DC - 1))
                return last

            def z_tile(i, k):
                pe.wait_ge(banks_free[k % 2], i * 2 + k // 2 + 1)
                project_parts(psum[:, k % 2, 0:T], halves_of(z_hi, k, D), halves_of(z_lo, k, D), (x_hi, x_lo),
                              S["z_hi_made"], S["z_lo_made"], i * RING + k + 1,
                              S["x_lo_made"] if k == 0 else None).then_inc(S["tiles_done"], 1)

            with pe.Fori(0, Z_TILES // RING) as i:
                for k in range(RING):
                    z_tile(i, k)
            for t in range(Z_TILES // RING * RING, Z_TILES):
                z_tile(t // RING, t % RING)

            pe.wait_ge(S["consts_loaded"], 16)
            pe.wait_ge(S["z_even_free"], 1 + Z_TILES // 2)
            pe.wait_ge(S["z_odd_free"], 1 + Z_TILES // 2)
            pe.wait_ge(S["lam_products"], 1)
            fill("wi")
            b = bank("wi")
            for qt in range(2):
                pe.matmul(b[:, 8 * qt:8 * qt + 8], z[0:8, WI, qt * P:(qt + 1) * P], ident[0:8, 0:8], start=True, stop=True)
            pe.matmul(b[0:64, 16:24], cst[0:8, C_HEADROW:C_HEADROW + 64], z[0:8, WI, TP:T], start=True, stop=True)
            pe.matmul(b[:, 128:130], ones[0:64, :], lam[0:64, 0:2], start=True, stop=True)\
                .then_inc(S["unit_filled"], 1)

            def scores(kind, u, q_tile, keys_of):
                qt, i, j0, n = SCORE_UNITS[u]
                fill(f"{kind}{u}")
                b, keys = bank(f"{kind}{u}"), P * (qt + 1)
                half = slice(i * HD, (i + 1) * HD)
                for j in range(n):
                    m = 2 * (j0 + j) + i
                    last = pe.matmul(b[:, j * keys:(j + 1) * keys],
                                     z[half, q_tile + m // 2, qt * P:(qt + 1) * P],
                                     z[half, keys_of(m), 0:keys], start=True, stop=True)
                last.then_inc(S["unit_filled"], 1)

            for u in range(6):
                scores("idx", u, QI, lambda m: KI)
            for kind, tile in (("diff", VA), ("sparse", VS)):
                for kt in range(2):
                    fill(f"v_{kind}{kt}")
                    for j in range(4):
                        last = pe.transpose(bank(f"v_{kind}{kt}")[:, j * P:(j + 1) * P],
                                            z[:, tile + j, kt * P:(kt + 1) * P], ident)
                    last.then_inc(S["unit_filled"], 1)
            for u in range(6):
                scores("diff", u, QA, lambda m: KA + m // 2)

            def ring_use(t):
                return 16 * (t // RING + 1)

            def gate_tile(n):
                t = Z_TILES + n
                pe.wait_ge(banks_free[n % 2], Z_TILES // 2 + n // 2 + 1)
                project(t % RING, ring_use(t), psum[:, n % 2, 0:T], lambda k: x[:, k, :]).then_inc(S["tiles_done"], 1)

            pe.wait_ge(S["qpad_ready"], 6)
            for b in range(TS):
                pe.wait_ge(S["k_ready"], b + 1)
                buf = kbuf[b % 2]
                for n, kind in enumerate(("diff", "sparse")):
                    for j in range(4):
                        last = pe.matmul(psum[0:64, 2 + n, 0:KEYS], qpad[kind][:, j, b, :], buf[kind][:, j, :],
                                         start=(b == 0 and j == 0), stop=(b == TS - 1 and j == 3 and n == 0))
                last = pe.matmul(psum[0:64, 4, 0:KEYS], qpad["idx"][:, b, :], buf["idx"],
                                 start=(b == 0), stop=(b == TS - 1))
                last.then_inc(S["k_used"] if b < TS - 1 else S["sample_scored"], 1)
                if 2 * b + 2 <= EARLY_GATES:
                    gate_tile(2 * b)
                    gate_tile(2 * b + 1)
            pe.wait_ge(S["relu_sample"], 1)
            await_drained(pe, "wi")
            fill("isum")
            pe.matmul(bank("isum")[0:TS, 0:KEYS], wsel[0:64, :], relu_samp[0:64, :], start=True, stop=True)\
                .then_inc(S["unit_filled"], 1)
            for u in range(6):
                scores("sparse", u, QS, lambda m: KS + m // 2)
            gate_tile(EARLY_GATES)
            gate_tile(EARLY_GATES + 1)

            def transposes(kind, buf, heads, head_of):
                for u in range(heads * 3 // 4):
                    fill(f"{kind}T{u}")
                    for q in range(4):
                        h, (qt, kt) = (4 * u + q) // 3, PT_TILES[(4 * u + q) % 3]
                        last = pe.transpose(bank(f"{kind}T{u}")[:, q * P:(q + 1) * P],
                                            s_view(buf, qt)[:, head_of(h), kt * P:(kt + 1) * P], ident)
                    last.then_inc(S["unit_filled"], 1)

            def outputs(kind, heads, width):
                for u in range(2):
                    fill(f"{kind}_o{u}")
                    n = heads // 2
                    for h in range(u * n, (u + 1) * n):
                        row = (h * width) % P
                        col = ((h * width) // P % 2) * TP
                        out = bank(f"{kind}_o{u}")[row:row + width, :]
                        v = v_tok[kind][:, :, h * width:(h + 1) * width]
                        pe.matmul(out[:, col:col + TP], v[:, 0, :],
                                  pt[:, 3 * h:3 * h + 2, :].rearrange("p n q -> p (n q)"), start=True, stop=False)
                        last = pe.matmul(out[:, col + P:col + TP], v[:, 1, :], pt[:, 3 * h + 2, :],
                                         start=False, stop=True)
                    last.then_inc(S["unit_filled"], 1)

            pe.wait_ge(S["diff_attn"], 2)
            transposes("diff", s_diff, 4, lambda h: 2 * h)
            await_drained(pe, "diffT2")
            outputs("diff", 4, P)
            pe.wait_ge(S["sel_sample"], 1)
            pe.matmul(psum[0:64, 3, 0:KEYS], cst[0:TS, C_EXPAND:C_EXPAND + 64], iscore[2][0:TS, :],
                      start=False, stop=True).then_inc(S["sample_scored"], 1)
            gate_tile(EARLY_GATES + 2)
            gate_tile(EARLY_GATES + 3)
            pe.wait_ge(S["sparse_attn"], 2)
            transposes("sparse", s_sparse, 8, lambda h: h)
            await_drained(pe, "sparseT5")
            outputs("sparse", 8, HD)

            pe.wait_ge(S["samp_attn"], 2)
            fill("sampT")
            b = bank("sampT")
            for n, kind in enumerate(("diff", "sparse")):
                for g in range(PAGES):
                    pe.transpose(b[:, 192 * n + 64 * g:192 * n + 64 * (g + 1)],
                                 s_samp[kind][0:64, g * PAGE:(g + 1) * PAGE], ident[0:64, 0:64])
                last = pe.matmul(b[:, 192 * n + 128:192 * n + 192], ones[0:64, :], new_diag[n][0:64, :],
                                 start=True, stop=True)
            last.then_inc(S["unit_filled"], 1)
            await_drained(pe, "sampT")
            pe.wait_ge(S["rms_square"], 1)
            for u in range(2):
                fill(f"rms{u}")
                pe.matmul(bank(f"rms{u}"), ones, s_diff[:, 512 * u:512 * (u + 1)], start=True, stop=True)\
                    .then_inc(S["unit_filled"], 1)
            for n, kind in enumerate(("diff", "sparse")):
                fill(f"samp_{kind}")
                pe.wait_ge(S["pad_filled"], n + 1)
                for b in range(TS):
                    pe.wait_ge(vc_loaded[b], 64)
                    for g in range(PAGES):
                        last = pe.matmul(bank(f"samp_{kind}")[0:64, :], samp_pad[:, n, g, 64 * b:64 * (b + 1)],
                                         vbuf[b][kind][:, g, :], start=(b == 0 and g == 0),
                                         stop=(b == TS - 1 and g == PAGES - 1))
                last.then_inc(S["unit_filled"], 1)
            fill("samp_o")
            for n, kind in enumerate(("diff", "sparse")):
                await_drained(pe, f"samp_{kind}")
                for j in range(4):
                    last = pe.matmul(bank("samp_o")[:, 32 * n + 8 * j:32 * n + 8 * (j + 1)],
                                     samp_rows[0:64, n, j * P:(j + 1) * P], cst[0:64, C_DIAG:C_DIAG + TS],
                                     start=True, stop=True)
            last.then_inc(S["unit_filled"], 1)
            pe.wait_ge(S["rms_square"], 2)
            fill("rms2")
            pe.matmul(bank("rms2")[:, 0:4 * TS], ones, s_diff[:, 4 * TP:4 * T], start=True, stop=True)\
                .then_inc(S["unit_filled"], 1)

            pe.wait_ge(S["out_sample_ready"], 1)
            await_drained(pe, "sparse_o1")
            with pe.Fori(0, DC // 4) as i:
                for k in range(4):
                    t = UP_AT + k
                    pe.wait_ge(S["up_b_free"], i * 4 + k + 1)
                    project(t % RING, i * 16 + ring_use(t), psum[:, k, 0:T], lambda c: o_sparse[:, c, :], chunks=4, first=4)\
                        .then_inc(S["up_b_filled"], 1)
                pe.wait_ge(S["out_sample_ready"], 2)
                for k in range(4):
                    pe.wait_ge(S["up_a_free"], i * 4 + k + 1)
                    project((UP_AT + k) % RING, None, psum[:, 4 + k, 0:T], lambda c: o_diff[:, c, :], chunks=4)\
                        .then_inc(S["tiles_done"], 1)
            pe.wait_ge(S["merged"], 2 + DC)
            with pe.Fori(0, DC // 4) as i:
                for k in range(4):
                    t = OUT_AT + k
                    pe.wait_ge(S["out_free"], i * 4 + k + 1)
                    project(t % RING, i * 16 + ring_use(t), psum[:, k, 0:T], lambda c: merged[:, c, :])\
                        .then_inc(S["tiles_done"], 1)

            def norm(n, src):
                for k in range(DC):
                    last = pe.matmul(psum[:, 6, 0:T], ones, src[:, k, :], start=(k == 0), stop=(k == DC - 1))
                last.then_inc(S["ln_stat"], 1)
                for k in range(DC):
                    pe.wait_ge(S["ln_square"], n * DC + k + 1)
                    last = pe.matmul(psum[:, 7, 0:T], ones, squares[:, k, :], start=(k == 0), stop=(k == DC - 1))
                last.then_inc(S["ln_stat"], 1)

            pe.wait_ge(S["up_a_free"], 4 + DC)
            pe.wait_ge(S["out_free"], 4 + DC)
            norm(0, pre)

            pe.sem_inc(S["u_hi_used"], 2)
            pe.sem_inc(S["u_done"], 2)
            pe.wait_ge(S["subkeys_loaded"], 16)
            pe.sem_inc(S["score_filled"], 2)
            with pe.Fori(0, HC // 4) as i:
                def sub_scores(k):
                    pe.wait_ge(S["q_evac"], 2 + i * 4 + k + 1)
                    pe.wait_ge(S["score_free"], i * 4 + k + 1)
                    for n, (t0, r) in enumerate(TOKEN_TILES):
                        last = pe.matmul(psum[0:r, 2 + k % 2, n * P:(n + 1) * P], q_sb[k % 2][:, t0:t0 + r],
                                         subk[:, bass.ds(i * 4 + k, 1), :].rearrange("p o n -> p (o n)"),
                                         start=True, stop=True)
                    last.then_inc(S["score_filled"], 1)

                for k in range(4):
                    pe.wait_ge(S["q_evac"], i * 4 + k + 1)
                    project_parts(psum[:, k % 2, 0:T], halves_of(wq_hi, k, D), halves_of(wq_lo, k, D), (h_hi, h_lo),
                                  S["wq_hi_made"], S["wq_lo_made"], i * 4 + k + 1,
                                  S["h_lo_made"] if k == 0 else None, 2).then_inc(S["tiles_done"], 1)
                    if k:
                        sub_scores(k - 1)
                sub_scores(3)

            with pe.Fori(0, NK // RING) as i:
                for k in range(RING):
                    out, hi, lo = psum[:, 4 + k, 0:T], halves_of(w_hi, k, D), halves_of(w_lo, k, D)
                    pe.wait_ge(S["gelu_done"], i * RING + k + 1)
                    pe.wait_ge(S["u_hi_made"], i * RING + k + 1)
                    for c in range(DC):
                        pe.matmul(out, part(hi, c, P), part(h_hi, c, T), start=(c == 0), stop=False)
                        last = pe.matmul(out, part(hi, c, P), part(h_lo, c, T), start=False, stop=False)
                    last.then_inc(S["u_hi_used"], 1)
                    pe.wait_ge(S["u_lo_made"], 2 + i * RING + k + 1)
                    for c in range(DC):
                        last = pe.matmul(out, part(lo, c, P), part(h_hi, c, T), start=False, stop=(c == DC - 1))
                    last.then_inc(S["u_done"], 1)

            for n, src in enumerate((first_id, second_id, top_val)):
                pe.wait_ge(S["route_ready"], 1)
                if n == 2:
                    pe.wait_ge(S["gates_normed"], 1)
                for g, (t0, r) in enumerate(TOKEN_TILES):
                    last = pe.transpose(psum[:, 1 + n, t0:t0 + r], src[0:r, g, :], ident[0:r, 0:r])
                last.then_inc(S["route_filled"], 1)
            pe.wait_ge(S["gelu_done"], 4 + NK)
            pe.sem_inc(S["g_filled"], 2)
            with pe.Fori(0, T // 8) as i:
                for q in range(2):
                    pe.wait_ge(S["rows_ready"], i * 2 + q + 1)
                    pe.wait_ge(S["rows_weighted"], (i * 2 + q) * 2 + 2)
                    pe.wait_ge(S["g_free"], i * 2 + q + 1)
                    for k in range(4):
                        last = pe.matmul(psum[:, 4 + q, k * P:(k + 1) * P], p1[:, 4 * q + k, :], p2[:, 4 * q + k, :],
                                         start=True, stop=True)
                    last.then_inc(S["g_filled"], 1)
            pe.sem_inc(S["v_hi_used"], 2)
            pe.sem_inc(S["v_done"], 2)
            pe.wait_ge(S["g_applied"], 2 + T // 4)

            def high_products(k, first=False):
                hi, cells = halves_of(w_hi, k, D), [halves_of(m, k, T) for m in (cells_hi, cells_lo)]
                for c in range(DC):
                    for n in range(2):
                        last = pe.matmul(psum[:, c, 0:T], part(hi, c, P), cells[n], start=(first and n == 0), stop=False)
                last.then_inc(S["v_hi_used"], 1)

            def contract(i, k, first=False):
                pe.wait_ge(S["v_hi_made"], i * RING + k + 1)
                pe.wait_ge(S["cells_split"], i * RING + k + 1)
                high_products(k, first)
                pe.wait_ge(S["v_lo_made"], 2 + i * RING + k + 1)
                for c in range(DC):
                    last = pe.matmul(psum[:, c, 0:T], part(halves_of(w_lo, k, D), c, P), halves_of(cells_hi, k, T),
                                     start=False, stop=False)
                last.then_inc(S["v_done"], 1)

            for k in range(RING):
                contract(0, k, first=(k == 0))
            with pe.Fori(1, NK // RING - 1) as i:
                for k in range(RING):
                    contract(i, k)
            for k in range(RING - 1):
                contract(NK // RING - 1, k)
            pe.wait_ge(S["v_hi_made"], NK)
            pe.wait_ge(S["cells_split"], NK)
            pe.wait_ge(S["v_lo_made"], 2 + NK)
            high_products(RING - 1)
            for c in range(DC):
                pe.matmul(psum[:, c, 0:T], part(halves_of(w_lo, RING - 1, D), c, P), halves_of(cells_hi, RING - 1, T),
                          start=False, stop=True).then_inc(S["v_filled"], 1)
            pe.wait_ge(S["acc_ready"], DC)
            norm(1, acc)


def shape_constants():
    f = np.float32
    consts = np.zeros((P, CONSTS), f)
    consts[:, C_IDENT:C_IDENT + P] = np.eye(P, dtype=f)
    consts[:, C_ONES:C_ONES + P] = 1
    consts[:, C_IOTA:C_IOTA + P] = np.arange(P, dtype=f)
    consts[:, C_IOTA16:C_IOTA16 + TOP] = np.arange(TOP, dtype=f)
    for b in range(TS):
        for m in range(8):
            consts[b, C_EXPAND + b * 8 + m] = 1
            consts[m, C_HEADROW + b * 8 + m] = 1
            consts[b * 8 + m, C_DIAG + b] = 1
            consts[b * 8 + m, C_PAIR + m // 2] = 1
            consts[b * 8 + m, C_HEAD + m] = 1
    slopes = lambda n: [2.0 ** (-8.0 * (i + 1) / n) for i in range(n)]
    dist = (128 + np.arange(P)[:, None] - np.arange(256)[None, :]).astype(f)
    alibi = np.zeros((P, BIASES, 256), f)
    for n, s in enumerate(slopes(4) + slopes(8) + [0.0]):
        alibi[:, n] = np.where(dist >= 0, -f(s) * dist, f(NEG))
    gap = (PAST - np.arange(KEYS)).astype(f)
    sample = np.zeros((64, SBIAS), f)
    for row in range(64):
        m = row % 8
        sample[row, 0:KEYS] = -f(slopes(4)[m // 2]) * gap
        sample[row, KEYS:2 * KEYS] = -f(slopes(8)[m]) * gap
        sample[row, SB_FIRST + m % 2] = 1
    return consts, alibi.reshape(P, -1), sample


def kernel(x_prompt, x_sample, cache_da_k, cache_da_v, cache_sa_k, cache_sa_v, cache_idx_k, page_table,
           w_in, lambda_q1, lambda_k1, lambda_q2, lambda_k2, da_subln_g, w_a_up, w_b_up, w_out,
           ln1_g, ln1_b, peer_wq, peer_sub_keys, peer_u, peer_v, ln2_g, ln2_b):
    import concourse.bacc as bacc
    from concourse.bass_utils import run_bass_kernel_spmd

    arr = lambda v: np.asarray(v)
    x = np.concatenate([arr(x_prompt).reshape(TP, D), arr(x_sample).reshape(TS, D)])
    x_t = x.T.reshape(DC, P, T).transpose(1, 0, 2)

    wi = arr(w_in)[0]
    at = np.cumsum([0, 512, 512, 512, 512, 512, 512, 512, 64, 8, 1024, 1024]).tolist()
    qa, ka, va, qs, ks, vs, qi, ki, wx, ga, gb = [wi[:, at[n]:at[n + 1]] for n in range(11)]
    pad = np.zeros((D, P - 8), wi.dtype)
    cols = np.concatenate([qa, qs, qi, ka, ks, va, vs, ki, ki, wx, pad, ga, gb], axis=1)
    tiled = lambda m: m.reshape(DC, P, -1, P).transpose(2, 1, 0, 3).reshape(-1, P, D)
    up = np.concatenate([arr(w_a_up)[0], arr(w_b_up)[0]], axis=0)
    weights = np.concatenate([tiled(cols), tiled(up), tiled(arr(w_out)[0]), tiled(arr(peer_wq)[0])])

    keys = lambda c: arr(c)[0].reshape(-1, PAGE, 4, P).transpose(0, 3, 2, 1)
    idx_t = arr(cache_idx_k)[0].transpose(0, 2, 1)
    rows = lambda c: arr(c)[0].reshape(-1, PAGE, 512)
    vec = lambda v: arr(v)[0].reshape(DC, P).T
    lam = np.zeros((P, 4), wi.dtype)
    for n, v in enumerate((lambda_q1, lambda_q2, lambda_k1, lambda_k2)):
        lam[0:HD, n] = arr(v)[0]
    params = np.concatenate([vec(ln1_g), vec(ln1_b), vec(ln2_g), vec(ln2_b), arr(da_subln_g)[0][:, None], lam], axis=1)
    consts, alibi, sample = shape_constants()
    ins = {
        "x_t": x_t, "weights": weights,
        "experts_u": arr(peer_u)[0].reshape(P, P, DC, P).transpose(1, 3, 2, 0).reshape(P, P, D),
        "experts_v": arr(peer_v)[0].reshape(P, P, D).transpose(1, 0, 2),
        "k_diff": keys(cache_da_k), "k_sparse": keys(cache_sa_k),
        "k_idx": np.concatenate([idx_t, idx_t], axis=1),
        "v_diff": rows(cache_da_v), "v_sparse": rows(cache_sa_v),
        "page_table": arr(page_table).astype(np.int32).reshape(1, -1),
        "sub_keys": arr(peer_sub_keys)[0].reshape(HC, NK, P).transpose(2, 0, 1),
        "params": params, "consts": consts, "alibi": alibi, "sample_bias": sample,
    }
    outs = {"kv_out": (P, KV_TILES, T), "y_out": (P, DC, T)}
    nc = bacc.Bacc("TRN2", target_bir_lowering=False, num_devices=1)
    arrays, args = {}, {}
    for name, v in ins.items():
        v = np.ascontiguousarray(v)
        arrays[f"{name}_dram"] = v
        args[name] = nc.dram_tensor(f"{name}_dram", v.shape, mybir.dt.from_np(v.dtype), kind="ExternalInput").ap()
    for name, shape in outs.items():
        args[name] = nc.dram_tensor(f"{name}_dram", shape, F32, kind="ExternalOutput").ap()
    build_program(nc, **args)
    r = run_bass_kernel_spmd(nc, [arrays], core_ids=[0]).results[0]
    kv, y = np.asarray(r["kv_out_dram"]), np.asarray(r["y_out_dram"])
    y = y.transpose(2, 1, 0).reshape(T, D)
    kv = kv.transpose(2, 1, 0)
    out = [y[:TP].reshape(1, TP, D), y[TP:].reshape(TS, 1, D)]
    for lo, hi, (bb, ss) in ((0, TP, (1, TP)), (TP, T, (TS, 1))):
        part = lambda t0, width: kv[lo:hi, t0 - KA:t0 - KA + 4].reshape(hi - lo, -1)[:, :width]
        out += [part(KA, 512).reshape(1, bb, ss, 4, 2, 64), part(VA, 512).reshape(1, bb, ss, 4, 128),
                part(KS, 512).reshape(1, bb, ss, 8, 64), part(VS, 512).reshape(1, bb, ss, 8, 64),
                kv[lo:hi, KI - KA, 0:HD].reshape(1, bb, ss, HD)]
    return tuple(np.ascontiguousarray(o) for o in out)
```

```python
import math
from contextlib import ExitStack

import numpy as np

import concourse.bass as bass
import concourse.mybir as mybir

F32 = mybir.dt.float32
F32R = mybir.dt.float32r
U32 = mybir.dt.uint32
I32 = mybir.dt.int32
ALU = mybir.AluOpType
ACT = mybir.ActivationFunctionType
AX = mybir.AxisListType

P = 128
D = 1024
DC = D // P
TP, TS = 256, 8
T = TP + TS
PAST = 256
PAGE = 128
PAGES = PAST // PAGE
KEYS = PAST + 1
HD = 64
SUBHEADS = 8
NSEL = 64
SCALE = HD ** -0.5
ALPHA = 2.0 ** 0.25
LAM_INIT = 0.8 - 0.6 * math.exp(0.0)
EPS = 1e-5
NEG = -1e30
TAKEN = -3e38
HC = 16
NK = 128
TOP = 16
TOKEN_TILES = [(0, P), (P, P), (TP, TS)]

QA, QS, QI, KA, KS, VA, VS, KI, WI, GA, GB = 0, 4, 8, 12, 16, 20, 24, 28, 29, 30, 38
Z_TILES, GATE_TILES = 30, 16
EARLY_GATES = 12
UP_AT = Z_TILES + GATE_TILES
OUT_AT = UP_AT + DC
WQ_AT = OUT_AT + DC
TILES = WQ_AT + HC
RING = 4
KV_TILES = KI + 1 - KA

C_IDENT, C_ONES, C_IOTA, C_IOTA16 = 0, P, 2 * P, 3 * P
C_EXPAND = C_IOTA16 + TOP
C_HEADROW = C_EXPAND + 64
C_DIAG = C_HEADROW + 64
C_PAIR = C_DIAG + TS
C_HEAD = C_PAIR + 4
CONSTS = C_HEAD + 8
B_SPARSE, B_CAUSAL = 4, 12
BIASES = 13
MERGED_PARTS = (Z_TILES + GATE_TILES) * T + 2 * 2048 + 512
ARENA_FREE = P * T - 4 * D
ROUTED = 96
SMALL = 1736
SB_FIRST, SB_SECOND, SBIAS = 2 * KEYS, 2 * KEYS + 1, 2 * KEYS + 2
P_LN1G, P_LN1B, P_LN2G, P_LN2B, P_SUBLN, P_LAM, PARAMS = 0, 8, 16, 24, 32, 33, 37

SCORE_UNITS = [(0, 0, 0, 4), (0, 1, 0, 4), (1, 0, 0, 2), (1, 0, 2, 2), (1, 1, 0, 2), (1, 1, 2, 2)]
PT_TILES = [(0, 0), (1, 0), (1, 1)]

UNIT_ORDER = (["wi"] + [f"idx{u}" for u in range(6)] + ["v_diff0", "v_diff1", "v_sparse0", "v_sparse1"]
              + [f"diff{u}" for u in range(6)] + ["isum"] + [f"sparse{u}" for u in range(6)]
              + [f"diffT{u}" for u in range(3)] + ["diff_o0", "diff_o1"]
              + [f"sparseT{u}" for u in range(6)] + ["sparse_o0", "sparse_o1"]
              + ["sampT", "rms0", "rms1", "samp_diff", "samp_sparse", "samp_o", "rms2"])
UNIT = {name: n for n, name in enumerate(UNIT_ORDER)}
ROT, ROT_AT = 3, 5
LN_BANKS = [(6, 7), (0, 1)]
RMS = 4 * T


def build_program(nc, x_t, weights, experts_u, experts_v, k_cache, v_cache,
                  page_table, sub_keys, params, consts, alibi, sample_bias, kv_out, y_out):
    with ExitStack() as ctx:
        map_at = {"next": 0}
        base = -(-nc.sbuf_base // 32) * 32

        def region(name, words, dt=F32, parts=P):
            map_at[name] = map_at["next"]
            map_at["next"] += -(-words // 8) * 8
            return nc.alloc_sbuf_tensor_at(name, [parts, words], dt, offset=base + 4 * map_at[name])

        def rounded(name, over, at, words):
            return nc.alloc_sbuf_tensor_at(name, [P, words], F32R, offset=base + 4 * (map_at[over] + at))

        names = """consts_loaded params_loaded alibi_loaded table_loaded subkeys_loaded gate_hi_made gate_lo_made
            sparse_hi_made sparse_lo_made diff_hi_made diff_lo_made diff_normed up_hi_made up_lo_made
            merged_hi_made merged_lo_made x_hi_made x_lo_made z_hi_made z_lo_made tiles_done z_even_free
            z_odd_free kv_stored y_stored unit_filled qpad_zero qpad_ready lam_products lam_ready
            pool_chain dve_chain relu_sample sel_prompt sel_sample bias_masked k_ready k_used sample_scored
            diff_max diff_exp diff_attn sparse_max sparse_exp sparse_attn samp_max samp_exp samp_attn
            pad_zero pad_filled out_sample_ready rms_square rms_recip rms_root up_b_filled up_b_free
            up_a_free merged out_free ln_stat ln_centred ln_square ln_recip ln_root ln_scaled ln_even
            ln_odd q_evac score_filled score_free wq_hi_made wq_lo_made h_hi_made h_lo_made u_hi_made
            u_hi_used u_lo_made u_done gelu_done route_ready route_exp gates_normed route_filled
            route_copied tok_ready rows_bare rows_ready rows_weighted g_filled g_free g_applied h_restored
            v_hi_made v_hi_used v_lo_made cells_hi_made cells_split v_done v_filled acc_ready chunks_summed""".split()
        S = {n: ctx.enter_context(nc.semaphore(n)) for n in names}
        x_loaded = [ctx.enter_context(nc.semaphore(f"x_loaded{n}")) for n in range(2)]
        w_loaded = [ctx.enter_context(nc.semaphore(f"w_loaded{s}")) for s in range(RING)]
        k_loaded = [ctx.enter_context(nc.semaphore(f"k_loaded{s}")) for s in range(2)]
        vc_loaded = [ctx.enter_context(nc.semaphore(f"vc_loaded{s}")) for s in range(TS)]
        drained = [ctx.enter_context(nc.semaphore(f"drained{s}")) for s in range(ROT)]

        ring = region("ring", RING * D)
        xt = region("xt", DC * T)
        ht = region("ht", DC * T)
        cst = region("cst", CONSTS)
        par = region("par", PARAMS)
        table = region("table", PAGES * TS, I32, 1)
        sbias = region("sbias", SBIAS)
        arena = region("arena", P * T)
        work = region("work", 8192)
        small = region("small", SMALL)

        x_hi = rounded("x_hi", "ht", 0, DC * T)
        x_lo = rounded("x_lo", "work", 0, DC * T)
        z_hi = rounded("z_hi", "work", 2112, 2 * D)
        z_lo = rounded("z_lo", "work", 4160, 2 * D)
        wq_hi = rounded("wq_hi", "arena", ARENA_FREE, 2 * D)
        wq_lo = rounded("wq_lo", "arena", ARENA_FREE + 2 * D, 2 * D)
        up_hi = rounded("up_hi", "ht", 0, 2 * D)
        up_lo = rounded("up_lo", "work", 3072, 2 * D)
        sparse_hi = rounded("sparse_hi", "arena", VA * T, 4 * T)
        sparse_lo = rounded("sparse_lo", "arena", VS * T, 4 * T)
        diff_hi = rounded("diff_hi", "arena", P * T - 8 * T, 4 * T)
        diff_lo = rounded("diff_lo", "arena", P * T - 4 * T, 4 * T)
        merged_hi = rounded("merged_hi", "arena", MERGED_PARTS, DC * T)
        merged_lo = rounded("merged_lo", "arena", MERGED_PARTS + DC * T, DC * T)
        h_hi = rounded("h_hi", "ht", 0, DC * T)
        h_lo = rounded("h_lo", "work", 0, DC * T)
        w_hi = rounded("w_hi", "xt", 0, 2 * D)
        w_lo = rounded("w_lo", "work", 3648, 2 * D)
        cells_hi = rounded("cells_hi", "work", 6144, 2 * T)
        cells_lo = rounded("cells_lo", "work", 6144 + 2 * T, 2 * T)

        class Carve:
            def __init__(self, of):
                self.of, self.at = of, 0

            def __call__(self, words):
                self.at += words
                return self.of[:, self.at - words:self.at]

        a = Carve(arena)
        z = a(Z_TILES * T).rearrange("p (n t) -> p n t", t=T)
        gate = a(GATE_TILES * T).rearrange("p (n t) -> p n t", t=T)
        qpad_flat = a(2 * 2048 + 512)
        qpad = {"diff": qpad_flat[:, 0:2048].rearrange("p (j b n) -> p j b n", j=4, b=TS),
                "sparse": qpad_flat[:, 2048:4096].rearrange("p (j b n) -> p j b n", j=4, b=TS),
                "idx": qpad_flat[:, 4096:4608].rearrange("p (b n) -> p b n", b=TS)}
        kspace_at = a.at
        assert kspace_at == MERGED_PARTS
        kbuf = [a(9 * KEYS).rearrange("p (j k) -> p j k", j=9) for _ in range(2)]
        vspace = [a(2 * PAGES * 512) for _ in range(2)]
        bias = a(BIASES * 256).rearrange("p (n k) -> p n k", n=BIASES)
        s_diff = a(8 * 384)
        kspace = arena[:, kspace_at:kspace_at + 2 * (8 * KEYS + KEYS)]
        bias_words = bias.rearrange("p n k -> p (n k)")
        qs_words = z[:, QS:QS + 4, :].rearrange("p n t -> p (n t)")
        halves = [(v[:, 0:1024], v[:, 1024:2048]) for v in
                  vspace + [qpad_flat[:, 0:2048], qpad_flat[:, 2048:4096], kspace[:, 0:2048], kspace[:, 2048:4096],
                            bias_words[:, 0:2048]]] + [(qs_words[:, 0:1024], bias_words[:, 2048:3072])]
        vbuf = [{"diff": d.rearrange("p (g e) -> p g e", g=PAGES), "sparse": e.rearrange("p (g e) -> p g e", g=PAGES)}
                for d, e in halves]
        gelu_all = arena[:, :].rearrange("p (b t) -> p b t", t=T)
        o_diff, o_sparse = z[:, QI:QI + 4, :], z[:, QA:QA + 4, :]
        merged = z[:, KA:KA + DC, :]

        w = Carve(work)
        s_sparse = w(8 * 384)
        pt = w(8 * 3 * P).rearrange("p (n q) -> p n q", q=P)
        samp_pad = s_sparse[:, 0:2048].rearrange("p (n g c) -> p n g c", n=2, g=PAGES)
        samp_rows = s_sparse[:, 2048:3072].rearrange("p (n e) -> p n e", n=2)
        v_tok = {k: w(2 * 512).rearrange("p (g e) -> p g e", g=2) for k in ("diff", "sparse")}
        pre = work[:, 0:DC * T].rearrange("p (c t) -> p c t", c=DC)
        squares = work[:, 8 * 384:8 * 384 + DC * T].rearrange("p (c t) -> p c t", c=DC)
        y_t = pre
        subk = work[:, 6144:8192].rearrange("p (n k) -> p n k", n=HC)
        route_val = work[:, 2112:2880].rearrange("p (g n k) -> p g n k", g=3, n=HC)
        route_idx = work[:, 2880:3648].bitcast(U32).rearrange("p (g n k) -> p g n k", g=3, n=HC)
        route_idxf = work[:, 2880:3648].rearrange("p (g n k) -> p g n k", g=3, n=HC)
        cand = onehot = work[:, 6144:8192]
        rest = [sbias[:, 256 * n:256 * (n + 1)] for n in range(2)]
        p1 = work[:, 6144:7168].rearrange("p (s k) -> p s k", s=8)
        p2 = work[:, 7168:8192].rearrange("p (s k) -> p s k", s=8)

        c = Carve(small)
        mx = c(32)
        sums = c(32)
        recip = c(32)
        lam = c(4)
        neglam = c(1)
        head_w = c(2 * 8 + 8)
        wsel = c(8)
        samp_small = c(8)
        top8 = c(3 * 8)
        phase = c.at
        iscore = [c(P), c(256), c(KEYS)]
        s_samp = {"diff": c(KEYS), "sparse": c(KEYS)}
        relu_samp = s_samp["diff"]
        new_diag = [iscore[1][:, 0:64], iscore[1][:, 64:128]]
        att = c(96)
        new_part = c(64)
        assert c.at <= SMALL, c.at
        c.at = phase
        ln_mean, ln_root, ln_sum = c(T), c(T), c(T)
        c.at = phase
        up_tmp = [c(T), c(T)]
        c.at = phase
        q_sb = [c(T), c(T)]
        rest128 = [c(P) for _ in range(3)]
        c.at = phase
        gtmp = c(8 * P).rearrange("p (q n) -> p q n", q=2)
        c.at = phase
        top_val = c(3 * P).rearrange("p (g n) -> p g n", g=3)
        top_pos = c(P).bitcast(U32)
        pos_part = c(P).bitcast(U32)
        pos_f = c(P)
        first_id = c(3 * P).rearrange("p (g n) -> p g n", g=3)
        second_id = c(3 * P).rearrange("p (g n) -> p g n", g=3)
        denom = c(24).rearrange("p (g n) -> p g n", g=3)
        assert c.at <= SMALL, c.at
        slots = work[:, 2112:2112 + 3 * T].rearrange("p (n t) -> p n t", n=3)
        tok = work[:, 2112 + 3 * T:2112 + 3 * T + 48].rearrange("p (h n t) -> p h n t", h=2, n=3)

        h = xt[:, :].rearrange("p (c t) -> p c t", c=DC)
        acc = ring[:, 0:DC * T].rearrange("p (c t) -> p c t", c=DC)
        ident = cst[:, C_IDENT:C_IDENT + P]
        ones = cst[:, C_ONES:C_ONES + P]
        iota = cst[:, C_IOTA:C_IOTA + P]
        iota16 = cst[:, C_IOTA16:C_IOTA16 + TOP]

        psum = ctx.enter_context(nc.psum_tensor("psum", [P, 8, 512], F32))

        def bank(name):
            return psum[:, ROT_AT + UNIT[name] % ROT, :]

        def s_view(buf, qt):
            return (buf[:, 0:1024] if qt == 0 else buf[:, 1024:3072]).rearrange("p (m k) -> p m k", m=8)

        def of_unit(heads, unit):
            _, i, j0, n = unit
            return heads.rearrange("p (j i) k -> p i j k", i=2)[:, i, j0:j0 + n, :]

        def await_unit(eng, name):
            eng.wait_ge(S["unit_filled"], UNIT[name] + 1)

        def drain_unit(ins, name):
            ins.then_inc(drained[UNIT[name] % ROT], 1)

        def await_drained(eng, name):
            eng.wait_ge(drained[UNIT[name] % ROT], UNIT[name] // ROT + 1)

        class Chain:
            def __init__(self, eng, sem):
                self.eng, self.sem, self.n = eng, sem, 0

            def put(self, ins):
                self.n += 1
                ins.then_inc(self.sem, 1)

            def settle(self):
                self.eng.wait_ge(self.sem, self.n)

            def __call__(self, ins):
                self.put(ins)
                self.settle()

        uses = [len(range(s, TILES, RING)) for s in range(RING)]
        U_SLOT = TILES % RING

        def expert_tile(i, k):
            s = (U_SLOT + k) % RING
            return ring[:, s * D:(s + 1) * D], w_loaded[s], 16 * (uses[s] + k // RING) + 16 + i * 16

        def halves_of(buf, k, n):
            return buf[:, (k % 2) * n:(k % 2 + 1) * n]

        def part(buf, k, n):
            return buf[:, k * n:(k + 1) * n]

        def token_cols(parts, t0, t1):
            return parts[:, 0:4 * T].rearrange("p (j t) -> p j t", j=4)[:, :, t0:t1]

        def gate_low_buf(n):
            return z_lo[:, 0:D] if n % 2 == 0 else wq_lo[:, D:2 * D]

        def ring_tile(t):
            return part(ring, t % RING, D), w_loaded[t % RING], 16 * (t // RING + 1)

        block = ctx.enter_context(nc.Block())

        @block.sync
        def _(sp):
            sp.dma_start(ring[:, 0:D], weights[0]).then_inc(w_loaded[0], 16)
            for n in range(2):
                sp.dma_start(xt[:, n * 4 * T:(n + 1) * 4 * T], x_t[:, n * 4:(n + 1) * 4, :]).then_inc(x_loaded[n], 16)
            for t in range(1, RING):
                sp.dma_start(ring[:, t * D:(t + 1) * D], weights[t]).then_inc(w_loaded[t], 16)

            def load_after(freed, count, slot, t):
                sp.wait_ge(S[freed], count)
                sp.dma_start(ring[:, slot * D:(slot + 1) * D], weights[t]).then_inc(w_loaded[slot], 16)

            with sp.Fori(1, Z_TILES // RING + 1) as i:
                for k in range(RING):
                    load_after("z_lo_made", i * RING + k - RING + 1, k, i * RING + k)
            for t in range((Z_TILES // RING + 1) * RING, UP_AT + RING):
                load_after("tiles_done", t - RING + 1, t % RING, t)
            with sp.Fori(0, 2 * DC // RING) as i:
                for k in range(RING):
                    load_after("up_lo_made", i * RING + k + 1, (UP_AT + k) % RING, UP_AT + RING + i * RING + k)
            with sp.Fori(0, HC // RING - 1) as i:
                for k in range(RING):
                    load_after("wq_lo_made", i * RING + k + 1, (WQ_AT + k) % RING, WQ_AT + RING + i * RING + k)

            for b in range(RING):
                s = (U_SLOT + b) % RING
                sp.wait_ge(S["wq_lo_made"], HC - RING + b + 1)
                sp.dma_start(ring[:, s * D:(s + 1) * D], experts_u[b]).then_inc(w_loaded[s], 16)
            with sp.Fori(1, NK // RING) as i:
                for k in range(RING):
                    s = (U_SLOT + k) % RING
                    sp.wait_ge(S["u_lo_made"], 2 + i * RING + k - RING + 1)
                    sp.dma_start(ring[:, s * D:(s + 1) * D], experts_u[i * RING + k]).then_inc(w_loaded[s], 16)
            for b in range(RING):
                s = (U_SLOT + b) % RING
                sp.wait_ge(S["u_lo_made"], 2 + NK - RING + b + 1)
                sp.dma_start(ring[:, s * D:(s + 1) * D], experts_v[b]).then_inc(w_loaded[s], 16)
            with sp.Fori(1, NK // RING) as i:
                for k in range(RING):
                    s = (U_SLOT + k) % RING
                    sp.wait_ge(S["v_lo_made"], 2 + i * RING + k - RING + 1)
                    sp.dma_start(ring[:, s * D:(s + 1) * D], experts_v[i * RING + k]).then_inc(w_loaded[s], 16)
            for k in range(0, DC, 2):
                sp.wait_ge(S["ln_even"], DC // 2 + k // 2 + 1)
                sp.wait_ge(S["ln_odd"], DC // 2 + k // 2 + 1)
                sp.dma_start(y_out[:, k:k + 2, :], y_t[:, k:k + 2, :]).then_inc(S["y_stored"], 16)
            sp.wait_ge(S["y_stored"], 16 * DC // 2)
            sp.wait_ge(S["kv_stored"], 16)

        @block.gpsimd
        def _(pool):
            chain = Chain(pool, S["pool_chain"])
            pool.dma_start(table[:, :], page_table).then_inc(S["table_loaded"], 16)
            pool.memset(qpad_flat, 0.0).then_inc(S["qpad_zero"], 1)
            pool.wait_ge(S["table_loaded"], 16)

            def page_of(b, g):
                return pool.value_load(table[0:1, b * PAGES + g:b * PAGES + g + 1], min_val=0,
                                       max_val=k_cache.shape[0] - 1)

            def load_keys(b):
                for g in range(PAGES):
                    page = page_of(b, g)
                    pool.dma_start(kbuf[b % 2][:, :, g * PAGE:(g + 1) * PAGE],
                                   k_cache[bass.ds(page, 1)].rearrange("o p j k -> p (o j) k")).then_inc(k_loaded[b % 2], 16)

            def load_values(b):
                for g in range(PAGES):
                    page = page_of(b, g)
                    diff, sparse = vbuf[b]["diff"][:, g, :], vbuf[b]["sparse"][:, g, :]
                    both = bass.AP(diff.tensor, diff.offset,
                                   [list(diff.ap[0]), [sparse.offset - diff.offset, 2], [1, 512]])
                    pool.dma_start(both, v_cache[bass.ds(page, 1)].rearrange("o p k e -> p (o k) e"))\
                        .then_inc(vc_loaded[b], 16)

            pool.wait_ge(S["tiles_done"], 4)
            load_keys(0)
            pool.wait_ge(S["tiles_done"], 8)
            pool.dma_start(bias, alibi).then_inc(S["alibi_loaded"], 16)
            pool.dma_start(sbias[0:64, :], sample_bias).then_inc(S["alibi_loaded"], 16)
            pool.wait_ge(S["tiles_done"], 16)
            load_keys(1)
            for b in range(2):
                pool.wait_ge(S["tiles_done"], 20 + 4 * b)
                load_values(b)
            pool.wait_ge(S["z_even_free"], 1 + Z_TILES // 2)
            pool.wait_ge(S["z_odd_free"], 1 + Z_TILES // 2)
            pool.dma_start(kv_out, z[:, KA:KI + 1, :]).then_inc(S["kv_stored"], 16)

            def new_key(b):
                buf = kbuf[b % 2]
                pool.wait_ge(k_loaded[b % 2], 32 * (b // 2 + 1))
                chain.put(pool.tensor_copy(buf[:, 0:8, PAST], z[:, KA:KA + 8, TP + b]))
                pool.tensor_copy(buf[:, 8, PAST:KEYS], z[:, KI, TP + b:TP + b + 1]).then_inc(S["k_ready"], 1)

            new_key(0)
            for b in range(TS - 2):
                new_key(b + 1)
                pool.wait_ge(S["k_used"], b + 1)
                load_keys(b + 2)
            new_key(TS - 1)
            pool.wait_ge(S["tiles_done"], Z_TILES + EARLY_GATES)
            for qt in range(2):
                pool.wait_ge(S["sel_prompt"], qt + 1)
                keys = P if qt == 0 else 2 * P
                pool.tensor_tensor(s_view(s_sparse, qt), bias[:, B_SPARSE:B_SPARSE + 8, 256 - keys:256],
                                   iscore[qt].unsqueeze(1).to_broadcast([P, 8, keys]), ALU.add)\
                    .then_inc(S["bias_masked"], 1)
            pool.wait_ge(S["sample_scored"], 1)
            for b in range(2, 6):
                load_values(b)
            pool.wait_ge(S["bias_masked"], 2)
            pool.wait_ge(S["diff_max"], 6)
            load_values(6)
            await_unit(pool, "sparse5")
            load_values(7)
            await_unit(pool, "sparseT5")
            pool.memset(s_sparse[:, 0:2048], 0.0).then_inc(S["pad_zero"], 1)
            await_unit(pool, "sparse_o1")
            pool.dma_start(subk, sub_keys).then_inc(S["subkeys_loaded"], 16)
            pool.sem_inc(S["merged"], 2)
            with pool.Fori(0, 2) as i:
                for k in range(4):
                    n = i * 4 + k
                    pool.wait_ge(S["up_a_free"], 2 + n + 1)
                    pool.wait_ge(S["table_loaded"], 16)
                    m = merged[:, bass.ds(n, 1), :].rearrange("p o t -> p (o t)")
                    pool.tensor_tensor(m, m, up_tmp[k % 2], ALU.add).then_inc(S["merged"], 1)
                    pool.wait_ge(S["merged_hi_made"], n + 1)
                    pool.wait_ge(S["table_loaded"], 16)
                    pool.tensor_tensor(merged_lo[:, bass.ds(n * T, T)], m, merged_hi[:, bass.ds(n * T, T)], ALU.subtract)\
                        .then_inc(S["merged_lo_made"], 1)
            def norm_scale(n, src):
                pool.wait_ge(S["ln_root"], n + 1)
                for k in range(0, DC, 2):
                    pool.tensor_tensor(src[:, k, :], src[:, k, :], ln_root, ALU.mult).then_inc(S["ln_scaled"], 1)

            def wq_low(i, k):
                raw, _, _ = ring_tile(WQ_AT + k)
                pool.wait_ge(S["wq_hi_made"], i * RING + k + 1)
                pool.tensor_tensor(halves_of(wq_lo, k, D), raw, halves_of(wq_hi, k, D), ALU.subtract)\
                    .then_inc(S["wq_lo_made"], 1)

            wq_low(0, 0)
            wq_low(0, 1)
            norm_scale(0, pre)
            with pool.Fori(0, HC // 4 - 1) as i:
                for k in range(4):
                    pool.wait_ge(S["tiles_done"], WQ_AT + i * 4 + k + 1)
                    wq_low(i, k + 2)
            for k in range(2):
                pool.wait_ge(S["tiles_done"], WQ_AT + HC - 4 + k + 1)
                wq_low(HC // 4 - 1, k + 2)
            pool.sem_inc(S["u_lo_made"], 2)
            with pool.Fori(0, NK // RING) as i:
                for k in range(RING):
                    raw, _, _ = expert_tile(i, k)
                    pool.wait_ge(S["u_hi_made"], i * RING + k + 1)
                    pool.wait_ge(S["u_done"], i * RING + k + 1)
                    pool.tensor_tensor(halves_of(w_lo, k, D), raw, halves_of(w_hi, k, D), ALU.subtract)\
                        .then_inc(S["u_lo_made"], 1)
            pool.wait_ge(S["u_done"], 2 + NK)
            pool.tensor_tensor(pre.rearrange("p c t -> p (c t)"), h_hi[:, :], h_lo[:, :], ALU.add)\
                .then_inc(S["h_restored"], 1)
            pool.wait_ge(S["gelu_done"], 4 + NK)
            pool.sem_inc(S["g_applied"], 2)
            with pool.Fori(0, T // 8) as i:
                for q in range(2):
                    pool.wait_ge(S["g_free"], 2 + i * 2 + q + 1)
                    pool.wait_ge(S["table_loaded"], 16)
                    cells = gelu_all[:, :, bass.ds(i * 8 + q * 4, 4)].rearrange("p b t -> p t b")
                    pool.tensor_tensor(cells, gtmp[:, q, :].rearrange("p (t b) -> p t b", t=4), cells, ALU.mult)\
                        .then_inc(S["g_applied"], 1)
            norm_scale(1, acc)

        @block.scalar
        def _(act):
            act.dma_start(cst[:, :], consts).then_inc(S["consts_loaded"], 16)
            act.dma_start(par[:, :], params).then_inc(S["params_loaded"], 16)
            act.sem_inc(S["z_even_free"], 1)
            act.wait_ge(S["consts_loaded"], 16)

            def evac_z(i, tile):
                act.wait_ge(S["tiles_done"], tile + 1)
                act.wait_ge(S["consts_loaded"], 16)
                act.activation(z[:, bass.ds(tile, 1), :].rearrange("p o t -> p (o t)"), psum[:, 0, 0:T], ACT.Copy)\
                    .then_inc(S["z_even_free"], 1)


            def z_high(i, k):
                raw, sem, count = ring_tile(k)
                act.wait_ge(sem, count + i * 16)
                act.activation(halves_of(z_hi, k, D), raw, ACT.Copy).then_inc(S["z_hi_made"], 1)

            z_high(0, 0)
            for k in range(DC):
                act.wait_ge(x_loaded[k // 4], 16)
                act.activation(part(x_hi, k, T), part(xt, k, T), ACT.Copy).then_inc(S["x_hi_made"], 1)
            z_high(0, 1)
            with act.Fori(0, Z_TILES // RING) as i:
                for k in range(RING):
                    act.wait_ge(S["tiles_done"], i * RING + k + 1)
                    z_high(i, k + 2)
                    if k % 2 == 0:
                        evac_z(i, i * RING + k)
            evac_z(0, Z_TILES - 2)
            await_unit(act, "wi")
            act.activation(lam[:, 2:4], bank("wi")[:, 128:130], ACT.Exp).then_inc(S["lam_ready"], 1)
            for u, unit in enumerate(SCORE_UNITS):
                await_unit(act, f"idx{u}")
                qt, keys = unit[0], P * (unit[0] + 1)
                drain_unit(act.activation(of_unit(s_view(s_sparse, qt), unit),
                                          bank(f"idx{u}").rearrange("p (m k) -> p m k", k=keys),
                                          ACT.Relu, scale=SCALE), f"idx{u}")
            for kind in ("diff", "sparse"):
                for kt in range(2):
                    await_unit(act, f"v_{kind}{kt}")
                    drain_unit(act.activation(v_tok[kind][:, kt, :], bank(f"v_{kind}{kt}"), ACT.Copy), f"v_{kind}{kt}")
            def prompt_exp(kind, buf, col):
                for u, (qt, i, j0, n) in enumerate(SCORE_UNITS):
                    act.wait_ge(S[f"{kind}_max"], u + 1)
                    for m in range(2 * j0 + i, 2 * (j0 + n) + i, 2):
                        at = col + qt * 8 + m
                        row = s_view(buf, qt)[:, m, :]
                        act.activation(row, row, ACT.Exp, bias=mx[:, at:at + 1], accum_out=sums[:, at:at + 1])\
                            .then_inc(S[f"{kind}_exp"], 1)

            def sample_exp(n, kind):
                act.wait_ge(S["samp_max"], n + 1)
                act.activation(s_samp[kind][0:64, :], s_samp[kind][0:64, :], ACT.Exp,
                               bias=samp_small[0:64, n:n + 1], accum_out=samp_small[0:64, 2 + n:3 + n])\
                    .then_inc(S["samp_exp"], 1)

            def evac_gate(n):
                act.wait_ge(S["tiles_done"], Z_TILES + n + 1)
                act.activation(gate[:, n, :], psum[:, n % 2, 0:T], ACT.Sigmoid)\
                    .then_inc(S[("z_even_free", "z_odd_free")[n % 2]], 1)

            def evac_pt(kind, u):
                name = f"{kind}T{u}"
                await_unit(act, name)
                drain_unit(act.activation(pt[:, 4 * u:4 * u + 4, :].rearrange("p n q -> p (n q)"), bank(name), ACT.Copy), name)

            def evac_o(kind, u, dst):
                name = f"{kind}_o{u}"
                await_unit(act, name)
                drain_unit(act.activation(dst[:, 2 * u:2 * u + 2, 0:TP], bank(name).rearrange("p (j q) -> p j q", j=2),
                                          ACT.Copy), name)

            def gate_high(n):
                raw, sem, count = ring_tile(Z_TILES + n)
                act.wait_ge(sem, count)
                if n >= 2:
                    act.wait_ge(S["tiles_done"], Z_TILES + n - 1)
                act.activation(halves_of(z_hi, n, D), raw, ACT.Copy).then_inc(S["gate_hi_made"], 1)

            prompt_exp("diff", s_diff, 0)
            gate_high(0)
            gate_high(1)
            for n in range(EARLY_GATES):
                evac_gate(n)
                if n + 2 < EARLY_GATES:
                    gate_high(n + 2)
            act.wait_ge(S["sample_scored"], 1)
            act.activation(relu_samp[0:64, :], psum[0:64, 4, 0:KEYS], ACT.Relu, scale=SCALE)\
                .then_inc(S["relu_sample"], 1)
            prompt_exp("sparse", s_sparse, 16)
            evac_gate(EARLY_GATES)
            evac_gate(EARLY_GATES + 1)
            for u in range(3):
                evac_pt("diff", u)
            for u in range(2):
                evac_o("diff", u, o_diff)
            await_drained(act, "diff_o1")
            act.activation(s_diff[:, 0:4 * TP].rearrange("p (j t) -> p j t", j=4), o_diff[:, :, 0:TP], ACT.Square)\
                .then_inc(S["rms_square"], 1)
            evac_gate(EARLY_GATES + 2)
            evac_gate(EARLY_GATES + 3)
            for u in range(6):
                evac_pt("sparse", u)
            sample_exp(0, "diff")
            sample_exp(1, "sparse")
            for u in range(2):
                evac_o("sparse", u, o_sparse)

            def up_high(i, m):
                raw, sem, count = ring_tile(UP_AT + m)
                act.wait_ge(sem, count + i * 16)
                act.activation(halves_of(up_hi, m, D), raw, ACT.Copy).then_inc(S["up_hi_made"], 1)

            up_high(0, 0)
            up_high(0, 1)
            act.wait_ge(S["kv_stored"], 16)
            await_drained(act, "sparse_o1")
            act.activation(token_cols(sparse_hi, 0, TP), o_sparse[:, :, 0:TP], ACT.Copy).then_inc(S["sparse_hi_made"], 1)
            act.wait_ge(S["rms_recip"], 1)
            act.activation(s_diff[:, RMS:RMS + 4 * TP], s_diff[:, RMS:RMS + 4 * TP], ACT.Sqrt).then_inc(S["rms_root"], 1)
            act.wait_ge(S["diff_normed"], 1)
            act.activation(token_cols(diff_hi, 0, TP), o_diff[:, :, 0:TP], ACT.Copy).then_inc(S["diff_hi_made"], 1)
            act.wait_ge(S["out_sample_ready"], 1)
            act.activation(s_diff[:, 4 * TP:4 * T].rearrange("p (j t) -> p j t", j=4), o_diff[:, :, TP:T], ACT.Square)\
                .then_inc(S["rms_square"], 1)
            act.activation(token_cols(sparse_hi, TP, T), o_sparse[:, :, TP:T], ACT.Copy).then_inc(S["sparse_hi_made"], 1)
            act.wait_ge(S["rms_recip"], 2)
            act.activation(s_diff[:, RMS + 4 * TP:RMS + 4 * T], s_diff[:, RMS + 4 * TP:RMS + 4 * T], ACT.Sqrt)\
                .then_inc(S["rms_root"], 1)
            act.wait_ge(S["out_sample_ready"], 2)
            act.activation(token_cols(diff_hi, TP, T), o_diff[:, :, TP:T], ACT.Copy).then_inc(S["diff_hi_made"], 1)
            with act.Fori(0, 2) as i:
                for k in range(4):
                    act.wait_ge(S["tiles_done"], UP_AT + i * 4 + k + 1)
                    up_high(i, k + 2)
                    act.wait_ge(S["merged"], 2 + i * 4 + k + 1)
                    act.wait_ge(S["consts_loaded"], 16)
                    act.activation(merged_hi[:, bass.ds((i * 4 + k) * T, T)],
                                   merged[:, bass.ds(i * 4 + k, 1), :].rearrange("p o t -> p (o t)"), ACT.Copy)\
                        .then_inc(S["merged_hi_made"], 1)
            for m in range(DC + 2, 2 * DC):
                act.wait_ge(S["tiles_done"], UP_AT + m - 1)
                up_high(0, m)

            def norm(n, src, dst, g, b):
                for k in range(DC):
                    act.wait_ge(S["ln_centred"], n * DC + k + 1)
                    act.activation(squares[:, k, :], src[:, k, :], ACT.Square).then_inc(S["ln_square"], 1)
                act.wait_ge(S["ln_recip"], n + 1)
                act.activation(ln_root, ln_root, ACT.Sqrt).then_inc(S["ln_root"], 1)
                for k in range(0, DC, 2):
                    act.wait_ge(S["ln_scaled"], n * DC // 2 + k // 2 + 1)
                    act.activation(dst[:, k, :], src[:, k, :], ACT.Identity, bias=par[:, b + k:b + k + 1],
                                   scale=par[:, g + k:g + k + 1]).then_inc(S["ln_even"], 1)
                    if n == 0:
                        act.wait_ge(S["ln_even"], k // 2 + 1)
                        act.wait_ge(S["ln_odd"], k // 2 + 1)
                        act.activation(h_hi[:, k * T:(k + 2) * T], xt[:, k * T:(k + 2) * T], ACT.Copy)\
                            .then_inc(S["h_hi_made"], 1)

            def wq_high(i, k):
                raw, sem, count = ring_tile(WQ_AT + k)
                act.wait_ge(sem, count + i * 16)
                act.activation(halves_of(wq_hi, k, D), raw, ACT.Copy).then_inc(S["wq_hi_made"], 1)

            act.wait_ge(S["out_sample_ready"], 2)
            act.wait_ge(S["merged"], 2 + DC)
            wq_high(0, 0)
            wq_high(0, 1)
            act.wait_ge(S["params_loaded"], 16)
            norm(0, pre, h, P_LN1G, P_LN1B)
            act.sem_inc(S["q_evac"], 2)

            def evac_q(i, k):
                act.wait_ge(S["score_filled"], i * 4 + k + 1)
                act.wait_ge(S["tiles_done"], WQ_AT + i * 4 + k + 1)
                act.activation(q_sb[k % 2], psum[:, k % 2, 0:T], ACT.Copy).then_inc(S["q_evac"], 1)

            with act.Fori(0, HC // 4 - 1) as i:
                for k in range(4):
                    evac_q(i, k)
                    wq_high(i, k + 2)
            for k in range(4):
                evac_q(HC // 4 - 1, k)
                if k < 2:
                    wq_high(HC // 4 - 1, k + 2)

            def high_part(i, k):
                raw, sem, count = expert_tile(i, k)
                act.wait_ge(sem, count)
                act.wait_ge(S["u_hi_used"], i * RING + k + 1)
                act.wait_ge(S["u_lo_made"], i * RING + k + 1)
                act.activation(halves_of(w_hi, k, D), raw, ACT.Copy).then_inc(S["u_hi_made"], 1)

            def gelu(i, k):
                act.wait_ge(S["u_done"], 2 + i * RING + k + 1)
                act.wait_ge(S["consts_loaded"], 16)
                act.activation(gelu_all[:, bass.ds(i * RING + k, 1), :].rearrange("p o t -> p (o t)"),
                               psum[:, 4 + k, 0:T], ACT.Gelu).then_inc(S["gelu_done"], 1)

            act.wait_ge(S["h_lo_made"], DC // 2)
            high_part(0, 0)
            high_part(0, 1)
            act.sem_inc(S["gelu_done"], 4)
            with act.Fori(0, ROUTED // RING) as i:
                for k in range(RING):
                    high_part(i, k + 2)
                    gelu(i, k)
            act.wait_ge(S["route_ready"], 1)
            for n, (_, rows) in enumerate(TOKEN_TILES):
                act.activation(top_val[0:rows, n, :], top_val[0:rows, n, :], ACT.Exp).then_inc(S["route_exp"], 1)
            with act.Fori(ROUTED // RING, NK // RING - 1) as i:
                for k in range(RING):
                    high_part(i, k + 2)
                    gelu(i, k)
            for k in range(RING):
                if k < RING - 2:
                    high_part(NK // RING - 1, k + 2)
                gelu(NK // RING - 1, k)
            act.sem_inc(S["g_free"], 2)

            def weigh(n, q, side):
                act.wait_ge(S["rows_bare"], n * 2 + q + 1)
                for k in range(4 * q, 4 * q + 2):
                    act.activation(p2[:, k, :], p2[:, k, :], ACT.Copy, scale=tok[:, side, 2, k:k + 1])\
                        .then_inc(S["rows_weighted"], 1)

            def evac_g(n, q):
                act.wait_ge(S["g_applied"], n * 2 + q + 1)
                act.wait_ge(S["g_filled"], 2 + n * 2 + q + 1)
                act.activation(gtmp[:, q, :], psum[:, 4 + q, :], ACT.Copy).then_inc(S["g_free"], 1)

            weigh(0, 0, 0)
            with act.Fori(0, T // 16) as i:
                for side in range(2):
                    n = i * 2 + side
                    weigh(n, 1, side)
                    evac_g(n, 0)
                    weigh(n + 1, 0, 1 - side)
                    evac_g(n, 1)
            weigh(T // 8 - 1, 1, 0)
            for q in range(2):
                evac_g(T // 8 - 1, q)
            with act.Fori(0, NK // RING) as i:
                for k in range(RING):
                    raw, sem, count = expert_tile(i, k)
                    act.wait_ge(sem, count + 16 * NK // RING)
                    act.wait_ge(S["v_hi_used"], i * RING + k + 1)
                    act.wait_ge(S["v_lo_made"], i * RING + k + 1)
                    act.activation(halves_of(w_hi, k, D), raw, ACT.Copy).then_inc(S["v_hi_made"], 1)
            norm(1, acc, y_t, P_LN2G, P_LN2B)

        @block.vector
        def _(dve):
            chain = Chain(dve, S["dve_chain"])
            dve.sem_inc(S["z_odd_free"], 1)
            dve.wait_ge(S["params_loaded"], 16)
            dve.tensor_tensor(lam[0:64, 0:2], par[0:64, P_LAM:P_LAM + 2], par[0:64, P_LAM + 2:P_LAM + 4], ALU.mult)\
                .then_inc(S["lam_products"], 1)
            for k in range(DC):
                dve.wait_ge(x_loaded[k // 4], 16)
                dve.wait_ge(S["x_hi_made"], k + 1)
                dve.tensor_tensor(part(x_lo, k, T), part(xt, k, T), part(x_hi, k, T), ALU.subtract)\
                    .then_inc(S["x_lo_made"], 1)

            def z_low(i, k):
                raw, _, _ = ring_tile(k)
                dve.wait_ge(S["z_hi_made"], i * RING + k + 1)
                dve.tensor_tensor(halves_of(z_lo, k, D), raw, halves_of(z_hi, k, D), ALU.subtract)\
                    .then_inc(S["z_lo_made"], 1)

            def evac_z(tile):
                dve.wait_ge(S["tiles_done"], tile + 1)
                dve.wait_ge(S["params_loaded"], 16)
                dve.tensor_copy(z[:, bass.ds(tile, 1), :].rearrange("p o t -> p (o t)"), psum[:, 1, 0:T])\
                    .then_inc(S["z_odd_free"], 1)

            z_low(0, 0)
            z_low(0, 1)
            with dve.Fori(0, Z_TILES // RING) as i:
                for k in range(RING):
                    dve.wait_ge(S["tiles_done"], i * RING + k + 1)
                    z_low(i, k + 2)
                    if k % 2:
                        evac_z(i * RING + k)
            evac_z(Z_TILES - 1)

            dve.wait_ge(S["qpad_zero"], 1)
            dve.wait_ge(S["z_even_free"], 1 + Z_TILES // 2)
            dve.wait_ge(S["z_odd_free"], 1 + Z_TILES // 2)
            for kind, at, tile, steps in (("diff", 0, QA, (514, 72)), ("sparse", 2048, QS, (514, 72)),
                                          ("idx", 4096, QI, (2, 72))):
                for i in range(2):
                    half = slice(i * HD, (i + 1) * HD)
                    spread = qpad_flat[half, at + i:at + i + 1]
                    dst = bass.AP(spread.tensor, spread.offset,
                                  [list(spread.ap[0]), [steps[0], 4], [steps[1], TS]])
                    dve.tensor_copy(dst, z[half, tile:tile + 4, TP:T]).then_inc(S["qpad_ready"], 1)

            await_unit(dve, "wi")
            dve.wait_ge(S["lam_ready"], 1)
            chain.put(dve.tensor_scalar(head_w[:, 0:16], bank("wi")[:, 0:16], SUBHEADS ** -0.5, None, ALU.mult))
            chain(dve.tensor_scalar(head_w[0:64, 16:24], bank("wi")[0:64, 16:24], SUBHEADS ** -0.5, None, ALU.mult))
            drain_unit(dve.tensor_tensor(wsel[0:64, :], head_w[0:64, 16:24], cst[0:64, C_DIAG:C_DIAG + TS],
                                         ALU.mult), "wi")
            chain(dve.tensor_tensor(neglam, lam[:, 3:4], lam[:, 2:3], ALU.subtract))
            chain(dve.tensor_scalar(neglam, neglam, -LAM_INIT, None, ALU.add))

            dve.wait_ge(S["alibi_loaded"], 32)
            for qt in range(2):
                keys = P * (qt + 1)
                for m in range(SUBHEADS):
                    u = next(u for u, (g, i, j0, n) in enumerate(SCORE_UNITS)
                             if g == qt and i == m % 2 and j0 <= m // 2 < j0 + n)
                    await_drained(dve, f"idx{u}")
                    r = s_view(s_sparse, qt)[:, m, :]
                    weight = head_w[:, qt * 8 + m:qt * 8 + m + 1]
                    if m == 0:
                        chain(dve.tensor_scalar(iscore[qt], r, weight, None, ALU.mult))
                    else:
                        chain(dve.scalar_tensor_tensor(iscore[qt], r, weight, iscore[qt], ALU.mult, ALU.add))
                chain(dve.tensor_tensor(iscore[qt], iscore[qt], bias[:, B_CAUSAL, 256 - keys:256], ALU.add))

            def score(kind, buf, col, u):
                qt, i, j0, n = unit = SCORE_UNITS[u]
                keys = P * (qt + 1)
                name = f"{kind}{u}"
                await_unit(dve, name)
                src = bank(name).rearrange("p (m k) -> p m k", k=keys)
                dst = of_unit(s_view(buf, qt), unit)
                if kind == "diff":
                    added = bias[:, j0:j0 + n, 256 - keys:256]
                else:
                    dve.wait_ge(S["bias_masked"], qt + 1)
                    added = dst
                drain_unit(dve.scalar_tensor_tensor(dst, src, SCALE, added, ALU.mult, ALU.add), name)
                await_drained(dve, name)
                rows_max = mx[:, col + qt * 8:col + qt * 8 + 8].rearrange("p (j i) -> p i j", i=2)[:, i, j0:j0 + n]
                dve.tensor_reduce(rows_max, dst, AX.X, ALU.max, negate=True)\
                    .then_inc(S[f"{kind}_max"], 1)

            for u in range(6):
                score("diff", s_diff, 0, u)

            def select(which, sem, meanwhile=None):
                for turn in range(NSEL // 8):
                    if meanwhile is not None and turn == NSEL // 16:
                        meanwhile()
                    for n, r in which:
                        chain.put(dve.max(top8[0:r, 8 * n:8 * n + 8], iscore[n][0:r, :]))
                    chain.settle()
                    for n, r in which:
                        chain.put(dve.match_replace(iscore[n][0:r, :], top8[0:r, 8 * n:8 * n + 8],
                                                    iscore[n][0:r, :], TAKEN))
                    chain.settle()
                for n, r in which:
                    dve.tensor_scalar(iscore[n][0:r, :], iscore[n][0:r, :], TAKEN * 0.97, NEG,
                                      ALU.is_gt, ALU.mult).then_inc(sem, 1)

            def gate_low(n):
                raw, _, _ = ring_tile(Z_TILES + n)
                dve.wait_ge(S["gate_hi_made"], n + 1)
                if n >= 2:
                    dve.wait_ge(S["tiles_done"], Z_TILES + n - 1)
                dve.tensor_tensor(gate_low_buf(n), raw, halves_of(z_hi, n, D), ALU.subtract)\
                    .then_inc(S["gate_lo_made"], 1)

            dve.tensor_tensor(x_lo[:, :], xt[:, :], x_hi[:, :], ALU.subtract).then_inc(S["x_lo_made"], 1)
            gate_low(0)
            gate_low(1)
            select([(0, P), (1, P)], S["sel_prompt"], meanwhile=lambda: gate_low(2))
            gate_low(3)

            def reciprocals(kind, col):
                dve.wait_ge(S[f"{kind}_exp"], 16)
                chain(dve.reciprocal(recip[:, col:col + 16], sums[:, col:col + 16]))

            reciprocals("diff", 0)
            odd = recip[:, 0:16].rearrange("p (m i) -> p m i", i=2)[:, :, 1]
            chain(dve.tensor_scalar(odd, odd, neglam, None, ALU.mult))
            for qt in range(2):
                s = s_view(s_diff, qt)
                keys = P * (qt + 1)
                chain(dve.tensor_tensor(s, s, recip[:, qt * 8:qt * 8 + 8].unsqueeze(2).to_broadcast([P, 8, keys]), ALU.mult))
                pairs = s.rearrange("p (j i) k -> p j i k", i=2)
                dve.tensor_tensor(pairs[:, :, 0, :], pairs[:, :, 0, :], pairs[:, :, 1, :], ALU.add)\
                    .then_inc(S["diff_attn"], 1)
                gate_low(4 + qt)
            for n in range(6, EARLY_GATES):
                gate_low(n)
            await_unit(dve, "isum")
            drain_unit(dve.tensor_copy(iscore[2][0:TS, :], bank("isum")[0:TS, 0:KEYS]), "isum")
            for u in range(6):
                score("sparse", s_sparse, 16, u)
            await_drained(dve, "isum")
            select([(2, TS)], S["sel_sample"])
            reciprocals("sparse", 16)
            for qt in range(2):
                s = s_view(s_sparse, qt)
                dve.tensor_tensor(s, s, recip[:, 16 + qt * 8:24 + qt * 8].unsqueeze(2)
                                  .to_broadcast([P, 8, P * (qt + 1)]), ALU.mult).then_inc(S["sparse_attn"], 1)
            for n, kind in enumerate(("diff", "sparse")):
                dve.wait_ge(S["sample_scored"], 1 + n)
                chain(dve.scalar_tensor_tensor(s_samp[kind][0:64, :], psum[0:64, 2 + n, 0:KEYS], SCALE,
                                               sbias[0:64, n * KEYS:(n + 1) * KEYS], ALU.mult, ALU.add))
                dve.tensor_reduce(samp_small[0:64, n:n + 1], s_samp[kind][0:64, :], AX.X, ALU.max, negate=True)\
                    .then_inc(S["samp_max"], 1)
            dve.wait_ge(S["samp_exp"], 2)
            chain(dve.reciprocal(samp_small[0:64, 4:6], samp_small[0:64, 2:4]))
            chain(dve.scalar_tensor_tensor(samp_small[0:64, 6:7], sbias[0:64, SB_SECOND:SB_SECOND + 1], neglam[0:64, :],
                                           sbias[0:64, SB_FIRST:SB_FIRST + 1], ALU.mult, ALU.add))
            chain(dve.tensor_tensor(samp_small[0:64, 4:5], samp_small[0:64, 4:5], samp_small[0:64, 6:7], ALU.mult))
            for n, kind in enumerate(("diff", "sparse")):
                chain(dve.tensor_scalar(s_samp[kind][0:64, :], s_samp[kind][0:64, :], samp_small[0:64, 4 + n:5 + n],
                                        None, ALU.mult))
                dve.tensor_scalar(new_diag[n][0:64, :], ident[0:64, 0:64], s_samp[kind][0:64, PAST:KEYS], None, ALU.mult)\
                    .then_inc(S["samp_attn"], 1)
            await_unit(dve, "sampT")
            dve.wait_ge(S["pad_zero"], 1)
            for n in range(2):
                base = samp_pad[:, n, 0, 0:1]
                dst = bass.AP(base.tensor, base.offset, [list(base.ap[0]), [512, PAGES], [72, TS], [1, 8]])
                dve.tensor_copy(dst, bank("sampT")[:, 192 * n:192 * n + 128].rearrange("p (g b m) -> p g b m", g=PAGES, b=TS))\
                    .then_inc(S["pad_filled"], 1)
            chain.put(dve.tensor_reduce(att[:, 0:32], bank("sampT")[:, 128:192].rearrange("p (n i) -> p n i", i=2),
                                        AX.X, ALU.add))
            chain.settle()
            drain_unit(dve.tensor_copy(att[:, 32:96], bank("sampT")[:, 320:384]), "sampT")
            await_drained(dve, "sampT")
            new_d = att[:, 0:32].rearrange("p (b j) -> p j b", j=4)
            new_s = att[:, 32:96].rearrange("p (b j i) -> p j b i", j=4, i=2)
            part_d = new_part[:, 0:32].rearrange("p (j b) -> p j b", j=4)
            part_s = new_part[:, 32:64].rearrange("p (j b) -> p j b", j=4)
            chain.put(dve.tensor_tensor(part_d, new_d, z[:, VA:VA + 4, TP:T], ALU.mult))
            for i in range(2):
                half = slice(i * HD, (i + 1) * HD)
                chain.put(dve.tensor_tensor(part_s[half], new_s[half, :, :, i], z[half, VS:VS + 4, TP:T], ALU.mult))
            chain.settle()

            def mean_squares(u, at, n):
                await_unit(dve, f"rms{u}")
                drain_unit(dve.tensor_scalar(s_diff[:, RMS + at:RMS + at + n], bank(f"rms{u}")[:, 0:n], 1.0 / P, EPS,
                                             ALU.mult, ALU.add), f"rms{u}")
                await_drained(dve, f"rms{u}")

            def rms_apply(t0, t1):
                o = o_diff[:, :, t0:t1]
                roots = s_diff[:, RMS + 4 * t0:RMS + 4 * t1].rearrange("p (j t) -> p j t", j=4)
                chain(dve.tensor_tensor(o, o, roots, ALU.mult))
                chain(dve.tensor_scalar(o, o, par[:, P_SUBLN:P_SUBLN + 1], 1.0 - LAM_INIT, ALU.mult, ALU.mult))

            def pick(n, name, mask, heads):
                await_unit(dve, name)
                drain_unit(dve.tensor_tensor(samp_rows[0:64, n, :].rearrange("p (h e) -> p h e", h=heads),
                                             bank(name)[0:64, :].rearrange("p (h e) -> p h e", h=heads),
                                             cst[0:64, mask:mask + heads].unsqueeze(2).to_broadcast([64, heads, 512 // heads]),
                                             ALU.mult), name)

            for u in range(2):
                mean_squares(u, 512 * u, 512)
            dve.reciprocal(s_diff[:, RMS:RMS + 4 * TP], s_diff[:, RMS:RMS + 4 * TP]).then_inc(S["rms_recip"], 1)

            def up_low(i, m):
                raw, _, _ = ring_tile(UP_AT + m)
                dve.wait_ge(S["up_hi_made"], i * 4 + m + 1)
                dve.tensor_tensor(halves_of(up_lo, m, D), raw, halves_of(up_hi, m, D), ALU.subtract)\
                    .then_inc(S["up_lo_made"], 1)

            up_low(0, 0)
            up_low(0, 1)
            dve.wait_ge(S["sparse_hi_made"], 1)
            dve.tensor_tensor(token_cols(sparse_lo, 0, TP), o_sparse[:, :, 0:TP], token_cols(sparse_hi, 0, TP),
                              ALU.subtract).then_inc(S["sparse_lo_made"], 1)
            pick(0, "samp_diff", C_PAIR, 4)
            dve.wait_ge(S["rms_root"], 1)
            rms_apply(0, TP)
            dve.sem_inc(S["diff_normed"], 1)
            dve.wait_ge(S["diff_hi_made"], 1)
            dve.tensor_tensor(token_cols(diff_lo, 0, TP), o_diff[:, :, 0:TP], token_cols(diff_hi, 0, TP), ALU.subtract)\
                .then_inc(S["diff_lo_made"], 1)
            pick(1, "samp_sparse", C_HEAD, 8)
            await_unit(dve, "samp_o")
            o_d = bank("samp_o")[:, 0:32].rearrange("p (j b) -> p j b", j=4)
            o_s = bank("samp_o")[:, 32:64].rearrange("p (j b) -> p j b", j=4)
            await_drained(dve, "sparse_o1")
            await_drained(dve, "diff_o1")
            chain(dve.tensor_tensor(o_sparse[:, :, TP:T], o_s, part_s, ALU.add))
            drain_unit(dve.tensor_tensor(o_diff[:, :, TP:T], o_d, part_d, ALU.add), "samp_o")
            await_drained(dve, "samp_o")
            dve.sem_inc(S["out_sample_ready"], 1)
            dve.wait_ge(S["sparse_hi_made"], 2)
            dve.tensor_tensor(token_cols(sparse_lo, TP, T), o_sparse[:, :, TP:T], token_cols(sparse_hi, TP, T),
                              ALU.subtract).then_inc(S["sparse_lo_made"], 1)
            mean_squares(2, 4 * TP, 4 * TS)
            dve.reciprocal(s_diff[:, RMS + 4 * TP:RMS + 4 * T], s_diff[:, RMS + 4 * TP:RMS + 4 * T])\
                .then_inc(S["rms_recip"], 1)
            dve.wait_ge(S["rms_root"], 2)
            rms_apply(TP, T)
            dve.sem_inc(S["out_sample_ready"], 1)
            dve.wait_ge(S["diff_hi_made"], 2)
            dve.tensor_tensor(token_cols(diff_lo, TP, T), o_diff[:, :, TP:T], token_cols(diff_hi, TP, T), ALU.subtract)\
                .then_inc(S["diff_lo_made"], 1)

            dve.wait_ge(S["kv_stored"], 16)
            dve.sem_inc(S["up_b_free"], 2)
            dve.sem_inc(S["up_a_free"], 2)
            with dve.Fori(0, 2) as i:
                def row(of, at):
                    return of[:, bass.ds(at, 1), :].rearrange("p o t -> p (o t)")

                for pair in range(2):
                    for k in range(2):
                        n = i * 4 + 2 * pair + k
                        dve.wait_ge(S["up_b_filled"], n + 1)
                        dve.tensor_tensor(row(merged, n), psum[:, k, 0:T], row(gate, n + DC), ALU.mult)\
                            .then_inc(S["up_b_free"], 1)
                    for k in range(2):
                        n = i * 4 + 2 * pair + k
                        dve.wait_ge(S["tiles_done"], UP_AT + n + 1)
                        dve.wait_ge(S["merged"], n + 1)
                        dve.tensor_tensor(up_tmp[k % 2], psum[:, 4 + k, 0:T], row(gate, n), ALU.mult)\
                            .then_inc(S["up_a_free"], 1)
                        up_low(i, 2 * pair + k + 2)
            dve.sem_inc(S["out_free"], 4)
            for n in range(DC):
                dve.wait_ge(S["tiles_done"], OUT_AT + n + 1)
                dve.scalar_tensor_tensor(pre[:, n, :], part(xt, n, T), ALPHA, psum[:, n % 4, 0:T], ALU.mult, ALU.add)\
                    .then_inc(S["out_free"], 1)
                if n:
                    dve.wait_ge(S["out_free"], 4 + n + 1)
                    if n >= 2:
                        dve.wait_ge(S["chunks_summed"], n - 1)
                    dve.tensor_tensor(ln_sum, pre[:, 0, :] if n == 1 else ln_sum, pre[:, n, :], ALU.add)\
                        .then_inc(S["chunks_summed"], 1)
                if n + 2 < DC:
                    up_low(0, DC + n + 2)

            def norm(n, src, dst, g, b):
                dve.wait_ge(S["ln_stat"], 2 * n + 1)
                chain(dve.tensor_scalar(ln_mean, psum[:, LN_BANKS[n][0], 0:T], 1.0 / D, None, ALU.mult))
                for k in range(DC):
                    dve.tensor_tensor(src[:, k, :], src[:, k, :], ln_mean, ALU.subtract).then_inc(S["ln_centred"], 1)
                dve.wait_ge(S["ln_stat"], 2 * n + 2)
                chain(dve.tensor_scalar(ln_root, psum[:, LN_BANKS[n][1], 0:T], 1.0 / D, EPS, ALU.mult, ALU.add))
                dve.reciprocal(ln_root, ln_root).then_inc(S["ln_recip"], 1)
                dve.wait_ge(S["ln_root"], n + 1)
                for k in range(1, DC, 2):
                    chain(dve.tensor_tensor(src[:, k, :], src[:, k, :], ln_root, ALU.mult))
                    dve.tensor_scalar(dst[:, k, :], src[:, k, :], par[:, g + k:g + k + 1], par[:, b + k:b + k + 1],
                                      ALU.mult, ALU.add).then_inc(S["ln_odd"], 1)

            norm(0, pre, h, P_LN1G, P_LN1B)
            for k in range(0, DC, 2):
                dve.wait_ge(S["h_hi_made"], k // 2 + 1)
                dve.tensor_tensor(h_lo[:, k * T:(k + 2) * T], xt[:, k * T:(k + 2) * T], h_hi[:, k * T:(k + 2) * T],
                                  ALU.subtract).then_inc(S["h_lo_made"], 1)

            dve.sem_inc(S["score_free"], 2)
            for hc in range(HC):
                dve.wait_ge(S["score_filled"], 2 + hc + 1)
                scores = [psum[0:r, 2 + hc % 2, n * P:(n + 1) * P] for n, (_, r) in enumerate(TOKEN_TILES)]
                val = [route_val[0:r, n, hc, :] for n, (_, r) in enumerate(TOKEN_TILES)]
                idx = [route_idx[0:r, n, hc, :] for n, (_, r) in enumerate(TOKEN_TILES)]
                left = [rest128[n][0:r, :] for n, (_, r) in enumerate(TOKEN_TILES)]
                for n in range(3):
                    chain.put(dve.max(val[n][:, 0:8], scores[n]))
                chain.settle()
                for n in range(3):
                    chain.put(dve.match_replace(left[n], val[n][:, 0:8], scores[n], TAKEN))
                for n in range(3):
                    last = dve.max_index(idx[n][:, 0:8], val[n][:, 0:8], scores[n])
                    if n == 2:
                        last.then_inc(S["score_free"], 1)
                chain.settle()
                for n in range(3):
                    chain.put(dve.max(val[n][:, 8:16], left[n]))
                chain.settle()
                for n in range(3):
                    chain.put(dve.max_index(idx[n][:, 8:16], val[n][:, 8:16], left[n]))
            chain.settle()

            for n, (_, r) in enumerate(TOKEN_TILES):
                chain(dve.tensor_copy(route_idxf[0:r, n], route_idx[0:r, n]))
                halves = route_val[0:r, n].rearrange("p (h c) k -> p h c k", c=2)
                first = halves[:, :, 0, :].unsqueeze(3).to_broadcast([r, 8, TOP, TOP])
                second = halves[:, :, 1, :].unsqueeze(2).to_broadcast([r, 8, TOP, TOP])
                sums4 = cand[0:r, :].rearrange("p (h i j) -> p h i j", h=8, i=TOP)
                chain(dve.tensor_tensor(sums4, first, second, ALU.add))
                best = top_val[0:r, n, :].rearrange("p (h k) -> p h k", h=8)
                pos = top_pos[0:r, :].rearrange("p (h k) -> p h k", h=8)
                for hp in range(0, 8, 2):
                    pair = [(cand[0:r, (hp + q) * 256:(hp + q + 1) * 256], rest[q][0:r, :], hp + q) for q in range(2)]
                    for rows_c, _, hh in pair:
                        chain.put(dve.max(best[:, hh, 0:8], rows_c))
                    chain.settle()
                    for rows_c, left, hh in pair:
                        chain.put(dve.match_replace(left, best[:, hh, 0:8], rows_c, TAKEN))
                    for rows_c, left, hh in pair:
                        chain.put(dve.max_index(pos[:, hh, 0:8], best[:, hh, 0:8], rows_c))
                    chain.settle()
                    for rows_c, left, hh in pair:
                        chain.put(dve.max(best[:, hh, 8:16], left))
                    chain.settle()
                    for rows_c, left, hh in pair:
                        chain.put(dve.max_index(pos[:, hh, 8:16], best[:, hh, 8:16], left))
                    chain.settle()
                for op, arg, c2, dst in ((ALU.logical_shift_right, 4, 0, first_id), (ALU.bitwise_and, 15, 1, second_id)):
                    chain(dve.tensor_single_scalar(pos_part[0:r, :], top_pos[0:r, :], arg, op))
                    chain(dve.tensor_copy(pos_f[0:r, :], pos_part[0:r, :]))
                    oh = onehot[0:r, :].rearrange("p (n i) -> p n i", i=TOP)
                    chain(dve.tensor_tensor(oh, pos_f[0:r, :].unsqueeze(2).to_broadcast([r, P, TOP]),
                                            iota16[0:r, :].unsqueeze(1).to_broadcast([r, P, TOP]), ALU.is_equal))
                    oh4 = onehot[0:r, :].rearrange("p (h k i) -> p h k i", h=8, k=TOP)
                    ids = route_idxf[0:r, n].rearrange("p (h c) k -> p h c k", c=2)[:, :, c2, :]
                    chain(dve.tensor_tensor(oh4, oh4, ids.unsqueeze(2).to_broadcast([r, 8, TOP, TOP]), ALU.mult))
                    chain(dve.tensor_reduce(dst[0:r, n, :], oh, AX.X, ALU.add))
                chain(dve.tensor_copy(denom[0:r, n, :], best[:, :, 0]))
                chain(dve.tensor_tensor(best, best, denom[0:r, n, :].unsqueeze(2).to_broadcast([r, 8, TOP]), ALU.subtract))
            dve.sem_inc(S["route_ready"], 1)
            for n, (_, r) in enumerate(TOKEN_TILES):
                best = top_val[0:r, n, :].rearrange("p (h k) -> p h k", h=8)
                dve.wait_ge(S["route_exp"], n + 1)
                chain(dve.tensor_reduce(denom[0:r, n, :], best, AX.X, ALU.add))
                chain(dve.reciprocal(denom[0:r, n, :], denom[0:r, n, :]))
                chain(dve.tensor_tensor(best, best, denom[0:r, n, :].unsqueeze(2).to_broadcast([r, 8, TOP]), ALU.mult))
            dve.sem_inc(S["gates_normed"], 1)
            for n in range(3):
                dve.wait_ge(S["route_filled"], n + 1)
                dve.tensor_copy(slots[:, n, :], psum[:, 1 + n, 0:T]).then_inc(S["route_copied"], 1)

            dve.wait_ge(S["route_copied"], 3)

            def rows_of(n, side, last_turn=False):
                dve.wait_ge(S["tok_ready"], n + 1)
                for q in range(2):
                    dve.wait_ge(S["g_filled"], n * 2 + q + 1)
                    if q and not last_turn:
                        dve.tensor_copy(tok[:, 1 - side], slots[:, :, bass.ds(n * 8 + 8, 8)])\
                            .then_inc(S["tok_ready"], 1)
                    four = slice(4 * q, 4 * q + 4)
                    two = slice(4 * q, 4 * q + 2)
                    dve.tensor_tensor(p2[:, two, :], iota.unsqueeze(1).to_broadcast([P, 2, P]),
                                      tok[:, side, 1, two].unsqueeze(2).to_broadcast([P, 2, P]), ALU.is_equal)\
                        .then_inc(S["rows_bare"], 1)
                    dve.tensor_tensor(p1[:, four, :], iota.unsqueeze(1).to_broadcast([P, 4, P]),
                                      tok[:, side, 0, four].unsqueeze(2).to_broadcast([P, 4, P]), ALU.is_equal)
                    for k in range(4 * q + 2, 4 * q + 4):
                        last = dve.tensor_scalar(p2[:, k, :], iota, tok[:, side, 1, k:k + 1], tok[:, side, 2, k:k + 1],
                                                 ALU.is_equal, ALU.mult)
                    last.then_inc(S["rows_ready"], 1)

            dve.tensor_copy(tok[:, 0], slots[:, :, 0:8]).then_inc(S["tok_ready"], 1)
            with dve.Fori(0, T // 16) as i:
                for side in range(2):
                    rows_of(i * 2 + side, side)
            rows_of(T // 8 - 1, 0, last_turn=True)

            dve.wait_ge(S["g_applied"], 2 + T // 4)
            dve.sem_inc(S["v_lo_made"], 2)
            with dve.Fori(0, NK // RING) as i:
                for k in range(RING):
                    raw, _, _ = expert_tile(i, k)
                    cells = gelu_all[:, bass.ds(i * RING + k, 1), :].rearrange("p o t -> p (o t)")
                    dve.wait_ge(S["v_done"], i * RING + k + 1)
                    dve.wait_ge(S["params_loaded"], 16)
                    dve.tensor_copy(halves_of(cells_hi, k, T), cells).then_inc(S["cells_hi_made"], 1)
                    dve.wait_ge(S["cells_hi_made"], i * RING + k + 1)
                    dve.wait_ge(S["params_loaded"], 16)
                    dve.tensor_tensor(halves_of(cells_lo, k, T), cells, halves_of(cells_hi, k, T), ALU.subtract)\
                        .then_inc(S["cells_split"], 1)
                    dve.wait_ge(S["v_hi_made"], i * RING + k + 1)
                    dve.tensor_tensor(halves_of(w_lo, k, D), raw, halves_of(w_hi, k, D), ALU.subtract)\
                        .then_inc(S["v_lo_made"], 1)
            dve.wait_ge(S["h_restored"], 1)
            dve.wait_ge(S["v_lo_made"], 2 + NK)
            for k in range(DC):
                dve.wait_ge(S["v_filled"], k + 1)
                dve.scalar_tensor_tensor(acc[:, k, :], pre[:, k, :], ALPHA, psum[:, k, 0:T], ALU.mult, ALU.add)\
                    .then_inc(S["acc_ready"], 1)
            dve.wait_ge(S["acc_ready"], DC)
            norm(1, acc, y_t, P_LN2G, P_LN2B)

        @block.tensor
        def _(pe):
            def fill(name):
                n = UNIT[name]
                if n >= ROT:
                    pe.wait_ge(drained[n % ROT], n // ROT)

            def project(slot, loaded, out, moving):
                pe.wait_ge(w_loaded[slot], loaded)
                for k in range(DC):
                    last = pe.matmul(out, part(ring, slot * DC + k, P), moving(k), start=(k == 0), stop=(k == DC - 1))
                return last

            x = xt[:, :].rearrange("p (c t) -> p c t", c=DC)
            for n in range(2):
                pe.wait_ge(x_loaded[n], 16)
            banks_free = (S["z_even_free"], S["z_odd_free"])

            def project_parts(out, hi, lo, x_parts, hi_sem, lo_sem, count, x_sem=None, x_step=1):
                pe.wait_ge(hi_sem, count)
                for c in range(DC):
                    if x_sem is not None and c % x_step == 0:
                        pe.wait_ge(x_sem, c // x_step + 1)
                    pe.matmul(out, part(hi, c, P), part(x_parts[0], c, T), start=(c == 0), stop=False)
                    pe.matmul(out, part(hi, c, P), part(x_parts[1], c, T), start=False, stop=False)
                pe.wait_ge(lo_sem, count)
                for c in range(DC):
                    last = pe.matmul(out, part(lo, c, P), part(x_parts[0], c, T), start=False, stop=(c == DC - 1))
                return last

            def z_tile(i, k):
                pe.wait_ge(banks_free[k % 2], i * 2 + k // 2 + 1)
                project_parts(psum[:, k % 2, 0:T], halves_of(z_hi, k, D), halves_of(z_lo, k, D), (x_hi, x_lo),
                              S["z_hi_made"], S["z_lo_made"], i * RING + k + 1,
                              S["x_lo_made"] if k == 0 else None).then_inc(S["tiles_done"], 1)

            with pe.Fori(0, Z_TILES // RING) as i:
                for k in range(RING):
                    z_tile(i, k)
            for t in range(Z_TILES // RING * RING, Z_TILES):
                z_tile(t // RING, t % RING)

            pe.wait_ge(S["consts_loaded"], 16)
            pe.wait_ge(S["z_even_free"], 1 + Z_TILES // 2)
            pe.wait_ge(S["z_odd_free"], 1 + Z_TILES // 2)
            pe.wait_ge(S["lam_products"], 1)
            fill("wi")
            b = bank("wi")
            for qt in range(2):
                pe.matmul(b[:, 8 * qt:8 * qt + 8], z[0:8, WI, qt * P:(qt + 1) * P], ident[0:8, 0:8], start=True, stop=True)
            pe.matmul(b[0:64, 16:24], cst[0:8, C_HEADROW:C_HEADROW + 64], z[0:8, WI, TP:T], start=True, stop=True)
            pe.matmul(b[:, 128:130], ones[0:64, :], lam[0:64, 0:2], start=True, stop=True)\
                .then_inc(S["unit_filled"], 1)

            def scores(kind, u, q_tile, keys_of):
                qt, i, j0, n = SCORE_UNITS[u]
                fill(f"{kind}{u}")
                b, keys = bank(f"{kind}{u}"), P * (qt + 1)
                half = slice(i * HD, (i + 1) * HD)
                for j in range(n):
                    m = 2 * (j0 + j) + i
                    last = pe.matmul(b[:, j * keys:(j + 1) * keys],
                                     z[half, q_tile + m // 2, qt * P:(qt + 1) * P],
                                     z[half, keys_of(m), 0:keys], start=True, stop=True)
                last.then_inc(S["unit_filled"], 1)

            for u in range(6):
                scores("idx", u, QI, lambda m: KI)
            for kind, tile in (("diff", VA), ("sparse", VS)):
                for kt in range(2):
                    fill(f"v_{kind}{kt}")
                    for j in range(4):
                        last = pe.transpose(bank(f"v_{kind}{kt}")[:, j * P:(j + 1) * P],
                                            z[:, tile + j, kt * P:(kt + 1) * P], ident)
                    last.then_inc(S["unit_filled"], 1)
            for u in range(6):
                scores("diff", u, QA, lambda m: KA + m // 2)

            def ring_use(t):
                return 16 * (t // RING + 1)

            def gate_tile(n):
                t = Z_TILES + n
                pe.wait_ge(banks_free[n % 2], Z_TILES // 2 + n // 2 + 1)
                if n < EARLY_GATES:
                    pe.wait_ge(S["x_lo_made"], DC + 1)
                    project_parts(psum[:, n % 2, 0:T], halves_of(z_hi, n, D), gate_low_buf(n), (x_hi, x_lo),
                                  S["gate_hi_made"], S["gate_lo_made"], n + 1).then_inc(S["tiles_done"], 1)
                    return
                project(t % RING, ring_use(t), psum[:, n % 2, 0:T], lambda k: x[:, k, :]).then_inc(S["tiles_done"], 1)

            pe.wait_ge(S["qpad_ready"], 6)
            for b in range(TS):
                pe.wait_ge(S["k_ready"], b + 1)
                buf = kbuf[b % 2]
                for n, kind in enumerate(("diff", "sparse")):
                    for j in range(4):
                        last = pe.matmul(psum[0:64, 2 + n, 0:KEYS], qpad[kind][:, j, b, :], buf[:, 4 * n + j, :],
                                         start=(b == 0 and j == 0), stop=(b == TS - 1 and j == 3 and n == 0))
                last = pe.matmul(psum[0:64, 4, 0:KEYS], qpad["idx"][:, b, :], buf[:, 8, :],
                                 start=(b == 0), stop=(b == TS - 1))
                last.then_inc(S["k_used"] if b < TS - 1 else S["sample_scored"], 1)
                if 2 * b + 2 <= EARLY_GATES:
                    gate_tile(2 * b)
                    gate_tile(2 * b + 1)
            pe.wait_ge(S["relu_sample"], 1)
            await_drained(pe, "wi")
            fill("isum")
            pe.matmul(bank("isum")[0:TS, 0:KEYS], wsel[0:64, :], relu_samp[0:64, :], start=True, stop=True)\
                .then_inc(S["unit_filled"], 1)
            for u in range(6):
                scores("sparse", u, QS, lambda m: KS + m // 2)
            gate_tile(EARLY_GATES)
            gate_tile(EARLY_GATES + 1)

            def transposes(kind, buf, heads, head_of):
                for u in range(heads * 3 // 4):
                    fill(f"{kind}T{u}")
                    for q in range(4):
                        h, (qt, kt) = (4 * u + q) // 3, PT_TILES[(4 * u + q) % 3]
                        last = pe.transpose(bank(f"{kind}T{u}")[:, q * P:(q + 1) * P],
                                            s_view(buf, qt)[:, head_of(h), kt * P:(kt + 1) * P], ident)
                    last.then_inc(S["unit_filled"], 1)

            def outputs(kind, heads, width):
                for u in range(2):
                    fill(f"{kind}_o{u}")
                    n = heads // 2
                    for h in range(u * n, (u + 1) * n):
                        row = (h * width) % P
                        col = ((h * width) // P % 2) * TP
                        out = bank(f"{kind}_o{u}")[row:row + width, :]
                        v = v_tok[kind][:, :, h * width:(h + 1) * width]
                        pe.matmul(out[:, col:col + TP], v[:, 0, :],
                                  pt[:, 3 * h:3 * h + 2, :].rearrange("p n q -> p (n q)"), start=True, stop=False)
                        last = pe.matmul(out[:, col + P:col + TP], v[:, 1, :], pt[:, 3 * h + 2, :],
                                         start=False, stop=True)
                    last.then_inc(S["unit_filled"], 1)

            pe.wait_ge(S["diff_attn"], 2)
            transposes("diff", s_diff, 4, lambda h: 2 * h)
            await_drained(pe, "diffT2")
            outputs("diff", 4, P)
            pe.wait_ge(S["sel_sample"], 1)
            pe.matmul(psum[0:64, 3, 0:KEYS], cst[0:TS, C_EXPAND:C_EXPAND + 64], iscore[2][0:TS, :],
                      start=False, stop=True).then_inc(S["sample_scored"], 1)
            gate_tile(EARLY_GATES + 2)
            gate_tile(EARLY_GATES + 3)
            pe.wait_ge(S["sparse_attn"], 2)
            transposes("sparse", s_sparse, 8, lambda h: h)
            await_drained(pe, "sparseT5")
            outputs("sparse", 8, HD)

            pe.wait_ge(S["samp_attn"], 2)
            fill("sampT")
            b = bank("sampT")
            for n, kind in enumerate(("diff", "sparse")):
                for g in range(PAGES):
                    pe.transpose(b[:, 192 * n + 64 * g:192 * n + 64 * (g + 1)],
                                 s_samp[kind][0:64, g * PAGE:(g + 1) * PAGE], ident[0:64, 0:64])
                last = pe.matmul(b[:, 192 * n + 128:192 * n + 192], ones[0:64, :], new_diag[n][0:64, :],
                                 start=True, stop=True)
            last.then_inc(S["unit_filled"], 1)
            await_drained(pe, "sampT")
            pe.wait_ge(S["rms_square"], 1)
            for u in range(2):
                fill(f"rms{u}")
                pe.matmul(bank(f"rms{u}"), ones, s_diff[:, 512 * u:512 * (u + 1)], start=True, stop=True)\
                    .then_inc(S["unit_filled"], 1)
            for n, kind in enumerate(("diff", "sparse")):
                fill(f"samp_{kind}")
                pe.wait_ge(S["pad_filled"], n + 1)
                for b in range(TS):
                    pe.wait_ge(vc_loaded[b], 32)
                    for g in range(PAGES):
                        last = pe.matmul(bank(f"samp_{kind}")[0:64, :], samp_pad[:, n, g, 64 * b:64 * (b + 1)],
                                         vbuf[b][kind][:, g, :], start=(b == 0 and g == 0),
                                         stop=(b == TS - 1 and g == PAGES - 1))
                last.then_inc(S["unit_filled"], 1)
            fill("samp_o")
            for n, kind in enumerate(("diff", "sparse")):
                await_drained(pe, f"samp_{kind}")
                for j in range(4):
                    last = pe.matmul(bank("samp_o")[:, 32 * n + 8 * j:32 * n + 8 * (j + 1)],
                                     samp_rows[0:64, n, j * P:(j + 1) * P], cst[0:64, C_DIAG:C_DIAG + TS],
                                     start=True, stop=True)
            last.then_inc(S["unit_filled"], 1)
            pe.wait_ge(S["rms_square"], 2)
            fill("rms2")
            pe.matmul(bank("rms2")[:, 0:4 * TS], ones, s_diff[:, 4 * TP:4 * T], start=True, stop=True)\
                .then_inc(S["unit_filled"], 1)

            pe.wait_ge(S["sparse_lo_made"], 2)
            await_drained(pe, "sparse_o1")

            def up_products(out, n, k, first, hi_part, lo_part):
                hi, lo = halves_of(up_hi, k, D), halves_of(up_lo, k, D)
                pe.wait_ge(S["up_hi_made"], n + 1)
                for c in range(4):
                    pe.matmul(out, part(hi, first + c, P), part(hi_part, c, T), start=(c == 0), stop=False)
                    pe.matmul(out, part(hi, first + c, P), part(lo_part, c, T), start=False, stop=False)
                pe.wait_ge(S["up_lo_made"], n + 1)
                for c in range(4):
                    last = pe.matmul(out, part(lo, first + c, P), part(hi_part, c, T), start=False, stop=(c == 3))
                return last

            with pe.Fori(0, DC // 2) as i:
                for k in range(2):
                    pe.wait_ge(S["up_b_free"], i * 2 + k + 1)
                    up_products(psum[:, k, 0:T], i * 2 + k, k, 4, sparse_hi, sparse_lo).then_inc(S["up_b_filled"], 1)
                pe.wait_ge(S["diff_lo_made"], 2)
                for k in range(2):
                    pe.wait_ge(S["up_a_free"], i * 2 + k + 1)
                    up_products(psum[:, 4 + k, 0:T], i * 2 + k, k, 0, diff_hi, diff_lo).then_inc(S["tiles_done"], 1)
            with pe.Fori(0, DC // 4) as i:
                for k in range(4):
                    pe.wait_ge(S["out_free"], i * 4 + k + 1)
                    project_parts(psum[:, k, 0:T], halves_of(up_hi, k, D), halves_of(up_lo, k, D),
                                  (merged_hi, merged_lo), S["up_hi_made"], S["up_lo_made"], DC + i * 4 + k + 1,
                                  S["merged_lo_made"] if k == 0 else None).then_inc(S["tiles_done"], 1)

            def norm_squares(n):
                for k in range(DC):
                    pe.wait_ge(S["ln_square"], n * DC + k + 1)
                    last = pe.matmul(psum[:, LN_BANKS[n][1], 0:T], ones, squares[:, k, :],
                                     start=(k == 0), stop=(k == DC - 1))
                last.then_inc(S["ln_stat"], 1)

            pe.wait_ge(S["up_a_free"], 2 + DC)
            pe.wait_ge(S["chunks_summed"], DC - 1)
            pe.matmul(psum[:, LN_BANKS[0][0], 0:T], ones, ln_sum, start=True, stop=True).then_inc(S["ln_stat"], 1)
            norm_squares(0)

            pe.sem_inc(S["u_hi_used"], 2)
            pe.sem_inc(S["u_done"], 2)
            pe.wait_ge(S["subkeys_loaded"], 16)
            pe.sem_inc(S["score_filled"], 2)
            with pe.Fori(0, HC // 4) as i:
                def sub_scores(k):
                    pe.wait_ge(S["q_evac"], 2 + i * 4 + k + 1)
                    pe.wait_ge(S["score_free"], i * 4 + k + 1)
                    for n, (t0, r) in enumerate(TOKEN_TILES):
                        last = pe.matmul(psum[0:r, 2 + k % 2, n * P:(n + 1) * P], q_sb[k % 2][:, t0:t0 + r],
                                         subk[:, bass.ds(i * 4 + k, 1), :].rearrange("p o n -> p (o n)"),
                                         start=True, stop=True)
                    last.then_inc(S["score_filled"], 1)

                for k in range(4):
                    pe.wait_ge(S["q_evac"], i * 4 + k + 1)
                    project_parts(psum[:, k % 2, 0:T], halves_of(wq_hi, k, D), halves_of(wq_lo, k, D), (h_hi, h_lo),
                                  S["wq_hi_made"], S["wq_lo_made"], i * 4 + k + 1,
                                  S["h_lo_made"] if k == 0 else None, 2).then_inc(S["tiles_done"], 1)
                    if k:
                        sub_scores(k - 1)
                sub_scores(3)

            with pe.Fori(0, NK // RING) as i:
                for k in range(RING):
                    out, hi, lo = psum[:, 4 + k, 0:T], halves_of(w_hi, k, D), halves_of(w_lo, k, D)
                    pe.wait_ge(S["gelu_done"], i * RING + k + 1)
                    pe.wait_ge(S["u_hi_made"], i * RING + k + 1)
                    for c in range(DC):
                        pe.matmul(out, part(hi, c, P), part(h_hi, c, T), start=(c == 0), stop=False)
                        last = pe.matmul(out, part(hi, c, P), part(h_lo, c, T), start=False, stop=False)
                    last.then_inc(S["u_hi_used"], 1)
                    pe.wait_ge(S["u_lo_made"], 2 + i * RING + k + 1)
                    for c in range(DC):
                        last = pe.matmul(out, part(lo, c, P), part(h_hi, c, T), start=False, stop=(c == DC - 1))
                    last.then_inc(S["u_done"], 1)

            for n, src in enumerate((first_id, second_id, top_val)):
                pe.wait_ge(S["route_ready"], 1)
                if n == 2:
                    pe.wait_ge(S["gates_normed"], 1)
                for g, (t0, r) in enumerate(TOKEN_TILES):
                    last = pe.transpose(psum[:, 1 + n, t0:t0 + r], src[0:r, g, :], ident[0:r, 0:r])
                last.then_inc(S["route_filled"], 1)
            pe.wait_ge(S["gelu_done"], 4 + NK)
            pe.sem_inc(S["g_filled"], 2)
            with pe.Fori(0, T // 8) as i:
                for q in range(2):
                    pe.wait_ge(S["rows_ready"], i * 2 + q + 1)
                    pe.wait_ge(S["rows_weighted"], (i * 2 + q) * 2 + 2)
                    pe.wait_ge(S["g_free"], i * 2 + q + 1)
                    for k in range(4):
                        last = pe.matmul(psum[:, 4 + q, k * P:(k + 1) * P], p1[:, 4 * q + k, :], p2[:, 4 * q + k, :],
                                         start=True, stop=True)
                    last.then_inc(S["g_filled"], 1)
            pe.sem_inc(S["v_hi_used"], 2)
            pe.sem_inc(S["v_done"], 2)
            pe.wait_ge(S["g_applied"], 2 + T // 4)

            def high_products(k, first=False):
                hi, cells = halves_of(w_hi, k, D), [halves_of(m, k, T) for m in (cells_hi, cells_lo)]
                for c in range(DC):
                    for n in range(2):
                        last = pe.matmul(psum[:, c, 0:T], part(hi, c, P), cells[n], start=(first and n == 0), stop=False)
                last.then_inc(S["v_hi_used"], 1)

            def contract(i, k, first=False):
                pe.wait_ge(S["v_hi_made"], i * RING + k + 1)
                pe.wait_ge(S["cells_split"], i * RING + k + 1)
                high_products(k, first)
                pe.wait_ge(S["v_lo_made"], 2 + i * RING + k + 1)
                for c in range(DC):
                    last = pe.matmul(psum[:, c, 0:T], part(halves_of(w_lo, k, D), c, P), halves_of(cells_hi, k, T),
                                     start=False, stop=False)
                last.then_inc(S["v_done"], 1)

            for k in range(RING):
                contract(0, k, first=(k == 0))
            with pe.Fori(1, NK // RING - 1) as i:
                for k in range(RING):
                    contract(i, k)
            for k in range(RING - 1):
                contract(NK // RING - 1, k)
            pe.wait_ge(S["v_hi_made"], NK)
            pe.wait_ge(S["cells_split"], NK)
            pe.wait_ge(S["v_lo_made"], 2 + NK)
            high_products(RING - 1)
            for c in range(DC):
                pe.matmul(psum[:, c, 0:T], part(halves_of(w_lo, RING - 1, D), c, P), halves_of(cells_hi, RING - 1, T),
                          start=False, stop=True).then_inc(S["v_filled"], 1)
            for c in range(DC):
                pe.wait_ge(S["acc_ready"], c + 1)
                last = pe.matmul(psum[:, LN_BANKS[1][0], 0:T], ones, acc[:, c, :], start=(c == 0), stop=(c == DC - 1))
            last.then_inc(S["ln_stat"], 1)
            norm_squares(1)


def shape_constants():
    f = np.float32
    consts = np.zeros((P, CONSTS), f)
    consts[:, C_IDENT:C_IDENT + P] = np.eye(P, dtype=f)
    consts[:, C_ONES:C_ONES + P] = 1
    consts[:, C_IOTA:C_IOTA + P] = np.arange(P, dtype=f)
    consts[:, C_IOTA16:C_IOTA16 + TOP] = np.arange(TOP, dtype=f)
    for b in range(TS):
        for m in range(8):
            consts[b, C_EXPAND + b * 8 + m] = 1
            consts[m, C_HEADROW + b * 8 + m] = 1
            consts[b * 8 + m, C_DIAG + b] = 1
            consts[b * 8 + m, C_PAIR + m // 2] = 1
            consts[b * 8 + m, C_HEAD + m] = 1
    slopes = lambda n: [2.0 ** (-8.0 * (i + 1) / n) for i in range(n)]
    dist = (128 + np.arange(P)[:, None] - np.arange(256)[None, :]).astype(f)
    alibi = np.zeros((P, BIASES, 256), f)
    for n, s in enumerate(slopes(4) + slopes(8) + [0.0]):
        alibi[:, n] = np.where(dist >= 0, -f(s) * dist, f(NEG))
    gap = (PAST - np.arange(KEYS)).astype(f)
    sample = np.zeros((64, SBIAS), f)
    for row in range(64):
        m = row % 8
        sample[row, 0:KEYS] = -f(slopes(4)[m // 2]) * gap
        sample[row, KEYS:2 * KEYS] = -f(slopes(8)[m]) * gap
        sample[row, SB_FIRST + m % 2] = 1
    return consts, alibi.reshape(P, -1), sample


def kernel(x_prompt, x_sample, cache_da_k, cache_da_v, cache_sa_k, cache_sa_v, cache_idx_k, page_table,
           w_in, lambda_q1, lambda_k1, lambda_q2, lambda_k2, da_subln_g, w_a_up, w_b_up, w_out,
           ln1_g, ln1_b, peer_wq, peer_sub_keys, peer_u, peer_v, ln2_g, ln2_b):
    import concourse.bacc as bacc
    from concourse.bass_utils import run_bass_kernel_spmd

    arr = lambda v: np.asarray(v)
    x = np.concatenate([arr(x_prompt).reshape(TP, D), arr(x_sample).reshape(TS, D)])
    x_t = x.T.reshape(DC, P, T).transpose(1, 0, 2)

    wi = arr(w_in)[0]
    at = np.cumsum([0, 512, 512, 512, 512, 512, 512, 512, 64, 8, 1024, 1024]).tolist()
    qa, ka, va, qs, ks, vs, qi, ki, wx, ga, gb = [wi[:, at[n]:at[n + 1]] for n in range(11)]
    pad = np.zeros((D, P - 8), wi.dtype)
    cols = np.concatenate([qa, qs, qi, ka, ks, va, vs, ki, ki, wx, pad, ga, gb], axis=1)
    tiled = lambda m: m.reshape(DC, P, -1, P).transpose(2, 1, 0, 3).reshape(-1, P, D)
    up = np.concatenate([arr(w_a_up)[0], arr(w_b_up)[0]], axis=0)
    weights = np.concatenate([tiled(cols), tiled(up), tiled(arr(w_out)[0]), tiled(arr(peer_wq)[0])])

    keys = lambda c: arr(c)[0].reshape(-1, PAGE, 4, P).transpose(0, 3, 2, 1)
    idx_t = arr(cache_idx_k)[0].transpose(0, 2, 1)
    rows = lambda c: arr(c)[0].reshape(-1, PAGE, 512)
    vec = lambda v: arr(v)[0].reshape(DC, P).T
    lam = np.zeros((P, 4), wi.dtype)
    for n, v in enumerate((lambda_q1, lambda_q2, lambda_k1, lambda_k2)):
        lam[0:HD, n] = arr(v)[0]
    params = np.concatenate([vec(ln1_g), vec(ln1_b), vec(ln2_g), vec(ln2_b), arr(da_subln_g)[0][:, None], lam], axis=1)
    consts, alibi, sample = shape_constants()
    ins = {
        "x_t": x_t, "weights": weights,
        "experts_u": arr(peer_u)[0].reshape(P, P, DC, P).transpose(1, 3, 2, 0).reshape(P, P, D),
        "experts_v": arr(peer_v)[0].reshape(P, P, D).transpose(1, 0, 2),
        "k_cache": np.concatenate([keys(cache_da_k), keys(cache_sa_k), np.concatenate([idx_t, idx_t], axis=1)[:, :, None, :]],
                                  axis=2),
        "v_cache": np.stack([rows(cache_da_v), rows(cache_sa_v)], axis=2),
        "page_table": arr(page_table).astype(np.int32).reshape(1, -1),
        "sub_keys": arr(peer_sub_keys)[0].reshape(HC, NK, P).transpose(2, 0, 1),
        "params": params, "consts": consts, "alibi": alibi, "sample_bias": sample,
    }
    outs = {"kv_out": (P, KV_TILES, T), "y_out": (P, DC, T)}
    nc = bacc.Bacc("TRN2", target_bir_lowering=False, num_devices=1)
    arrays, args = {}, {}
    for name, v in ins.items():
        v = np.ascontiguousarray(v)
        arrays[f"{name}_dram"] = v
        args[name] = nc.dram_tensor(f"{name}_dram", v.shape, mybir.dt.from_np(v.dtype), kind="ExternalInput").ap()
    for name, shape in outs.items():
        args[name] = nc.dram_tensor(f"{name}_dram", shape, F32, kind="ExternalOutput").ap()
    build_program(nc, **args)
    r = run_bass_kernel_spmd(nc, [arrays], core_ids=[0]).results[0]
    kv, y = np.asarray(r["kv_out_dram"]), np.asarray(r["y_out_dram"])
    y = y.transpose(2, 1, 0).reshape(T, D)
    kv = kv.transpose(2, 1, 0)
    out = [y[:TP].reshape(1, TP, D), y[TP:].reshape(TS, 1, D)]
    for lo, hi, (bb, ss) in ((0, TP, (1, TP)), (TP, T, (TS, 1))):
        part = lambda t0, width: kv[lo:hi, t0 - KA:t0 - KA + 4].reshape(hi - lo, -1)[:, :width]
        out += [part(KA, 512).reshape(1, bb, ss, 4, 2, 64), part(VA, 512).reshape(1, bb, ss, 4, 128),
                part(KS, 512).reshape(1, bb, ss, 8, 64), part(VS, 512).reshape(1, bb, ss, 8, 64),
                kv[lo:hi, KI - KA, 0:HD].reshape(1, bb, ss, HD)]
    return tuple(np.ascontiguousarray(o) for o in out)
```
